# Optimizing a Trainium2 kernel written in Bass

```python
import math
import jax, jax.numpy as jnp
from jax import lax
import numpy as np

D_MODEL = 1024
BATCH = 1
SEQ = 512
DEPTH = 2

RMS_EPS = 1e-6
SSD_D_INNER = D_MODEL
SSD_HEAD_DIM = 64
SSD_HEADS = SSD_D_INNER // SSD_HEAD_DIM
SSD_GROUPS = 2
SSD_HEADS_PER_GROUP = SSD_HEADS // SSD_GROUPS
SSD_STATE = 128
SSD_CONV = 4
SSD_CONV_DIM = SSD_D_INNER + 2 * SSD_GROUPS * SSD_STATE
SSD_CHUNK = 128
SSD_NORM_EPS = 1e-5
RET_HEADS = 4
RET_QK_DIM = D_MODEL // 2
RET_V_DIM = D_MODEL
RET_QK_HEAD = RET_QK_DIM // RET_HEADS
RET_V_HEAD = RET_V_DIM // RET_HEADS
RET_CHUNK = 128
ROPE_BASE = 10000.0
IN_WIDTHS = (SSD_D_INNER, SSD_CONV_DIM, SSD_HEADS, RET_QK_DIM, RET_QK_DIM, RET_V_DIM, RET_V_DIM)
IN_PROJ_DIM = SSD_D_INNER + SSD_CONV_DIM + SSD_HEADS + 2 * RET_QK_DIM + 2 * RET_V_DIM
MIX_WIDTH = SSD_D_INNER + RET_V_DIM
RWKV_HEAD = 64
RWKV_HEADS = D_MODEL // RWKV_HEAD
RWKV_DECAY_LORA = 64
RWKV_A_LORA = 64
RWKV_GATE_LORA = 160
RWKV_LN_EPS = 64e-5
MOE_GROUPS = 4
MOE_EXPERTS_PER_GROUP = 4
MOE_EXPERTS = MOE_GROUPS * MOE_EXPERTS_PER_GROUP
MOE_TOP_K = 2
MOE_D_FF = 512

kernel_name = "hybrid_ssd_retention_rwkv7_hmoe"

def rms_norm(x, w, eps=RMS_EPS):
    xf = x.astype(jnp.float32)
    y = xf * lax.rsqrt(jnp.mean(xf * xf, axis=-1, keepdims=True) + eps)
    return (y * w).astype(x.dtype)

def split_cols(t, widths):
    out, start = [], 0
    for w in widths:
        out.append(t[..., start:start + w])
        start += w
    return out

def to_chunks(t, c):
    b, s = t.shape[:2]
    return jnp.moveaxis(t.reshape(b, s // c, c, *t.shape[2:]), 1, 0)

def from_chunks(t):
    nc, b, c = t.shape[:3]
    return jnp.moveaxis(t, 0, 1).reshape(b, nc * c, *t.shape[3:])

def causal_depthwise_conv(x, w, b):
    K = w.shape[0]
    S = x.shape[1]
    xp = jnp.pad(x, ((0, 0), (K - 1, 0), (0, 0)))
    out = xp[:, 0:S] * w[0]
    for j in range(1, K):
        out = out + xp[:, j:j + S] * w[j]
    return out + b

def rotary(x, pos):
    d = x.shape[-1]
    half = d // 2
    inv_freq = ROPE_BASE ** (-jnp.arange(half, dtype=jnp.float32) / half)
    ang = pos[:, None] * inv_freq[None, :]
    cos = jnp.cos(ang)[None, :, None, :]
    sin = jnp.sin(ang)[None, :, None, :]
    xf = x.astype(jnp.float32)
    x1, x2 = xf[..., :half], xf[..., half:]
    return jnp.concatenate([x1 * cos - x2 * sin, x1 * sin + x2 * cos], axis=-1).astype(x.dtype)

def ssd_mixer(z, xbc, dt_raw, conv_w, conv_b, dt_bias, a_log, d_skip, norm_w):
    Bsz, S, _ = z.shape
    G, Hg, P, N = SSD_GROUPS, SSD_HEADS_PER_GROUP, SSD_HEAD_DIM, SSD_STATE
    xbc = jax.nn.silu(causal_depthwise_conv(xbc, conv_w, conv_b))
    xs, Bm, Cm = split_cols(xbc, (SSD_D_INNER, G * N, G * N))
    xs = xs.reshape(Bsz, S, G, Hg, P)
    Bm = Bm.reshape(Bsz, S, G, N)
    Cm = Cm.reshape(Bsz, S, G, N)
    dt = jax.nn.softplus(dt_raw.astype(jnp.float32) + dt_bias).reshape(Bsz, S, G, Hg)
    A = -jnp.exp(a_log.astype(jnp.float32)).reshape(G, Hg)
    a = dt * A
    xdt = xs * dt[..., None]
    L = SSD_CHUNK
    causal = jnp.tril(jnp.ones((L, L), dtype=bool))[None, :, :, None, None]

    def step(h, inp):
        xc, ac, bc, cc = inp
        acum = jnp.cumsum(ac, axis=1)
        seg = acum[:, :, None] - acum[:, None, :]
        decay = jnp.exp(jnp.where(causal, seg, -jnp.inf))
        cb = jnp.einsum('bign,bjgn->bijg', cc, bc)
        m = cb[..., None] * decay
        y_diag = jnp.einsum('bijgh,bjghp->bighp', m, xc)
        y_off = jnp.einsum('bign,bghpn->bighp', cc, h) * jnp.exp(acum)[..., None]
        decay_end = jnp.exp(acum[:, -1:] - acum)
        h = h * jnp.exp(acum[:, -1])[..., None, None] + jnp.einsum(
            'bjgn,bjghp->bghpn', bc, xc * decay_end[..., None])
        return h, y_diag + y_off

    h0 = jnp.zeros((Bsz, G, Hg, P, N), jnp.float32)
    _, y = lax.scan(step, h0, (to_chunks(xdt, L), to_chunks(a, L), to_chunks(Bm, L), to_chunks(Cm, L)))
    y = from_chunks(y)
    y = y + xs * d_skip.reshape(G, Hg)[..., None]
    y = y.reshape(Bsz, S, SSD_D_INNER) * jax.nn.silu(z.astype(jnp.float32))
    yg = y.reshape(Bsz, S, G, SSD_D_INNER // G)
    yg = yg * lax.rsqrt(jnp.mean(yg * yg, axis=-1, keepdims=True) + SSD_NORM_EPS)
    return (yg.reshape(Bsz, S, SSD_D_INNER) * norm_w).astype(z.dtype)

def retention_mixer(q, k, v, g, pos):
    Bsz, S, _ = q.shape
    H, dk, dv, C = RET_HEADS, RET_QK_HEAD, RET_V_HEAD, RET_CHUNK
    q = rotary(q.reshape(Bsz, S, H, dk), pos)
    k = rotary(k.reshape(Bsz, S, H, dk), pos) * (dk ** -0.5)
    v = v.reshape(Bsz, S, H, dv)
    log_gamma = jnp.log(1.0 - 2.0 ** (-5.0 - jnp.arange(H, dtype=jnp.float32)))
    idx = jnp.arange(C, dtype=jnp.float32)
    diff = idx[:, None] - idx[None, :]
    dmask = jnp.where(diff[None] >= 0, jnp.exp(jnp.maximum(diff, 0.0)[None] * log_gamma[:, None, None]), 0.0)
    q_decay = jnp.exp((idx[:, None] + 1.0) * log_gamma[None, :])
    k_decay = jnp.exp((C - 1.0 - idx[:, None]) * log_gamma[None, :])
    chunk_decay = jnp.exp(C * log_gamma)

    def step(R, inp):
        qc, kc, vc = inp
        s = jnp.einsum('bihd,bjhd->bhij', qc, kc) * dmask[None]
        inner = jnp.einsum('bhij,bjhv->bihv', s, vc)
        cross = jnp.einsum('bihd,bhdv->bihv', qc, R) * q_decay[None, :, :, None]
        R = R * chunk_decay[None, :, None, None] + jnp.einsum(
            'bjhd,bjhv->bhdv', kc * k_decay[None, :, :, None], vc)
        return R, inner + cross

    R0 = jnp.zeros((Bsz, H, dk, dv), jnp.float32)
    _, y = lax.scan(step, R0, (to_chunks(q, C), to_chunks(k, C), to_chunks(v, C)))
    y = from_chunks(y)
    y = y * lax.rsqrt(jnp.mean(y * y, axis=-1, keepdims=True) + RMS_EPS)
    y = y.reshape(Bsz, S, RET_V_DIM) * jax.nn.silu(g.astype(jnp.float32))
    return y.astype(q.dtype)

def ssd_retention_layer(u, pos, w_in, conv_w, conv_b, dt_bias, a_log, d_skip, norm_w, w_out):
    proj = u @ w_in
    z, xbc, dt_raw, q, k, v, g = split_cols(proj, IN_WIDTHS)
    y_a = ssd_mixer(z, xbc, dt_raw, conv_w, conv_b, dt_bias, a_log, d_skip, norm_w)
    y_b = retention_mixer(q, k, v, g, pos)
    return jnp.concatenate([y_a, y_b], axis=-1) @ w_out

def rwkv7_layer(u, mu, w_r, w_k, w_v, w_o, w0, w1, w2, a0, a1, a2, g1, g2, k_k, k_a, r_k, lnx_w, lnx_b):
    Bsz, S, D = u.shape
    H, N = RWKV_HEADS, RWKV_HEAD
    xx = jnp.pad(u, ((0, 0), (1, 0), (0, 0)))[:, :S] - u
    xr, xw, xk, xv, xa, xg = [u + xx * mu[j] for j in range(6)]
    r = xr @ w_r
    k = xk @ w_k
    v = xv @ w_v
    w_log = -jax.nn.softplus(-(w0 + jnp.tanh(xw @ w1) @ w2)) - 0.5
    decay = jnp.exp(-jnp.exp(w_log.astype(jnp.float32)))
    a = jax.nn.sigmoid((a0 + (xa @ a1) @ a2).astype(jnp.float32))
    g = jax.nn.sigmoid(xg @ g1) @ g2
    kk = (k * k_k).reshape(Bsz, S, H, N).astype(jnp.float32)
    kk = kk * lax.rsqrt(jnp.maximum(jnp.sum(kk * kk, axis=-1, keepdims=True), 1e-24))
    k = k * (1.0 + (a - 1.0) * k_a)
    heads = lambda t: t.reshape(Bsz, S, H, N)
    r_h, k_h, v_h, w_h, a_h = heads(r), heads(k), heads(v), heads(decay), heads(a)
    aa = -kk
    bb = kk * a_h

    def step(state, inp):
        r_t, w_t, k_t, v_t, aa_t, bb_t = inp
        sa = jnp.einsum('bhij,bhj->bhi', state, aa_t)
        state = (state * w_t[:, :, None, :] + sa[..., None] * bb_t[:, :, None, :]
                 + v_t[..., None] * k_t[:, :, None, :])
        return state, jnp.einsum('bhij,bhj->bhi', state, r_t)

    seq_first = lambda t: jnp.moveaxis(t, 1, 0)
    state0 = jnp.zeros((Bsz, H, N, N), jnp.float32)
    _, y = lax.scan(step, state0, (seq_first(r_h), seq_first(w_h), seq_first(k_h),
                                   seq_first(v_h), seq_first(aa), seq_first(bb)))
    y = jnp.moveaxis(y, 0, 1)
    mean = jnp.mean(y, axis=-1, keepdims=True)
    var = jnp.mean((y - mean) ** 2, axis=-1, keepdims=True)
    y = ((y - mean) * lax.rsqrt(var + RWKV_LN_EPS)).reshape(Bsz, S, D) * lnx_w + lnx_b
    bonus = jnp.sum(r_h * k_h * r_k, axis=-1, keepdims=True) * v_h
    y = y + bonus.reshape(Bsz, S, D)
    return (y * g).astype(u.dtype) @ w_o

def hier_moe(h, wg, bg, we, be, w1, w3, w2):
    Bsz, S, D = h.shape
    t = h.reshape(-1, D)
    g_logits = (t @ wg + bg).astype(jnp.float32)
    g_prob = jax.nn.softmax(g_logits, axis=-1)
    g_idx = jnp.argmax(g_logits, axis=-1)
    g_gate = jnp.take_along_axis(g_prob, g_idx[:, None], axis=-1)[:, 0]
    e_logits = (t @ we + be).astype(jnp.float32).reshape(-1, MOE_GROUPS, MOE_EXPERTS_PER_GROUP)
    e_sel = jnp.take_along_axis(e_logits, g_idx[:, None, None], axis=1)[:, 0]
    top_v, top_i = lax.top_k(e_sel, MOE_TOP_K)
    top_w = jax.nn.softmax(top_v, axis=-1) * g_gate[:, None]
    expert_id = g_idx[:, None] * MOE_EXPERTS_PER_GROUP + top_i
    combine = jnp.sum(jax.nn.one_hot(expert_id, MOE_EXPERTS, dtype=jnp.float32) * top_w[..., None], axis=1)
    out = jnp.zeros(t.shape, jnp.float32)
    for e in range(MOE_EXPERTS):
        he = jax.nn.silu(t @ w1[e]) * (t @ w3[e])
        out = out + combine[:, e:e + 1] * (he @ w2[e])
    return out.reshape(Bsz, S, D).astype(h.dtype)

def setup_inputs(seed: int = 0) -> dict:
    key = jax.random.key(seed)
    ks = iter(jax.random.split(key, 64))
    f32 = jnp.float32
    nrm = lambda shape, scale: scale * jax.random.normal(next(ks), shape, f32)
    D = D_MODEL
    NE = (DEPTH + 1) // 2
    NO = DEPTH // 2
    x = nrm((BATCH, SEQ, D), 1.0)
    norm_mix_w = 1.0 + nrm((DEPTH, D), 0.02)
    norm_ffn_w = 1.0 + nrm((DEPTH, D), 0.02)
    norm_final_w = 1.0 + nrm((D,), 0.02)
    w_in_e = nrm((NE, D, IN_PROJ_DIM), D ** -0.5)
    ssd_conv_w = nrm((NE, SSD_CONV, SSD_CONV_DIM), SSD_CONV ** -0.5)
    ssd_conv_b = nrm((NE, SSD_CONV_DIM), 0.02)
    dt = jnp.exp(jax.random.uniform(next(ks), (NE, SSD_HEADS), f32, math.log(1e-3), math.log(1e-1)))
    ssd_dt_bias = dt + jnp.log(-jnp.expm1(-dt))
    ssd_a_log = jnp.log(jax.random.uniform(next(ks), (NE, SSD_HEADS), f32, 1.0, 16.0))
    ssd_d = 1.0 + nrm((NE, SSD_HEADS), 0.1)
    ssd_norm_w = 1.0 + nrm((NE, SSD_D_INNER), 0.02)
    w_out_e = nrm((NE, MIX_WIDTH, D), MIX_WIDTH ** -0.5)
    rw_mu = jax.random.uniform(next(ks), (NO, 6, D), f32, 0.0, 1.0)
    rw_wr = nrm((NO, D, D), D ** -0.5)
    rw_wk = nrm((NO, D, D), D ** -0.5)
    rw_wv = nrm((NO, D, D), D ** -0.5)
    rw_wo = nrm((NO, D, D), D ** -0.5)
    ramp = jnp.linspace(0.0, 1.0, D, dtype=f32) ** 0.9
    rw_w0 = -6.0 + 5.0 * ramp + nrm((NO, D), 0.1)
    rw_w1 = nrm((NO, D, RWKV_DECAY_LORA), D ** -0.5)
    rw_w2 = nrm((NO, RWKV_DECAY_LORA, D), 0.1 * RWKV_DECAY_LORA ** -0.5)
    rw_a0 = nrm((NO, D), 0.1)
    rw_a1 = nrm((NO, D, RWKV_A_LORA), D ** -0.5)
    rw_a2 = nrm((NO, RWKV_A_LORA, D), 0.5 * RWKV_A_LORA ** -0.5)
    rw_g1 = nrm((NO, D, RWKV_GATE_LORA), D ** -0.5)
    rw_g2 = nrm((NO, RWKV_GATE_LORA, D), RWKV_GATE_LORA ** -0.5)
    rw_kk = 0.85 + nrm((NO, D), 0.02)
    rw_ka = 1.0 + nrm((NO, D), 0.02)
    rw_rk = nrm((NO, RWKV_HEADS, RWKV_HEAD), 0.1)
    rw_lnx_w = 1.0 + nrm((NO, D), 0.02)
    rw_lnx_b = nrm((NO, D), 0.02)
    moe_wg = nrm((DEPTH, D, MOE_GROUPS), D ** -0.5)
    moe_bg = nrm((DEPTH, MOE_GROUPS), 0.01)
    moe_we = nrm((DEPTH, D, MOE_EXPERTS), D ** -0.5)
    moe_be = nrm((DEPTH, MOE_EXPERTS), 0.01)
    moe_w1 = nrm((DEPTH, MOE_EXPERTS, D, MOE_D_FF), D ** -0.5)
    moe_w3 = nrm((DEPTH, MOE_EXPERTS, D, MOE_D_FF), D ** -0.5)
    moe_w2 = nrm((DEPTH, MOE_EXPERTS, MOE_D_FF, D), MOE_D_FF ** -0.5)
    return {"x": x, "norm_mix_w": norm_mix_w, "norm_ffn_w": norm_ffn_w, "norm_final_w": norm_final_w,
            "w_in_e": w_in_e, "ssd_conv_w": ssd_conv_w, "ssd_conv_b": ssd_conv_b,
            "ssd_dt_bias": ssd_dt_bias, "ssd_a_log": ssd_a_log, "ssd_d": ssd_d,
            "ssd_norm_w": ssd_norm_w, "w_out_e": w_out_e,
            "rw_mu": rw_mu, "rw_wr": rw_wr, "rw_wk": rw_wk, "rw_wv": rw_wv, "rw_wo": rw_wo,
            "rw_w0": rw_w0, "rw_w1": rw_w1, "rw_w2": rw_w2, "rw_a0": rw_a0, "rw_a1": rw_a1,
            "rw_a2": rw_a2, "rw_g1": rw_g1, "rw_g2": rw_g2, "rw_kk": rw_kk, "rw_ka": rw_ka,
            "rw_rk": rw_rk, "rw_lnx_w": rw_lnx_w, "rw_lnx_b": rw_lnx_b,
            "moe_wg": moe_wg, "moe_bg": moe_bg, "moe_we": moe_we, "moe_be": moe_be,
            "moe_w1": moe_w1, "moe_w3": moe_w3, "moe_w2": moe_w2}

def reference(x, norm_mix_w, norm_ffn_w, norm_final_w,
              w_in_e, ssd_conv_w, ssd_conv_b, ssd_dt_bias, ssd_a_log, ssd_d, ssd_norm_w, w_out_e,
              rw_mu, rw_wr, rw_wk, rw_wv, rw_wo, rw_w0, rw_w1, rw_w2, rw_a0, rw_a1, rw_a2,
              rw_g1, rw_g2, rw_kk, rw_ka, rw_rk, rw_lnx_w, rw_lnx_b,
              moe_wg, moe_bg, moe_we, moe_be, moe_w1, moe_w3, moe_w2):
    pos = jnp.arange(x.shape[1], dtype=jnp.float32)
    h = x
    for layer in range(DEPTH):
        i = layer // 2
        u = rms_norm(h, norm_mix_w[layer])
        if layer % 2 == 0:
            mix = ssd_retention_layer(u, pos, w_in_e[i], ssd_conv_w[i], ssd_conv_b[i], ssd_dt_bias[i],
                                      ssd_a_log[i], ssd_d[i], ssd_norm_w[i], w_out_e[i])
        else:
            mix = rwkv7_layer(u, rw_mu[i], rw_wr[i], rw_wk[i], rw_wv[i], rw_wo[i], rw_w0[i], rw_w1[i],
                              rw_w2[i], rw_a0[i], rw_a1[i], rw_a2[i], rw_g1[i], rw_g2[i], rw_kk[i],
                              rw_ka[i], rw_rk[i], rw_lnx_w[i], rw_lnx_b[i])
        h = h + mix
        h = h + hier_moe(rms_norm(h, norm_ffn_w[layer]), moe_wg[layer], moe_bg[layer], moe_we[layer],
                         moe_be[layer], moe_w1[layer], moe_w3[layer], moe_w2[layer])
    return rms_norm(h, norm_final_w)


_drawn_inputs = setup_inputs


def setup_inputs(seed=0):
    import zlib

    import numpy as np

    out = dict(_drawn_inputs(seed))
    spreads = {}
    factors = {'norm_final_w': 2.996,
     'rw_w1': 7.85,
     'rw_w2': 8.0,
     'rw_kk': 5.086,
     'rw_ka': 3.61,
     'rw_lnx_w': 3.757,
     'rw_lnx_b': 4.879,
     'moe_bg': 3.303,
     'moe_be': 4.424}
    for name, (base, spread) in spreads.items():
        noise = np.random.default_rng([zlib.crc32(name.encode()), seed]).standard_normal(out[name].shape)
        drawn = base * np.exp(spread * noise) if base else spread * noise
        out[name] = __import__('jax').numpy.asarray(drawn.astype(out[name].dtype))
    for name, factor in factors.items():
        out[name] = (out[name] * factor).astype(out[name].dtype)
    return out
```

```python
from contextlib import ExitStack

import concourse.bass as bass
import numpy as np
from concourse import mybir

ALU = mybir.AluOpType
ACT = mybir.ActivationFunctionType
F32 = mybir.dt.float32
I32 = mybir.dt.int32
U32 = mybir.dt.uint32
AX = mybir.AxisListType

P = 128
SEQ, D = 512, 1024
NT = SEQ // P
KD = D // P
HALF = 512
DEPTH = 2
RMS_EPS = 1e-6
S_HEADS, S_HD, S_GROUPS, S_N, S_CONV = 16, 64, 2, 128, 4
S_HPG = S_HEADS // S_GROUPS
XBC_BLOCKS = (D + 2 * S_GROUPS * S_N) // P
XPAD = SEQ + S_CONV - 1
R_HEADS, R_QK, R_V = 4, 128, 256
W_HEADS, W_HD, W_LORA, G_LORA = 16, 64, 64, 160
LN_EPS = 64e-5
LOG_DECAY = -float(np.exp(-0.5))
LEVELS = 7
GROUPS, EPG = 4, 4
EXPERTS, FF = GROUPS * EPG, 512
SLOTS = P
MAX_BLOCKS = 24

Z0, X0 = 0, D
DT0 = X0 + XBC_BLOCKS * P
Q0 = DT0 + S_HEADS
K0 = Q0 + R_HEADS * R_QK
V0 = K0 + R_HEADS * R_QK
G0 = V0 + D
IN_CHUNKS = ([("x", X0 + HALF * i, HALF) for i in range(3)] + [("q", Q0, HALF), ("k", K0, HALF)]
             + [("dt", DT0, S_HEADS)] + [("v", V0, HALF), ("v", V0 + HALF, HALF)]
             + [("z", Z0, HALF), ("z", Z0 + HALF, HALF), ("g", G0, HALF), ("g", G0 + HALF, HALF)])

COLS = {}
for _n, _w in (("mix0", KD), ("mix1", KD), ("ffn0", KD), ("ffn1", KD), ("conv", S_CONV * XBC_BLOCKS),
               ("convb", XBC_BLOCKS), ("ssdn", KD), ("mu", 6 * KD), ("w0", KD), ("a0", KD), ("kk", KD),
               ("ka", KD), ("rk", KD)):
    COLS[_n] = (sum(w for _, w in COLS.values()), _w)
N_COLS = sum(w for _, w in COLS.values())
ROWS = {}
for _n, _w in (("dtb", S_HEADS), ("alog", S_HEADS), ("dskip", S_HEADS), ("mb0", GROUPS + EXPERTS), ("mb1", GROUPS + EXPERTS)):
    ROWS[_n] = (sum(w for _, w in ROWS.values()), _w)
N_ROWS = sum(w for _, w in ROWS.values())


def shape_constants():
    i = np.arange(P)
    f = np.float32
    ident = np.eye(P)
    upto = (i[:, None] <= i[None, :])
    before = (i[:, None] < i[None, :])
    neg = np.where(upto, 0.0, -1e30)
    same_half = (i[:, None] // 64 == i[None, :] // 64)
    half_sel = np.stack([i < 64, i >= 64], 1)
    iota4 = np.tile(np.arange(4), (P, 1))
    blk = np.tile(np.arange(MAX_BLOCKS), (P, 1))
    common = np.concatenate([ident, upto, before, neg, same_half, half_sel, iota4, blk, np.ones((P, P))], 1).astype(f)
    lg = np.log(1.0 - 2.0 ** (-5.0 - np.arange(R_HEADS)))
    ret = np.where(upto[:, None, :], np.exp(-(i[:, None, None] + 1.0) * lg[None, :, None]) * R_QK ** -0.5, 0.0)
    qdec = np.exp((i[:, None] + 1.0) * lg[None])
    kdec = np.exp((P - 1.0 - i[:, None]) * lg[None]) * R_QK ** -0.5
    half = R_QK // 2
    inv = f(10000.0) ** (-np.arange(half, dtype=f) / f(half))
    ang = np.arange(SEQ, dtype=f)[:, None] * inv[None]
    cos = np.cos(ang.astype(np.float64)).reshape(NT, P, half).transpose(1, 0, 2).reshape(P, -1)
    sin = np.sin(ang.astype(np.float64)).reshape(NT, P, half).transpose(1, 0, 2).reshape(P, -1)
    layer0 = np.concatenate([ret.reshape(P, -1), qdec, kdec, cos, sin], 1).astype(f)
    lev = []
    for l in range(LEVELS):
        b = i >> l
        lev.append((b[:, None] >> 1 == b[None, :] >> 1) & (b[:, None] & 1 == 1) & (b[None, :] & 1 == 0))
    low = np.stack(lev, 1)
    up = np.stack([m.T for m in lev], 1)
    layer1 = np.concatenate([low.reshape(P, -1), up.reshape(P, -1)], 1).astype(f)
    return common, layer0, layer1


C_IDENT, C_UPTO, C_BEFORE, C_NEG, C_SAME = (P * n for n in range(5))
C_HALF = 5 * P
C_IOTA = C_HALF + 2
C_BLK = C_IOTA + 4
C_ONES = C_BLK + MAX_BLOCKS
C_ALL = C_ONES + P
L0_RET = 0
L0_QDEC = R_HEADS * P
L0_KDEC = L0_QDEC + R_HEADS
L0_COS = L0_KDEC + R_HEADS
L0_SIN = L0_COS + NT * R_QK // 2
L0_ALL = L0_SIN + NT * R_QK // 2
L1_ALL = 2 * LEVELS * P


class Chain:

    def __init__(self, engine, sem):
        self.engine, self.sem, self.n = engine, sem, 0

    def add(self, ins):
        ins.then_inc(self.sem, 1)
        self.n += 1
        return self.n

    def wait(self, n=None):
        self.engine.wait_ge(self.sem, self.n if n is None else n)

    def link(self, ins):
        self.add(ins)
        self.wait()


class Trunk:

    def __init__(self, nc):
        self.nc, self.phase_semaphores = nc, []

    def semaphore(self, name):
        self.phase_semaphores.append(self.nc.alloc_semaphore(name))
        return self.phase_semaphores[-1]

    def recycle_semaphores(self):
        self.nc.clear_and_free_semaphores(self.phase_semaphores)
        self.nc.all_engine_barrier()
        self.phase_semaphores = []


def wide(ap, *shape):
    return ap.to_broadcast(list(shape))


def norm_phase(t, tag, w_col, xn, ut):
    nc = t.nc
    with ExitStack() as c:
        s_ms = t.semaphore(f"{tag}_ms")
        s_rs = t.semaphore(f"{tag}_rs")
        s_xn = t.semaphore(f"{tag}_xn")
        s_tr = t.semaphore(f"{tag}_transposed")
        s_ev = t.semaphore(f"{tag}_evacuated")
        ms = c.enter_context(nc.sbuf_tensor(f"{tag}_ms", [P, NT], F32))
        block = c.enter_context(nc.Block())

        @block.vector
        def _(dve):
            def evacuate(m):
                for b in range(2):
                    dve.wait_ge(s_tr, 2 * m + b + 1)
                    nc.vector.tensor_tensor(ut[:, 4 * b:4 * b + 4, m * P:(m + 1) * P],
                                            t.bank[(2 * m + b) % 8][:, :].rearrange("p (k n) -> p k n", k=4),
                                            wide(w_col[:, 4 * b:4 * b + 4].unsqueeze(2), P, 4, P), ALU.mult).then_inc(s_ev, 1)

            for m in range(NT):
                nc.vector.tensor_tensor_reduce(xn[:, m, :], t.h[:, m, :], t.h[:, m, :], 1.0 / D, 0.0,
                                               ALU.mult, ALU.add, ms[:, m:m + 1]).then_inc(s_ms, 1)
            dve.wait_ge(s_rs, 1)
            nc.vector.reciprocal(ms[:, :], ms[:, :]).then_inc(s_rs, 1)
            dve.wait_ge(s_rs, 2)
            for m in range(NT):
                nc.vector.tensor_scalar(xn[:, m, :], t.h[:, m, :], ms[:, m:m + 1], None, ALU.mult).then_inc(s_xn, 1)
                if m:
                    evacuate(m - 1)
            evacuate(NT - 1)

        @block.scalar
        def _(act):
            act.wait_ge(s_ms, NT)
            nc.scalar.activation(ms[:, :], ms[:, :], ACT.Sqrt, bias=t.eps[:, 0:1]).then_inc(s_rs, 1)

        @block.tensor
        def _(pe):
            for m in range(NT):
                pe.wait_ge(s_xn, m + 1)
                for k in range(KD):
                    mm = nc.tensor.transpose(t.bank[(2 * m + k // 4) % 8][:, (k % 4) * P:(k % 4 + 1) * P],
                                             xn[:, m, k * P:(k + 1) * P], t.ident)
                    if k % 4 == 3:
                        mm.then_inc(s_tr, 1)


def load_phase(t, a):
    nc = t.nc
    with ExitStack() as c:
        s_ld = t.semaphore("loaded")
        s_z = t.semaphore("zero_tile")
        block = c.enter_context(nc.Block())

        @block.sync
        def _(sp):
            sp.dma_start(t.h[:, :, :], a["x"].rearrange("o (m p) d -> p (o m) d", p=P)).then_inc(s_ld, 16)
            sp.dma_start(t.cols[:, :], a["cols"]).then_inc(s_ld, 16)
            sp.dma_start(t.common[:, :], a["common"]).then_inc(s_ld, 16)
            sp.dma_start(t.l0c[:, :], a["layer0"]).then_inc(s_ld, 16)
            sp.dma_start(t.rows[:, :], wide(a["rows"], P, N_ROWS)).then_inc(s_ld, 16)
            sp.wait_ge(s_ld, 5 * 16)
            for n in range(2):
                _, c0, width = IN_CHUNKS[n]
                sp.dma_start(t.ring[n][:, :, 0:width], a["w_in_e"][0].rearrange("(k p) n -> p k n", p=P)[:, :, c0:c0 + width]).then_inc(t.s_win[n % 2], 16)

        @block.vector
        def _(dve):
            nc.vector.memset(t.zero[:, :], 0.0).then_inc(s_z, 1)
            for i, eps in enumerate((RMS_EPS, 1e-5, LN_EPS)):
                nc.vector.memset(t.eps[:, i:i + 1], eps)

        @block.gpsimd
        def _(pool):
            pool.wait_ge(s_z, 1)
            for b in range(MAX_BLOCKS):
                pool.dma_start(t.xg[b * SLOTS:(b + 1) * SLOTS, :], t.zero[:, :]).then_inc(t.s_clear, 16)


def in_proj_phase(t, a, ut, xbc, xc, z, g, v, q, k, dt):
    nc = t.nc
    win = a["w_in_e"][0].rearrange("(k p) n -> p k n", p=P)
    out = {"z": z, "g": g, "v": v, "q": q, "k": k}
    first = {"z": Z0, "g": G0, "v": V0, "q": Q0, "k": K0}
    order = [kind for kind, _, _ in IN_CHUNKS]
    n_x = order.count("x")
    with ExitStack() as c:
        s_pe = t.semaphore("in_group")
        s_ev = t.semaphore("in_evacuated")
        s_pad = t.semaphore("in_pad")
        s_dve = t.semaphore("in_dve")
        s_conv = t.semaphore("in_conv")
        block = c.enter_context(nc.Block())

        @block.sync
        def _(sp):
            for n in range(2, len(IN_CHUNKS)):
                sp.wait_ge(s_pe, NT * (n - 1))
                _, c0, width = IN_CHUNKS[n]
                sp.dma_start(t.ring[n % 2][:, :, 0:width], win[:, :, c0:c0 + width]).then_inc(t.s_win[n % 2], 16)

        @block.tensor
        def _(pe):
            for n, (kind, _, width) in enumerate(IN_CHUNKS):
                pe.wait_ge(t.s_win[n % 2], 16 * (n // 2 + 1))
                w = t.ring[n % 2]
                for m in range(NT):
                    i = NT * n + m
                    if i >= 8:
                        pe.wait_ge(s_ev, i - 7)
                    for kk in range(KD):
                        if kind == "x":
                            mm = nc.tensor.matmul(t.bank[i % 8][:, :], w[:, kk, m * P:(m + 1) * P], ut[:, kk, :],
                                                  start=kk == 0, stop=kk == KD - 1)
                        else:
                            mm = nc.tensor.matmul(t.bank[i % 8][:, 0:width], ut[:, kk, m * P:(m + 1) * P],
                                                  w[:, kk, 0:width], start=kk == 0, stop=kk == KD - 1)
                    mm.then_inc(s_pe, 1)

        @block.scalar
        def _(act):
            act.wait_ge(s_pad, 1)
            for n, (kind, c0, width) in enumerate(IN_CHUNKS):
                for m in range(NT):
                    i = NT * n + m
                    act.wait_ge(s_pe, i + 1)
                    src = t.bank[i % 8]
                    if kind == "x":
                        nc.scalar.activation(xbc[:, NT * n + m, S_CONV - 1:XPAD], src[:, :], ACT.Copy).then_inc(s_ev, 1)
                    elif kind == "dt":
                        nc.scalar.activation(dt[:, m, :], src[:, 0:width], ACT.Copy).then_inc(s_ev, 1)
                    else:
                        o = c0 - first[kind]
                        nc.scalar.activation(out[kind][:, m, o:o + width], src[:, 0:width],
                                             ACT.Silu if kind in "zg" else ACT.Copy).then_inc(s_ev, 1)
            act.wait_ge(s_conv, XBC_BLOCKS)
            for b in range(XBC_BLOCKS):
                nc.scalar.activation(xc[:, b, :], xc[:, b, :], ACT.Silu)

        @block.vector
        def _(dve):
            chain = Chain(dve, s_dve)
            nc.vector.memset(xbc[:, :, 0:S_CONV - 1], 0.0).then_inc(s_pad, 1)
            cw, cb = t.col("conv"), t.col("convb")
            for b in range(XBC_BLOCKS):
                dve.wait_ge(s_ev, b + 1)
                chain.link(nc.vector.tensor_scalar(xc[:, b, :], xbc[:, b, 0:SEQ], cw[:, b:b + 1], cb[:, b:b + 1],
                                                   ALU.mult, ALU.add))
                for j in range(1, S_CONV):
                    w = cw[:, j * XBC_BLOCKS + b:j * XBC_BLOCKS + b + 1]
                    ins = nc.vector.scalar_tensor_tensor(out=xc[:, b, :], in0=xbc[:, b, j:j + SEQ], scalar=w,
                                                         in1=xc[:, b, :], op0=ALU.mult, op1=ALU.add)
                    if j < S_CONV - 1:
                        chain.link(ins)
                    else:
                        ins.then_inc(s_conv, 1)


def rope(nc, chain, t, dst, src, tmp, s_done):
    h = R_QK // 2
    s4 = src[:, :, :].rearrange("p m (h d) -> p m h d", h=R_HEADS)
    d4 = dst[:, :, :].rearrange("p m (h d) -> p m h d", h=R_HEADS)
    cos = t.l0c[:, L0_COS:L0_SIN].rearrange("p (m d) -> p m d", m=NT)
    sin = t.l0c[:, L0_SIN:L0_ALL].rearrange("p (m d) -> p m d", m=NT)
    for m in range(NT):
        c = wide(cos[:, m, :].unsqueeze(1), P, R_HEADS, h)
        s = wide(sin[:, m, :].unsqueeze(1), P, R_HEADS, h)
        x1, x2, y1, y2 = s4[:, m, :, 0:h], s4[:, m, :, h:], d4[:, m, :, 0:h], d4[:, m, :, h:]
        chain.add(nc.vector.tensor_tensor(y1, x1, c, ALU.mult))
        chain.add(nc.vector.tensor_tensor(tmp[:, 0, m], x2, s, ALU.mult))
        chain.add(nc.vector.tensor_tensor(y2, x1, s, ALU.mult))
        chain.add(nc.vector.tensor_tensor(tmp[:, 1, m], x2, c, ALU.mult))
    chain.wait()
    for m in range(NT):
        y1, y2 = d4[:, m, :, 0:h], d4[:, m, :, h:]
        nc.vector.tensor_tensor(y1, y1, tmp[:, 0, m], ALU.subtract).then_inc(s_done, 1)
        nc.vector.tensor_tensor(y2, y2, tmp[:, 1, m], ALU.add).then_inc(s_done, 1)


def rows_phase(t, xc, xs, bt, q, k, qr, kr, qt, kt, kd, tmp, dt, a_dt, nacum, cum, ecum, ea):
    nc = t.nc
    n_x, n_b, n_q = KD * NT // 4, S_GROUPS * NT // 4, 2 * R_HEADS
    with ExitStack() as c:
        s_tr = t.semaphore("row_transposed")
        s_ev = t.semaphore("row_evacuated")
        s_dve = t.semaphore("row_dve")
        s_abs = t.semaphore("row_abs")
        s_exp = t.semaphore("row_exp")
        s_rope = t.semaphore("row_rope")
        s_a = t.semaphore("row_a")
        s_sum = t.semaphore("row_sum")
        s_cum = t.semaphore("row_cum")
        block = c.enter_context(nc.Block())

        @block.tensor
        def _(pe):
            todo = [[xc[:, b + j, m * P:(m + 1) * P] for j in range(4)] for m in range(NT) for b in (0, 4)]
            todo += [[xc[:, KD + j % 2, (m + j // 2) * P:(m + j // 2 + 1) * P] for j in range(4)] for m in (0, 2)]
            todo += [[src[:, m, h * P:(h + 1) * P] for m in range(NT)] for src in (qr, kr) for h in range(R_HEADS)]
            for n, four in enumerate(todo):
                if n == n_x + n_b:
                    pe.wait_ge(s_a, 1)
                    nc.tensor.matmul(t.bank[7][:, 0:NT * S_HEADS], t.common[:, C_UPTO:C_UPTO + P], a_dt[:, :], start=True, stop=True)
                    nc.tensor.matmul(t.bank[7][:, NT * S_HEADS:2 * NT * S_HEADS], t.common[:, C_ONES:C_ONES + P], a_dt[:, :],
                                     start=True, stop=True).then_inc(s_sum, 1)
                    pe.wait_ge(s_rope, 2 * NT)
                if n == n_x + n_b + R_HEADS:
                    pe.wait_ge(s_rope, 4 * NT)
                if n >= 7:
                    pe.wait_ge(s_ev, n - 6)
                for j, src in enumerate(four):
                    mm = nc.tensor.transpose(t.bank[n % 7][:, j * P:(j + 1) * P], src, t.ident)
                mm.then_inc(s_tr, 1)

        @block.scalar
        def _(act):
            act.wait_ge(s_abs, 1)
            nc.scalar.activation(ea[:, 0:NT * S_HEADS], ea[:, 0:NT * S_HEADS], ACT.Exp, scale=-1.0).then_inc(s_exp, 1)
            nc.scalar.activation(ea[:, NT * S_HEADS:], t.row("alog"), ACT.Exp).then_inc(s_exp, 1)
            act.wait_ge(s_exp, 1)
            nc.scalar.activation(ea[:, 0:NT * S_HEADS], ea[:, 0:NT * S_HEADS], ACT.Ln, bias=1.0).then_inc(s_exp, 1)
            for n in range(n_x + n_b + n_q):
                act.wait_ge(s_tr, n + 1)
                if n < n_x:
                    dst = xs[:, n // 2, (n % 2) * HALF:(n % 2 + 1) * HALF]
                elif n < n_x + n_b:
                    dst = bt[:, 2 * (n - n_x):2 * (n - n_x) + 2, :].rearrange("p a b -> p (a b)")
                else:
                    dst = (qt, kt)[(n - n_x - n_b) // R_HEADS][:, (n - n_x - n_b) % R_HEADS, :]
                nc.scalar.activation(dst, t.bank[n % 7][:, :], ACT.Copy).then_inc(s_ev, 1)
            act.wait_ge(s_cum, 3)
            nc.scalar.activation(ecum[:, :], cum[:, :], ACT.Exp)

        @block.vector
        def _(dve):
            ch = Chain(dve, s_dve)
            w = NT * S_HEADS
            per_head = wide(t.row("dtb").unsqueeze(1), P, NT, S_HEADS)
            ch.link(nc.vector.tensor_tensor(dt[:, :, :], dt[:, :, :], per_head, ALU.add))
            flat = dt[:, :, :].rearrange("p m h -> p (m h)")
            nc.vector.scalar_tensor_tensor(out=ea[:, 0:w], in0=flat, scalar=-1.0, in1=flat, op0=ALU.mult, op1=ALU.max).then_inc(s_abs, 1)
            ch.link(nc.vector.tensor_scalar(flat, flat, 0.0, None, ALU.max))
            dve.wait_ge(s_exp, 3)
            ch.link(nc.vector.tensor_tensor(flat, flat, ea[:, 0:w], ALU.add))
            a3 = a_dt[:, :].rearrange("p (m h) -> p m h", m=NT)
            nc.vector.scalar_tensor_tensor(out=a3, in0=dt[:, :, :], scalar=-1.0, in1=wide(ea[:, w:].unsqueeze(1), P, NT, S_HEADS),
                                           op0=ALU.mult, op1=ALU.mult).then_inc(s_a, 1)
            rope(nc, ch, t, qr, q, tmp, s_rope)
            dve.wait_ge(s_sum, 1)
            nc.vector.tensor_copy(cum[:, 0:2 * w], t.bank[7][:, 0:2 * w]).then_inc(s_cum, 1)
            dve.wait_ge(s_cum, 1)
            nc.vector.tensor_scalar(nacum[:, :], cum[:, 0:w], -1.0, None, ALU.mult).then_inc(s_cum, 1)
            nc.vector.tensor_tensor(cum[:, 2 * w:], cum[:, w:2 * w], cum[:, 0:w], ALU.subtract).then_inc(s_cum, 1)
            dve.wait_ge(s_rope, 2 * NT)
            rope(nc, ch, t, kr, k, tmp, s_rope)
            dve.wait_ge(s_rope, 4 * NT)
            for h in range(R_HEADS):
                hs = slice(h * R_QK, (h + 1) * R_QK)
                nc.vector.tensor_scalar(kd[:, :, hs], kr[:, :, hs], t.l0c[:, L0_KDEC + h:L0_KDEC + h + 1], None, ALU.mult)


def retention_phase(t, qt, kt, kd, v, g, s, state, yraw, y):
    nc = t.nc
    gamma = [1.0 - 2.0 ** (-5.0 - h) for h in range(R_HEADS)]
    with ExitStack() as c:
        s_qk = t.semaphore("ret_scores")
        s_msk = t.semaphore("ret_masked")
        s_y = t.semaphore("ret_y")
        s_up = t.semaphore("ret_update")
        s_st = t.semaphore("ret_state")
        s_raw = t.semaphore("ret_raw")
        s_ms = t.semaphore("ret_ms")
        s_rs = t.semaphore("ret_rs")
        ss = c.enter_context(nc.sbuf_tensor("ret_ss", [P, NT, R_HEADS], F32))
        block = c.enter_context(nc.Block())

        @block.tensor
        def _(pe):
            def scores(m):
                ms = slice(m * P, (m + 1) * P)
                if m >= 2:
                    pe.wait_ge(s_msk, m - 1)
                for h in range(R_HEADS):
                    mm = nc.tensor.matmul(t.bank[m % 2][:, h * P:(h + 1) * P], kt[:, h, ms], qt[:, h, ms], start=True, stop=True)
                mm.then_inc(s_qk, 1)

            scores(0)
            for m in range(NT):
                if m + 1 < NT:
                    scores(m + 1)
                    if m:
                        pe.wait_ge(s_st, R_HEADS * m)
                    for h in range(R_HEADS):
                        mm = nc.tensor.matmul(t.bank[6 + h // 2][:, (h % 2) * R_V:(h % 2 + 1) * R_V], kd[:, m, h * P:(h + 1) * P],
                                              v[:, m, h * R_V:(h + 1) * R_V], start=True, stop=True)
                    mm.then_inc(s_up, 1)
                pe.wait_ge(s_msk, m + 1)
                if m >= 2:
                    pe.wait_ge(s_raw, R_HEADS * (m - 1))
                if m:
                    pe.wait_ge(s_st, R_HEADS * m)
                for h in range(R_HEADS):
                    o = t.bank[2 + 2 * (m % 2) + h // 2][:, (h % 2) * R_V:(h % 2 + 1) * R_V]
                    mm = nc.tensor.matmul(o, s[:, m % 2, h, :], v[:, m, h * R_V:(h + 1) * R_V], start=True, stop=m == 0)
                    if m:
                        mm = nc.tensor.matmul(o, qt[:, h, m * P:(m + 1) * P], state[:, (m - 1) % 2, h, :], start=False, stop=True)
                mm.then_inc(s_y, 1)

        @block.scalar
        def _(act):
            for m in range(NT):
                act.wait_ge(s_y, m + 1)
                for h in range(R_HEADS):
                    o = t.bank[2 + 2 * (m % 2) + h // 2][:, (h % 2) * R_V:(h % 2 + 1) * R_V]
                    nc.scalar.activation(yraw[:, m, h * R_V:(h + 1) * R_V], o, ACT.Copy,
                                         scale=t.l0c[:, L0_QDEC + h:L0_QDEC + h + 1]).then_inc(s_raw, 1)
            act.wait_ge(s_ms, NT * R_HEADS)
            nc.scalar.activation(ss[:, :, :], ss[:, :, :], ACT.Sqrt, bias=t.eps[:, 0:1]).then_inc(s_rs, 1)

        @block.vector
        def _(dve):
            table = t.l0c[:, L0_RET:L0_RET + R_HEADS * P].rearrange("p (h n) -> p h n", h=R_HEADS)

            def squares(m):
                dve.wait_ge(s_raw, R_HEADS * (m + 1))
                for h in range(R_HEADS):
                    hs = slice(h * R_V, (h + 1) * R_V)
                    nc.vector.tensor_tensor_reduce(y[:, m, hs], yraw[:, m, hs], yraw[:, m, hs], 1.0 / R_V, 0.0, ALU.mult, ALU.add,
                                                   ss[:, m, h:h + 1]).then_inc(s_ms, 1)

            def norm(m):
                for h in range(R_HEADS):
                    hs = slice(h * R_V, (h + 1) * R_V)
                    nc.vector.scalar_tensor_tensor(out=y[:, m, hs], in0=yraw[:, m, hs], scalar=ss[:, m, h:h + 1],
                                                   in1=g[:, m, hs], op0=ALU.mult, op1=ALU.mult)

            for m in range(NT):
                dve.wait_ge(s_qk, m + 1)
                if m >= 2:
                    dve.wait_ge(s_y, m - 1)
                nc.vector.tensor_tensor(s[:, m % 2], t.bank[m % 2][:, :].rearrange("p (h n) -> p h n", h=R_HEADS), table,
                                        ALU.mult).then_inc(s_msk, 1)
                if m + 1 < NT:
                    dve.wait_ge(s_up, m + 1)
                    if m:
                        dve.wait_ge(s_st, R_HEADS * m)
                    if m >= 2:
                        dve.wait_ge(s_y, m)
                    for h in range(R_HEADS):
                        up = t.bank[6 + h // 2][:, (h % 2) * R_V:(h % 2 + 1) * R_V]
                        if m:
                            ins = nc.vector.scalar_tensor_tensor(out=state[:, m % 2, h, :], in0=state[:, (m - 1) % 2, h, :],
                                                                 scalar=gamma[h] ** P, in1=up, op0=ALU.mult, op1=ALU.add)
                        else:
                            ins = nc.vector.tensor_copy(state[:, m % 2, h, :], up)
                        ins.then_inc(s_st, 1)
                if m:
                    squares(m - 1)
            squares(NT - 1)
            dve.wait_ge(s_rs, 1)
            nc.vector.reciprocal(ss[:, :, :], ss[:, :, :]).then_inc(s_rs, 1)
            dve.wait_ge(s_rs, 2)
            for m in range(NT):
                norm(m)


def ssd_phase(t, xc, xs, bt, z, dt, a_dt, nacum, ecum, e, xdt, xde, state, decayed, y1, y):
    nc = t.nc
    steps = [(m, gr) for m in range(NT) for gr in range(S_GROUPS)]
    w = S_HPG * S_HD
    nh = NT * S_HEADS
    with ExitStack() as c:
        s_seg = t.semaphore("ssd_segments")
        s_e = t.semaphore("ssd_decays")
        s_cb = t.semaphore("ssd_scores")
        s_m = t.semaphore("ssd_masked")
        s_x = t.semaphore("ssd_x")
        s_off = t.semaphore("ssd_state_read")
        s_y = t.semaphore("ssd_y")
        s_h = t.semaphore("ssd_state")
        s_t = t.semaphore("ssd_y_read")
        s_dve = t.semaphore("ssd_dve")
        s_pool = t.semaphore("ssd_pool")
        s_skip = t.semaphore("ssd_skip")
        s_ms = t.semaphore("ssd_ms")
        s_rs = t.semaphore("ssd_rs")
        ss = c.enter_context(nc.sbuf_tensor("ssd_ss", [P, len(steps)], F32))
        block = c.enter_context(nc.Block())

        @block.tensor
        def _(pe):
            def front(u):
                m, gr = steps[u]
                if u:
                    pe.wait_ge(s_e, S_HPG * u)
                for i in range(2):
                    nc.tensor.matmul(t.bank[i][:, :].rearrange("p (h n) -> p h n", h=4), t.ident,
                                     wide(t.common[:, C_NEG:C_NEG + P].unsqueeze(1), P, 4, P), start=True, stop=False)
                    for j in range(4):
                        col = m * S_HEADS + gr * S_HPG + 4 * i + j
                        mm = nc.tensor.matmul(t.bank[i][:, j * P:(j + 1) * P], wide(a_dt[:, col:col + 1], P, P),
                                              t.common[:, C_UPTO:C_UPTO + P], start=False, stop=j == 3)
                mm.then_inc(s_seg, 1)
                if u:
                    pe.wait_ge(s_m, u)
                ms = slice(m * P, (m + 1) * P)
                nc.tensor.matmul(t.bank[2][:, 0:P], xc[:, KD + gr, ms], xc[:, KD + S_GROUPS + gr, ms],
                                 start=True, stop=True).then_inc(s_cb, 1)

            front(0)
            for u, (m, gr) in enumerate(steps):
                ms = slice(m * P, (m + 1) * P)
                if u >= 2:
                    pe.wait_ge(s_t, u - 1)
                if m:
                    pe.wait_ge(s_h, u - 1)
                    nc.tensor.matmul(t.bank[3 + u % 2][:, :], xc[:, KD + S_GROUPS + gr, ms], state[:, gr, :],
                                     start=True, stop=True).then_inc(s_off, 1)
                pe.wait_ge(s_x, u + 1)
                if m + 1 < NT:
                    if u:
                        pe.wait_ge(s_h, u)
                    nc.tensor.matmul(t.bank[7][:, :], bt[:, m, gr * P:(gr + 1) * P], xde[:, u % 2, :], start=True, stop=True)
                if u + 1 < len(steps):
                    front(u + 1)
                pe.wait_ge(s_m, u + 1)
                for h in range(S_HPG):
                    mm = nc.tensor.matmul(t.bank[5 + u % 2][:, h * S_HD:(h + 1) * S_HD], e[:, u % 2, h, :],
                                          xdt[:, u % 2, h * S_HD:(h + 1) * S_HD], start=True, stop=True)
                mm.then_inc(s_y, 1)

        @block.scalar
        def _(act):
            for u, (m, gr) in enumerate(steps):
                act.wait_ge(s_seg, u + 1)
                if u >= 2:
                    act.wait_ge(s_y, u - 1)
                for h in range(S_HPG):
                    col = m * S_HEADS + gr * S_HPG + h
                    nc.scalar.activation(e[:, u % 2, h, :], t.bank[h // 4][:, (h % 4) * P:(h % 4 + 1) * P], ACT.Exp,
                                         bias=nacum[:, col:col + 1]).then_inc(s_e, 1)
            act.wait_ge(s_ms, len(steps))
            nc.scalar.activation(ss[:, :], ss[:, :], ACT.Sqrt, bias=t.eps[:, 1:2]).then_inc(s_rs, 1)

        @block.gpsimd
        def _(pool):
            ch = Chain(pool, s_pool)

            for u, (m, gr) in enumerate(steps):
                c0 = m * S_HEADS + gr * S_HPG
                x = xs[:, m, gr * w:(gr + 1) * w].rearrange("p (h d) -> p h d", h=S_HPG)
                xd = xdt[:, u % 2, :].rearrange("p (h d) -> p h d", h=S_HPG)
                xe = xde[:, u % 2, :].rearrange("p (h d) -> p h d", h=S_HPG)
                if u >= 2:
                    pool.wait_ge(s_y, u - 1)
                dts = dt[:, m, gr * S_HPG:(gr + 1) * S_HPG]
                ch.link(nc.gpsimd.tensor_tensor(xd, x, wide(dts.unsqueeze(2), P, S_HPG, S_HD), ALU.mult))
                if m:
                    pool.wait_ge(s_h, u - 1)
                    ch.add(nc.gpsimd.tensor_tensor(decayed[:, gr, :].rearrange("p (h d) -> p h d", h=S_HPG),
                                                   state[:, gr, :].rearrange("p (h d) -> p h d", h=S_HPG),
                                                   wide(ecum[:, nh + c0:nh + c0 + S_HPG].unsqueeze(2), P, S_HPG, S_HD), ALU.mult))
                ch.wait()
                nc.gpsimd.tensor_tensor(xe, xd, wide(ecum[:, 2 * nh + c0:2 * nh + c0 + S_HPG].unsqueeze(2), P, S_HPG, S_HD),
                                        ALU.mult).then_inc(s_x, 1)
                nc.gpsimd.tensor_tensor(x, x, wide(t.row("dskip")[:, gr * S_HPG:(gr + 1) * S_HPG].unsqueeze(2), P, S_HPG, S_HD),
                                        ALU.mult).then_inc(s_skip, 1)


        @block.vector
        def _(dve):
            ch = Chain(dve, s_dve)

            def tail(u):
                m, gr = steps[u]
                c0 = m * S_HEADS + gr * S_HPG
                gs = slice(gr * w, (gr + 1) * w)
                yy = y1[:, u % 2, :]
                dve.wait_ge(s_y, u + 1)
                if m + 1 < NT:
                    if m:
                        nc.vector.tensor_tensor(state[:, gr, :], decayed[:, gr, :], t.bank[7][:, :], ALU.add).then_inc(s_h, 1)
                    else:
                        nc.vector.tensor_copy(state[:, gr, :], t.bank[7][:, :]).then_inc(s_h, 1)
                if m:
                    ch.link(nc.vector.tensor_tensor(yy.rearrange("p (h d) -> p h d", h=S_HPG),
                                                    t.bank[3 + u % 2][:, :].rearrange("p (h d) -> p h d", h=S_HPG),
                                                    wide(ecum[:, c0:c0 + S_HPG].unsqueeze(2), P, S_HPG, S_HD), ALU.mult))
                    ch.link(nc.vector.tensor_tensor(yy, yy, xs[:, m, gs], ALU.add))
                    nc.vector.tensor_tensor(yy, yy, t.bank[5 + u % 2][:, :], ALU.add).then_inc(s_t, 1)
                else:
                    nc.vector.tensor_tensor(yy, xs[:, m, gs], t.bank[5 + u % 2][:, :], ALU.add).then_inc(s_t, 1)
                dve.wait_ge(s_t, u + 1)
                ch.link(nc.vector.tensor_tensor(y[:, m, gs], yy, z[:, m, gs], ALU.mult))
                nc.vector.tensor_tensor_reduce(yy, y[:, m, gs], y[:, m, gs], 1.0 / w, 0.0, ALU.mult, ALU.add,
                                               ss[:, u:u + 1]).then_inc(s_ms, 1)
                dve.wait_ge(s_ms, u + 1)

            for u in range(len(steps)):
                dve.wait_ge(s_e, S_HPG * (u + 1))
                dve.wait_ge(s_cb, u + 1)
                nc.vector.tensor_tensor(e[:, u % 2], e[:, u % 2], wide(t.bank[2][:, 0:P].unsqueeze(1), P, S_HPG, P),
                                        ALU.mult).then_inc(s_m, 1)
                dve.wait_ge(s_skip, u + 1)
                tail(u)
            dve.wait_ge(s_rs, 1)
            nc.vector.reciprocal(ss[:, :], ss[:, :]).then_inc(s_rs, 1)
            dve.wait_ge(s_rs, 2)
            for u, (m, gr) in enumerate(steps):
                gs = slice(gr * w, (gr + 1) * w)
                nc.vector.tensor_scalar(y[:, m, gs], y[:, m, gs], ss[:, u:u + 1], None, ALU.mult)


def proj_phase(t, tag, srcs, scales, mt, chunks, ring, w_sem):
    nc = t.nc
    n_half = len(srcs)
    with ExitStack() as c:
        s_tr = t.semaphore(f"{tag}_transposed")
        s_ev = t.semaphore(f"{tag}_evacuated")
        s_pe = t.semaphore(f"{tag}_group")
        s_add = t.semaphore(f"{tag}_added")
        s_use = t.semaphore(f"{tag}_chunk_used")
        block = c.enter_context(nc.Block())
        banks = n_half * KD

        @block.sync
        def _(sp):
            for n in range(len(chunks)):
                if n >= 2:
                    half, part = divmod(n - 2, n_half)
                    if part == n_half - 1:
                        sp.wait_ge(s_pe, NT * (half + 1))
                    else:
                        sp.wait_ge(s_use, half + 1)
                sp.dma_start(ring[n % 2], chunks[n]).then_inc(w_sem[n % 2], 16)

        @block.tensor
        def _(pe):
            for n in range(banks):
                if n >= 8:
                    pe.wait_ge(s_ev, n - 7)
                for m in range(NT):
                    mm = nc.tensor.transpose(t.bank[n % 8][:, m * P:(m + 1) * P], srcs[n // KD][:, m, (n % KD) * P:(n % KD + 1) * P], t.ident)
                mm.then_inc(s_tr, 1)
            pe.wait_ge(s_ev, banks)
            for n in range(len(chunks)):
                half, part = divmod(n, n_half)
                pe.wait_ge(w_sem[n % 2], 16 * (n // 2 + 1))
                for m in range(NT):
                    for kk in range(KD):
                        mm = nc.tensor.matmul(t.bank[4 * half + m][:, :], mt[:, part * KD + kk, m * P:(m + 1) * P],
                                              ring[n % 2][:, kk, :], start=part == 0 and kk == 0,
                                              stop=part == n_half - 1 and kk == KD - 1)
                    if part == n_half - 1:
                        mm.then_inc(s_pe, 1)
                    elif m == NT - 1:
                        mm.then_inc(s_use, 1)

        @block.scalar
        def _(act):
            for n in range(0, banks):
                act.wait_ge(s_tr, n + 1)
                sc = scales[n // KD]
                nc.scalar.activation(mt[:, n, :], t.bank[n % 8][:, :], ACT.Copy,
                                     scale=1.0 if sc is None else sc[:, n % KD:n % KD + 1]).then_inc(s_ev, 1)

        @block.vector
        def _(dve):
            for half in range(2):
                for m in range(NT):
                    dve.wait_ge(s_pe, NT * half + m + 1)
                    hs = t.h[:, m, half * HALF:(half + 1) * HALF]
                    nc.vector.tensor_tensor(hs, hs, t.bank[4 * half + m][:, :], ALU.add).then_inc(s_add, 1)


def first_max(nc, chain, onehot, x, mx, least, cand, iota):
    shape = [P, NT, x.shape[2]]
    chain.link(nc.vector.tensor_reduce(mx, x, AX.X, ALU.max))
    chain.link(nc.vector.tensor_tensor(cand, x, wide(mx.unsqueeze(2), *shape), ALU.is_equal))
    chain.link(nc.vector.scalar_tensor_tensor(out=cand, in0=cand, scalar=-8.0, in1=wide(iota.unsqueeze(1), *shape),
                                              op0=ALU.mult, op1=ALU.add))
    chain.link(nc.vector.tensor_reduce(least, cand, AX.X, ALU.min))
    chain.link(nc.vector.tensor_tensor(onehot, cand, wide(least.unsqueeze(2), *shape), ALU.is_equal))


def route_phase(t, layer, ut, xn, router_dram, at):
    nc = t.nc
    NL = GROUPS + EXPERTS
    with ExitStack() as c:
        sem = lambda n: t.semaphore(f"route{layer}_{n}")
        s_w, s_lg, s_exp, s_dve, s_pick, s_rank, s_slot, s_put = (sem(n) for n in (
            "weights", "logits", "exp", "dve", "picked", "ranked", "slots", "scattered"))
        taken = [at]

        def sb(n, shape):
            v = views(t, taken[0], [(n, tuple(shape[1:]))])[n]
            taken[0] += int(np.prod(shape[1:]))
            return v

        wr = sb("w", [P, KD, NL])
        lg = sb("logits", [P, NT, NL])
        oh_g, sel, sel2, cand = (sb(n, [P, NT, EPG]) for n in ("group", "sel", "sel2", "cand"))
        oh = [sb(f"first{j}", [P, NT, EPG]) for j in range(2)]
        mx = [sb(f"max{j}", [P, NT]) for j in range(3)]
        least, ex, den, gsum = (sb(n, [P, NT]) for n in ("least", "ex", "den", "gsum"))
        gexp = sb("gexp", [P, NT, GROUPS])
        pick = [sb(f"pick{j}", [P, NT, EXPERTS]) for j in range(3)]
        prod = sb("prod", [P, NT, EXPERTS])
        cnt, nb, incl, base = (sb(n, [P, EXPERTS]) for n in ("count", "blocks", "incl", "base"))
        pos = sb("pos", [P, NT, 2])
        table = sb("table", [P, MAX_BLOCKS, EXPERTS])
        ebf = sb("expert_of", [P, 1 + MAX_BLOCKS])
        even = sb("even", [P, MAX_BLOCKS // 2])
        block = c.enter_context(nc.Block())

        @block.sync
        def _(sp):
            sp.dma_start(wr[:, :, :], router_dram).then_inc(s_w, 16)

        @block.tensor
        def _(pe):
            pe.wait_ge(s_w, 16)
            for m in range(NT):
                for k in range(KD):
                    mm = nc.tensor.matmul(t.bank[0][:, m * NL:(m + 1) * NL], ut[:, k, m * P:(m + 1) * P], wr[:, k, :],
                                          start=k == 0, stop=k == KD - 1)
            mm.then_inc(s_lg, 1)
            pe.wait_ge(s_pick, 1)
            before, ones = t.common[:, C_BEFORE:C_BEFORE + P], t.common[:, C_ONES:C_ONES + P]
            for m in range(NT + 1):
                o = t.bank[1][:, m * EXPERTS:(m + 1) * EXPERTS]
                n = min(m, NT)
                for j in range(n):
                    mm = nc.tensor.matmul(o, ones, pick[2][:, j, :], start=j == 0, stop=m == NT and j == n - 1)
                if m < NT:
                    mm = nc.tensor.matmul(o, before, pick[2][:, m, :], start=m == 0, stop=True)
            mm.then_inc(s_rank, 1)

        @block.scalar
        def _(act):
            act.wait_ge(s_exp, 1)
            nc.scalar.activation(gexp[:, :, :], gexp[:, :, :], ACT.Exp).then_inc(s_exp, 1)
            act.wait_ge(s_exp, 3)
            nc.scalar.activation(ex[:, :], ex[:, :], ACT.Exp).then_inc(s_exp, 1)

        @block.vector
        def _(dve):
            ch = Chain(dve, s_dve)
            iota = t.common[:, C_IOTA:C_IOTA + EPG]
            shape = [P, NT, EPG]
            dve.wait_ge(s_lg, 1)
            ch.link(nc.vector.tensor_tensor(lg[:, :, :], t.bank[0][:, 0:NT * NL].rearrange("p (m n) -> p m n", m=NT),
                                            wide(t.row(f"mb{layer}").unsqueeze(1), P, NT, NL), ALU.add))
            g = lg[:, :, 0:GROUPS]
            first_max(nc, ch, oh_g[:, :, :], g, mx[0][:, :], least[:, :], cand[:, :, :], iota)
            nc.vector.tensor_tensor(gexp[:, :, :], g, wide(mx[0][:, :].unsqueeze(2), *shape), ALU.subtract).then_inc(s_exp, 1)
            for gr in range(GROUPS):
                e = lg[:, :, GROUPS + gr * EPG:GROUPS + (gr + 1) * EPG]
                on = wide(oh_g[:, :, gr:gr + 1], *shape)
                if gr == 0:
                    ch.link(nc.vector.tensor_tensor(sel[:, :, :], e, on, ALU.mult))
                else:
                    ch.link(nc.vector.tensor_tensor(cand[:, :, :], e, on, ALU.mult))
                    ch.link(nc.vector.tensor_tensor(sel[:, :, :], sel[:, :, :], cand[:, :, :], ALU.add))
            first_max(nc, ch, oh[0][:, :, :], sel[:, :, :], mx[1][:, :], least[:, :], cand[:, :, :], iota)
            ch.link(nc.vector.scalar_tensor_tensor(out=sel2[:, :, :], in0=oh[0][:, :, :], scalar=-3e38, in1=sel[:, :, :],
                                                   op0=ALU.mult, op1=ALU.add))
            first_max(nc, ch, oh[1][:, :, :], sel2[:, :, :], mx[2][:, :], least[:, :], cand[:, :, :], iota)
            dve.wait_ge(s_exp, 2)
            nc.vector.tensor_tensor(ex[:, :], mx[2][:, :], mx[1][:, :], ALU.subtract).then_inc(s_exp, 1)
            for j in range(2):
                for gr in range(GROUPS):
                    ch.add(nc.vector.tensor_tensor(pick[j][:, :, gr * EPG:(gr + 1) * EPG], oh[j][:, :, :],
                                                   wide(oh_g[:, :, gr:gr + 1], *shape), ALU.mult))
            ch.wait()
            nc.vector.tensor_tensor(pick[2][:, :, :], pick[0][:, :, :], pick[1][:, :, :], ALU.add).then_inc(s_pick, 1)
            ch.link(nc.vector.tensor_reduce(gsum[:, :], gexp[:, :, :], AX.X, ALU.add))
            dve.wait_ge(s_exp, 4)
            ch.link(nc.vector.tensor_scalar(den[:, :], ex[:, :], 1.0, None, ALU.add))
            ch.link(nc.vector.tensor_tensor(den[:, :], den[:, :], gsum[:, :], ALU.mult))
            ch.link(nc.vector.reciprocal(t.weight[:, :, 0], den[:, :]))
            ch.link(nc.vector.tensor_tensor(t.weight[:, :, 1], t.weight[:, :, 0], ex[:, :], ALU.mult))
            dve.wait_ge(s_rank, 1)
            ch.link(nc.vector.tensor_copy(cnt[:, :], t.bank[1][:, NT * EXPERTS:(NT + 1) * EXPERTS]))
            ch.link(nc.vector.tensor_scalar(nb[:, :], cnt[:, :], 0.0, None, ALU.is_gt))
            for j in range(1, SEQ // SLOTS):
                ch.link(nc.vector.scalar_tensor_tensor(out=nb[:, :], in0=cnt[:, :], scalar=float(j * SLOTS), in1=nb[:, :],
                                                       op0=ALU.is_gt, op1=ALU.add))
            ch.link(nc.vector.tensor_tensor_scan(incl[:, :], t.common[:, C_ONES:C_ONES + EXPERTS], nb[:, :], 0.0, ALU.mult, ALU.add))
            ch.link(nc.vector.tensor_tensor(base[:, :], incl[:, :], nb[:, :], ALU.subtract))
            ch.link(nc.vector.tensor_scalar(base[:, :], base[:, :], float(SLOTS), None, ALU.mult))
            ch.link(nc.vector.tensor_tensor(prod[:, :, :], t.bank[1][:, 0:NT * EXPERTS].rearrange("p (m e) -> p m e", m=NT),
                                            wide(base[:, :].unsqueeze(1), P, NT, EXPERTS), ALU.add))
            for j in range(2):
                ch.link(nc.vector.tensor_tensor(pick[j][:, :, :], pick[j][:, :, :], prod[:, :, :], ALU.mult))
                ch.link(nc.vector.tensor_reduce(pos[:, :, j], pick[j][:, :, :], AX.X, ALU.add))
            nc.vector.tensor_copy(t.slot[:, :, :], pos[:, :, :]).then_inc(s_slot, 1)
            ch.link(nc.vector.tensor_tensor(table[:, :, :], wide(t.common[:, C_BLK:C_BLK + MAX_BLOCKS].unsqueeze(2), P, MAX_BLOCKS, EXPERTS),
                                            wide(incl[:, :].unsqueeze(1), P, MAX_BLOCKS, EXPERTS), ALU.is_ge))
            ch.link(nc.vector.tensor_reduce(ebf[:, 1:], table[:, :, :], AX.X, ALU.add))
            ch.link(nc.vector.tensor_scalar(ebf[:, 1:], ebf[:, 1:], float(EXPERTS - 1), None, ALU.min))
            ch.link(nc.vector.tensor_scalar(even[:, :], t.common[:, C_BLK:C_BLK + MAX_BLOCKS].rearrange("p (b two) -> p b two", two=2)[:, :, 0],
                                            incl[:, EXPERTS - 1:EXPERTS], None, ALU.is_lt))
            ch.link(nc.vector.tensor_reduce(ebf[:, 0:1], even[:, :], AX.X, ALU.add))
            nc.vector.tensor_copy(t.meta[:, :], ebf[0:1, :])

        @block.gpsimd
        def _(pool):
            pool.wait_ge(t.s_clear, 16 * MAX_BLOCKS)
            pool.wait_ge(s_slot, 1)
            for m in range(NT):
                for j in range(2):
                    nc.gpsimd.indirect_dma_start(out=t.xg[:, :], out_offset=bass.IndirectOffsetOnAxis(ap=t.slot[:, m, j:j + 1], axis=0),
                                                 in_=xn[:, m, :], in_offset=None).then_inc(s_put, 16)
            pool.wait_ge(s_put, 16 * 2 * NT)


def experts_phase(t, layer, w_col, b, w1, w3, w2):
    nc = t.nc
    with ExitStack() as c:
        sem = lambda n: t.semaphore(f"moe{layer}_{n}")
        s_x = [sem(f"x_loaded{i}") for i in range(2)]
        s_w13 = [sem(f"w13_loaded{i}") for i in range(2)]
        s_w2 = [sem(f"w2_loaded{i}") for i in range(2)]
        s_xt, s_xte = sem("x_transposed"), sem("x_evacuated")
        s_h, s_silu, s_u = sem("hidden"), sem("silu"), sem("gated")
        s_ht, s_hte = sem("gated_transposed"), sem("gated_evacuated")
        s_y, s_ye = sem("y"), sem("y_evacuated")
        s_st = [sem(f"y_stored{i}") for i in range(2)]
        s_yfree = sem("y_free")
        block = c.enter_context(nc.Block())
        bank = t.bank

        def pairs(engine):
            return engine.value_load(t.meta[0:1, 0:1], min_val=1, max_val=MAX_BLOCKS // 2)

        @block.sync
        def _(sp):
            n = pairs(sp)
            with sp.Fori(0, n) as i:
                for s in range(2):
                    sp.wait_ge(s_xt, 4 * i + 2 * s + 2)
                    sp.dma_start(b["x"][:, s, :], t.xg[bass.ds(i * 2 * SLOTS + s * SLOTS, SLOTS), :]).then_inc(s_x[s], 16)
                    e = sp.value_load(t.meta[0:1, bass.ds(i * 2 + s + 1, 1)], min_val=0, max_val=EXPERTS - 1)
                    sp.wait_ge(s_h, 4 * i + 2 * s + 2)
                    for w, name in ((w1, "w1"), (w3, "w3")):
                        sp.dma_start(b[name][:, s], w[bass.ds(e, 1)].rearrange("o (k p) n -> p (o k) n", p=P)).then_inc(s_w13[s], 16)
                    sp.wait_ge(s_y, 4 * i + 2 * s + 2)
                    sp.dma_start(b["w2"][:, s], w2[bass.ds(e, 1)].rearrange("o (k p) n -> p (o k) n", p=P)).then_inc(s_w2[s], 16)

        @block.tensor
        def _(pe):
            n = pairs(pe)
            pe.sem_inc(s_xt, 4)
            pe.sem_inc(s_h, 4)
            pe.sem_inc(s_y, 4)
            with pe.Fori(0, n) as i:
                for s in range(2):
                    pe.wait_ge(s_x[s], 16 * i + 16)
                    if s:
                        pe.wait_ge(s_ye, 4 * i + 2)
                    for k in range(KD):
                        mm = nc.tensor.transpose(bank[2 * s + k // 4][:, (k % 4) * P:(k % 4 + 1) * P], b["x"][:, s, k * P:(k + 1) * P], t.ident)
                        if k % 4 == 3:
                            mm.then_inc(s_xt, 1)
                for s in range(2):
                    pe.wait_ge(s_w13[s], 32 * i + 32)
                    pe.wait_ge(s_xte, 4 * i + 2 * s + 2)
                    if s == 0:
                        pe.wait_ge(s_ye, 4 * i + 4)
                    for j, name in enumerate(("w1", "w3")):
                        for k in range(KD):
                            mm = nc.tensor.matmul(bank[4 + 2 * s + j][:, :], b["xt"][:, s, k, :], b[name][:, s, k, :],
                                                  start=k == 0, stop=k == KD - 1)
                        mm.then_inc(s_h, 1)
                for s in range(2):
                    pe.wait_ge(s_u, 2 * i + s + 1)
                    for k in range(FF // P):
                        mm = nc.tensor.transpose(bank[s][:, k * P:(k + 1) * P], b["u"][:, s, k * P:(k + 1) * P], t.ident)
                    mm.then_inc(s_ht, 1)
                    pe.wait_ge(s_w2[s], 16 * i + 16)
                    pe.wait_ge(s_hte, 2 * i + s + 1)
                    for j in range(2):
                        for k in range(FF // P):
                            mm = nc.tensor.matmul(bank[2 + 2 * s + j][:, :], b["ht"][:, s, k, :], b["w2"][:, s, k, j * HALF:(j + 1) * HALF],
                                                  start=k == 0, stop=k == FF // P - 1)
                        mm.then_inc(s_y, 1)

        @block.vector
        def _(dve):
            n = pairs(dve)
            with dve.Fori(0, n) as i:
                for s in range(2):
                    for j in range(2):
                        dve.wait_ge(s_xt, 4 + 4 * i + 2 * s + j + 1)
                        nc.vector.tensor_tensor(b["xt"][:, s, 4 * j:4 * j + 4, :], bank[2 * s + j][:, :].rearrange("p (k n) -> p k n", k=4),
                                                wide(w_col[:, 4 * j:4 * j + 4].unsqueeze(2), P, 4, P), ALU.mult).then_inc(s_xte, 1)
                for s in range(2):
                    dve.wait_ge(s_h, 4 + 4 * i + 2 * s + 2)
                    dve.wait_ge(s_silu, 2 * i + s + 1)
                    nc.vector.tensor_tensor(b["u"][:, s, :], b["u"][:, s, :], bank[5 + 2 * s][:, :], ALU.mult).then_inc(s_u, 1)

        @block.scalar
        def _(act):
            n = pairs(act)
            act.sem_inc(s_ye, 4)
            with act.Fori(0, n) as i:
                for s in range(2):
                    act.wait_ge(s_h, 4 + 4 * i + 2 * s + 1)
                    nc.scalar.activation(b["u"][:, s, :], bank[4 + 2 * s][:, :], ACT.Silu).then_inc(s_silu, 1)
                for s in range(2):
                    act.wait_ge(s_ht, 2 * i + s + 1)
                    nc.scalar.activation(b["ht"][:, s].rearrange("p k n -> p (k n)"), bank[s][:, :], ACT.Copy).then_inc(s_hte, 1)
                    act.wait_ge(s_yfree, 2 * i + s + 1)
                    for j in range(2):
                        act.wait_ge(s_y, 4 + 4 * i + 2 * s + j + 1)
                        nc.scalar.activation(b["y"][:, s, j * HALF:(j + 1) * HALF], bank[2 + 2 * s + j][:, :], ACT.Copy).then_inc(s_ye, 1)

        @block.gpsimd
        def _(pool):
            n = pairs(pool)
            pool.sem_inc(s_yfree, 2)
            with pool.Fori(0, n) as i:
                for s in range(2):
                    pool.wait_ge(s_ye, 4 + 4 * i + 2 * s + 2)
                    pool.dma_start(t.xg[bass.ds(i * 2 * SLOTS + s * SLOTS, SLOTS), :], b["y"][:, s, :]).then_inc(s_st[s], 16)
                    pool.wait_ge(s_st[s], 16 * i + 16)
                    pool.sem_inc(s_yfree, 1)


def combine_phase(t, layer, y):
    nc = t.nc
    with ExitStack() as c:
        s_y = [t.semaphore(f"combine{layer}_row{i}") for i in range(4)]
        s_add = t.semaphore(f"combine{layer}_added")
        block = c.enter_context(nc.Block())
        steps = [(m, j) for m in range(NT) for j in range(2)]

        @block.gpsimd
        def _(pool):
            for n, (m, j) in enumerate(steps):
                if n >= 4:
                    pool.wait_ge(s_y[n % 4], 16)
                nc.gpsimd.indirect_dma_start(out=y[:, n, :], out_offset=None, in_=t.xg[:, :],
                                             in_offset=bass.IndirectOffsetOnAxis(ap=t.slot[:, m, j:j + 1], axis=0)).then_inc(s_y[n % 4], 16)

        @block.vector
        def _(dve):
            for n, (m, j) in enumerate(steps):
                dve.wait_ge(s_y[n % 4], 16 * (n // 4 + 1))
                if j:
                    dve.wait_ge(s_add, n)
                nc.vector.scalar_tensor_tensor(out=t.h[:, m, :], in0=y[:, n, :], scalar=t.weight[:, m, j:j + 1], in1=t.h[:, m, :],
                                               op0=ALU.mult, op1=ALU.add).then_inc(s_add, 1)


def moe(t, a, layer):
    at = 3 * (2 * KD * HALF)
    A = views(t, at, [("ut", (KD, SEQ)), ("xn", (NT, D))])
    w_col = t.col(f"ffn{layer}")
    norm_phase(t, f"ffn{layer}", w_col, A["xn"], A["ut"])
    route_phase(t, layer, A["ut"], A["xn"], a["router"][layer], at + KD * SEQ + NT * D)
    b = views(t, 0, [("w1", (2, KD, FF)), ("w3", (2, KD, FF)), ("w2", (2, FF // P, D)), ("x", (2, D)), ("xt", (2, KD, P)),
                     ("u", (2, FF)), ("ht", (2, FF // P, P)), ("y", (2, D))])
    experts_phase(t, layer, w_col, b, a["moe_w1"][layer], a["moe_w3"][layer], a["moe_w2"][layer])
    combine_phase(t, layer, views(t, 0, [("y", (2 * NT, D))])["y"])


def rwkv_proj_phase(t, a, ut, xj, sg, lora, sigma, ag, r, k, v, g, keep):
    nc = t.nc
    W1, A1, W2, A2, R0, K0_, V0_, G1, G2, END = 0, 1, 2, 10, 18, 26, 34, 42, 44, 52
    order = (1, 4, 0, 2, 3, 5)
    last_use = (W1, A1, R0 + 7, K0_ + 7)
    GB = G_LORA - P
    flat = [t.ring[i].rearrange("p k n -> p (k n)") for i in range(2)]
    with ExitStack() as c:
        sem = lambda n: t.semaphore(f"rw_{n}")
        s_w = [sem(f"weights{i}") for i in range(2)]
        s_xj, s_pe, s_ev, s_one, s_dve = sem("mix"), sem("group"), sem("evacuated"), sem("one_minus_mu"), sem("proj_dve")
        block = c.enter_context(nc.Block())
        mu = t.col("mu")

        @block.sync
        def _(sp):
            def lora_weights(slot, first, second):
                sp.dma_start(flat[slot][:, 0:KD * W_LORA].rearrange("p (k n) -> p k n", k=KD),
                             a[first][0].rearrange("(k p) n -> p k n", p=P)).then_inc(s_w[slot], 16)
                sp.dma_start(flat[slot][0:W_LORA, KD * W_LORA:KD * W_LORA + D], a[second][0]).then_inc(s_w[slot], 16)

            lora_weights(0, "rw_w1", "rw_w2")
            lora_weights(1, "rw_a1", "rw_a2")
            for n, (name, half, done) in enumerate((("rw_wr", 0, W2 + 8), ("rw_wr", 1, A2 + 8), ("rw_wk", 0, R0 + 4), ("rw_wk", 1, R0 + 8),
                                                    ("rw_wv", 0, K0_ + 4), ("rw_wv", 1, K0_ + 8))):
                sp.wait_ge(s_pe, done)
                sp.dma_start(t.ring[n % 2][:, :, :], a[name][0].rearrange("(k p) n -> p k n", p=P)[:, :, half * HALF:(half + 1) * HALF]
                             ).then_inc(s_w[n % 2], 16)
            sp.wait_ge(s_pe, V0_ + 4)
            n1 = KD * G_LORA
            sp.dma_start(flat[0][:, 0:n1].rearrange("p (k n) -> p k n", k=KD), a["rw_g1"][0].rearrange("(k p) n -> p k n", p=P)).then_inc(s_w[0], 16)
            sp.dma_start(flat[0][:, n1:n1 + D], a["rw_g2"][0, 0:P, :]).then_inc(s_w[0], 16)
            sp.dma_start(flat[0][0:GB, n1 + D:n1 + 2 * D], a["rw_g2"][0, P:G_LORA, :]).then_inc(s_w[0], 16)

        @block.vector
        def _(dve):
            ch = Chain(dve, s_dve)
            one = keep["one_minus_mu"]
            nc.vector.tensor_scalar(one, mu, -1.0, 1.0, ALU.mult, ALU.add).then_inc(s_one, 1)
            dve.wait_ge(s_one, 1)
            for j, which in enumerate(order):
                if j >= 2:
                    dve.wait_ge(s_pe, last_use[j - 2] + 1)
                for b in range(KD):
                    col = which * KD + b
                    dst = xj[j % 2][:, b, :]
                    ch.add(nc.vector.tensor_scalar(dst, ut[:, b, :], one[:, col:col + 1], None, ALU.mult))
                ch.wait()
                for b in range(KD):
                    col = which * KD + b
                    dst = xj[j % 2][:, b, 1:]
                    nc.vector.scalar_tensor_tensor(out=dst, in0=ut[:, b, 0:SEQ - 1], scalar=mu[:, col:col + 1], in1=dst,
                                                   op0=ALU.mult, op1=ALU.add).then_inc(s_xj, 1)

        @block.tensor
        def _(pe):
            def group(i, rows, pairs):
                if i >= 8:
                    pe.wait_ge(s_ev, i - 7)
                for n, (left, right) in enumerate(pairs):
                    mm = nc.tensor.matmul(t.bank[i % 8][0:rows, :], left, right, start=n == 0, stop=n == len(pairs) - 1)
                mm.then_inc(s_pe, 1)

            for j, i in enumerate((W1, A1)):
                pe.wait_ge(s_w[j], 32)
                pe.wait_ge(s_xj, KD * (j + 1))
                group(i, W_LORA, [(flat[j][:, k_ * W_LORA:(k_ + 1) * W_LORA], xj[j][:, k_, :]) for k_ in range(KD)])
            for j, i0 in enumerate((W2, A2)):
                pe.wait_ge(s_ev, j + 1)
                for b in range(KD):
                    o = KD * W_LORA + b * P
                    group(i0 + b, P, [(flat[j][0:W_LORA, o:o + P], lora[j][0:W_LORA, :])])
            for j, i0 in ((2, R0), (3, K0_)):
                pe.wait_ge(s_xj, KD * (j + 1))
                for b in range(KD):
                    if b % 4 == 0:
                        pe.wait_ge(s_w[b // 4], 32 + 16 * (j - 1))
                    group(i0 + b, P, [(t.ring[b // 4][:, k_, (b % 4) * P:(b % 4 + 1) * P], xj[j % 2][:, k_, :]) for k_ in range(KD)])
            pe.wait_ge(s_xj, KD * 5)
            for half in range(2):
                pe.wait_ge(s_w[half], 32 + 16 * 3)
                for m in range(NT):
                    group(V0_ + NT * half + m, P, [(xj[0][:, k_, m * P:(m + 1) * P], t.ring[half][:, k_, :]) for k_ in range(KD)])
            pe.wait_ge(s_xj, KD * 6)
            pe.wait_ge(s_w[0], 32 + 16 * 6)
            for j, (c0, rows) in enumerate(((0, P), (P, GB))):
                group(G1 + j, rows, [(flat[0][:, k_ * G_LORA + c0:k_ * G_LORA + c0 + rows], xj[1][:, k_, :]) for k_ in range(KD)])
            pe.wait_ge(s_ev, G2)
            for m in range(NT):
                ms = slice(m * P, (m + 1) * P)
                for half in range(2):
                    o = KD * G_LORA + half * HALF
                    group(G2 + 2 * m + half, P, [(sg[:, 0, ms], flat[0][:, o:o + HALF]), (sg[0:GB, 1, ms], flat[0][0:GB, o + D:o + D + HALF])])

        @block.scalar
        def _(act):
            def evacuate(i, dst, func, rows=P, bias=0.0):
                act.wait_ge(s_pe, i + 1)
                kw = {} if func is ACT.Copy else {"bias": bias}
                nc.scalar.activation(dst, t.bank[i % 8][0:rows, :], func, **kw).then_inc(s_ev, 1)

            for j, i in enumerate((W1, A1)):
                evacuate(i, lora[j][0:W_LORA, :], ACT.Copy if j else ACT.Tanh, W_LORA)
            for b in range(KD):
                evacuate(W2 + b, sigma[:, b, :], ACT.Sigmoid, bias=t.col("w0")[:, b:b + 1])
            for b in range(KD):
                evacuate(A2 + b, ag[:, b, :], ACT.Sigmoid, bias=t.col("a0")[:, b:b + 1])
            for b in range(KD):
                evacuate(R0 + b, r[:, b, :], ACT.Copy)
            for b in range(KD):
                evacuate(K0_ + b, k[:, b, :], ACT.Copy)
            for half in range(2):
                for m in range(NT):
                    evacuate(V0_ + NT * half + m, v[:, m, half * HALF:(half + 1) * HALF], ACT.Copy)
            evacuate(G1, sg[:, 0, :], ACT.Sigmoid)
            evacuate(G1 + 1, sg[0:GB, 1, :], ACT.Sigmoid, GB)
            act.wait_ge(s_xj, KD * 6)
            for m in range(NT):
                for half in range(2):
                    evacuate(G2 + 2 * m + half, g[:, m, half * HALF:(half + 1) * HALF], ACT.Copy)


def rwkv_keys_phase(t, a, k, kkn, sq, root, l1c):
    nc = t.nc
    with ExitStack() as c:
        sem = lambda n: t.semaphore(f"key_{n}")
        s_sq, s_sum, s_max, s_root, s_inv, s_tab = (sem(n) for n in ("squares", "sums", "floored", "roots", "inverse", "tables"))
        block = c.enter_context(nc.Block())

        @block.sync
        def _(sp):
            sp.dma_start(l1c, a["layer1"]).then_inc(s_tab, 16)
            sp.wait_ge(s_tab, 16)

        @block.scalar
        def _(act):
            for b in range(KD):
                if b >= 2:
                    act.wait_ge(s_sum, b - 1)
                nc.scalar.activation(sq[:, b % 2, :], k[:, b, :], ACT.Square, scale=t.col("kk")[:, b:b + 1]).then_inc(s_sq, 1)
                if b:
                    act.wait_ge(s_max, b)
                    nc.scalar.activation(root[:, (b - 1) % 2, :], root[:, (b - 1) % 2, :], ACT.Sqrt).then_inc(s_root, 1)
            act.wait_ge(s_max, KD)
            nc.scalar.activation(root[:, (KD - 1) % 2, :], root[:, (KD - 1) % 2, :], ACT.Sqrt).then_inc(s_root, 1)

        @block.tensor
        def _(pe):
            for b in range(KD):
                pe.wait_ge(s_sq, b + 1)
                nc.tensor.matmul(t.bank[b][:, :], t.common[:, C_SAME:C_SAME + P], sq[:, b % 2, :], start=True, stop=True).then_inc(s_sum, 1)

        @block.vector
        def _(dve):
            def finish(b):
                dve.wait_ge(s_root, b + 1)
                nc.vector.reciprocal(root[:, b % 2, :], root[:, b % 2, :]).then_inc(s_inv, 1)
                dve.wait_ge(s_inv, 2 * b + 1)
                nc.vector.scalar_tensor_tensor(out=kkn[:, b, :], in0=k[:, b, :], scalar=t.col("kk")[:, b:b + 1], in1=root[:, b % 2, :],
                                               op0=ALU.mult, op1=ALU.mult).then_inc(s_inv, 1)

            for b in range(KD):
                dve.wait_ge(s_sum, b + 1)
                if b >= 2:
                    dve.wait_ge(s_inv, 2 * (b - 1))
                nc.vector.tensor_scalar(root[:, b % 2, :], t.bank[b][:, :], 1e-24, None, ALU.max).then_inc(s_max, 1)
                if b:
                    finish(b - 1)
            finish(KD - 1)


def rwkv_decay_phase(t, sigma, ag, r, k, kkn, tmp, keep):
    nc = t.nc
    MID = P // 2 - 1
    with ExitStack() as c:
        sem = lambda n: t.semaphore(f"decay_{n}")
        s_d, s_p, s_bb, s_k2, s_bon, s_out, s_pool, s_dve, s_ends, s_rk = (sem(n) for n in (
            "sums", "exps", "rate", "key", "bonus", "done", "pool", "dve", "ends", "rk"))
        block = c.enter_context(nc.Block())
        ones = t.common[:, C_ONES:C_ONES + P]

        @block.vector
        def _(dve):
            ch = Chain(dve, s_dve)

            def sums(b):
                cs = tmp["c"][:, b % 2]
                for m in range(NT):
                    ch.add(nc.vector.tensor_tensor_scan(cs[:, m, :], ones, sigma[:, b, m * P:(m + 1) * P], 0.0, ALU.mult, ALU.add))
                ch.wait()
                if b >= 2:
                    dve.wait_ge(s_p, 3 * (b - 1))
                ch.add(nc.vector.tensor_tensor(tmp["d1"][:, b % 2], cs, wide(cs[:, :, MID:MID + 1], P, NT, P), ALU.subtract))
                ch.add(nc.vector.tensor_copy(keep["mid"][:, b, :].unsqueeze(2), cs[:, :, MID:MID + 1]))
                ch.wait()
                ch.add(nc.vector.tensor_copy(keep["end"][:, b, :].unsqueeze(2), tmp["d1"][:, b % 2][:, :, P - 1:P]))
                nc.vector.tensor_tensor(tmp["d2"][:, b % 2], tmp["d1"][:, b % 2], sigma[:, b, :].rearrange("p (m n) -> p m n", m=NT),
                                        ALU.subtract).then_inc(s_d, 1)
                ch.wait()
                dve.wait_ge(s_d, b + 1)

            def products(b):
                pt, pinv, pb = (tmp[n][:, b % 2].rearrange("p m n -> p (m n)") for n in ("pt", "pinv", "pb"))
                k2, x = tmp["k2"][:, b % 2], tmp["x"][:, b % 2]
                if b >= 2:
                    dve.wait_ge(s_out, 2 * (b - 1))
                    dve.wait_ge(s_bon, b - 1)
                ch.link(nc.vector.tensor_scalar(k2, ag[:, b, :], 1.0, t.col("ka")[:, b:b + 1], ALU.subtract, ALU.mult))
                ch.link(nc.vector.scalar_tensor_tensor(out=k2, in0=k2, scalar=1.0, in1=k[:, b, :], op0=ALU.add, op1=ALU.mult))
                nc.vector.scalar_tensor_tensor(out=x, in0=r[:, b, :], scalar=t.col("rk")[:, b:b + 1], in1=k2, op0=ALU.mult,
                                               op1=ALU.mult).then_inc(s_rk, 1)
                dve.wait_ge(s_p, 3 * (b + 1))
                nc.vector.tensor_tensor(k[:, b, :], k2, pinv, ALU.mult)
                nc.vector.scalar_tensor_tensor(out=sigma[:, b, :], in0=kkn[:, b, :], scalar=-1.0, in1=pb, op0=ALU.mult,
                                               op1=ALU.mult).then_inc(s_k2, 1)

            for b in range(KD):
                sums(b)
                if b:
                    products(b - 1)
            products(KD - 1)
            dve.wait_ge(s_ends, 2)
            nc.vector.tensor_tensor(keep["factor"][:, :, 0:NT - 1], keep["end"][:, :, 0:NT - 1], keep["mid"][:, :, 1:NT], ALU.mult)
            dve.wait_ge(s_bon, KD)
            nc.vector.tensor_copy(keep["bonus"], t.bank[0][:, 0:NT * W_HEADS])

        @block.scalar
        def _(act):
            for b in range(KD):
                act.wait_ge(s_d, b + 1)
                if b >= 2:
                    act.wait_ge(s_out, 2 * (b - 1))
                    act.wait_ge(s_k2, b - 1)
                for name, src, sign in (("pt", "d1", 1.0), ("pinv", "d1", -1.0), ("pb", "d2", 1.0)):
                    nc.scalar.activation(tmp[name][:, b % 2], tmp[src][:, b % 2], ACT.Exp, scale=sign * LOG_DECAY).then_inc(s_p, 1)
            for name in ("mid", "end"):
                nc.scalar.activation(keep[name], keep[name], ACT.Exp, scale=LOG_DECAY).then_inc(s_ends, 1)

        @block.gpsimd
        def _(pool):
            ch = Chain(pool, s_pool)
            for b in range(KD):
                pt, pinv = (tmp[n][:, b % 2].rearrange("p m n -> p (m n)") for n in ("pt", "pinv"))
                pool.wait_ge(s_p, 3 * (b + 1))
                pool.wait_ge(s_rk, b + 1)
                nc.gpsimd.tensor_tensor(r[:, b, :], r[:, b, :], pt, ALU.mult).then_inc(s_out, 1)
                ch.link(nc.gpsimd.tensor_tensor(ag[:, b, :], ag[:, b, :], kkn[:, b, :], ALU.mult))
                nc.gpsimd.tensor_tensor(ag[:, b, :], ag[:, b, :], pinv, ALU.mult).then_inc(s_out, 1)

        @block.tensor
        def _(pe):
            for b in range(KD):
                pe.wait_ge(s_rk, b + 1)
                for m in range(NT):
                    mm = nc.tensor.matmul(t.bank[0][:, m * W_HEADS + 2 * b:m * W_HEADS + 2 * b + 2], tmp["x"][:, b % 2, m * P:(m + 1) * P],
                                          t.common[:, C_HALF:C_HALF + 2], start=True, stop=True)
                mm.then_inc(s_bon, 1)


def rwkv_rows_phase(t, ag, k, btok, ktok):
    nc = t.nc
    with ExitStack() as c:
        s_tr = t.semaphore("bk_transposed")
        s_ev = [t.semaphore(f"bk_evacuated{i}") for i in range(2)]
        block = c.enter_context(nc.Block())
        todo = [(src, dst, m, j) for src, dst in ((ag, btok), (k, ktok)) for m in range(NT) for j in range(2)]

        @block.tensor
        def _(pe):
            for n, (src, _, m, j) in enumerate(todo):
                if n >= 8:
                    pe.wait_ge(s_ev[n % 2], (n - 8) // 2 + 1)
                for i in range(4):
                    mm = nc.tensor.transpose(t.bank[n % 8][:, i * P:(i + 1) * P], src[:, 4 * j + i, m * P:(m + 1) * P], t.ident)
                mm.then_inc(s_tr, 1)

        @block.scalar
        def _(act):
            for n, (_, dst, m, j) in enumerate(todo):
                if n % 2 == 0:
                    act.wait_ge(s_tr, n + 1)
                    nc.scalar.activation(dst[:, m, j * HALF:(j + 1) * HALF], t.bank[n % 8][:, :], ACT.Copy).then_inc(s_ev[0], 1)

        @block.vector
        def _(dve):
            for n, (_, dst, m, j) in enumerate(todo):
                if n % 2:
                    dve.wait_ge(s_tr, n + 1)
                    nc.vector.tensor_copy(dst[:, m, j * HALF:(j + 1) * HALF], t.bank[n % 8][:, :]).then_inc(s_ev[1], 1)


def rwkv_scan_phase(t, sigma, ag, r, k, v, btok, ktok, buf, state, keep, l1c):
    nc = t.nc
    steps = [(m, p) for m in range(NT) for p in range(2)]
    USES = (9, 9, 7, 7, 8, 8, 2, 2)
    TOP = LEVELS - 1
    L, RHS, SA = 0, TOP + 1, TOP + 2
    LT, Y = 0, TOP
    AK, UP = 0, TOP + 1

    def nth(bank, it, use):
        return it * USES[bank] + use + 1

    four = lambda ap: ap.rearrange("p (h n) -> p h n", h=4)
    with ExitStack() as c:
        sem = lambda n: t.semaphore(f"scan_{n}")
        full = [sem(f"full{i}") for i in range(8)]
        read = [sem(f"read{i}") for i in range(8)]
        s_t0, s_et, s_st, s_dve = sem("T_begun"), sem("E_masked"), sem("state"), sem("dve")
        block = c.enter_context(nc.Block())
        mask = lambda col: wide(t.common[:, col:col + P].unsqueeze(1), P, 4, P)
        low0 = wide(l1c[:, 0:P].unsqueeze(1), P, 4, P)
        up = lambda l: wide(l1c[:, (LEVELS + l) * P:(LEVELS + l + 1) * P].unsqueeze(1), P, 4, P)

        @block.tensor
        def _(pe):
            for it, (m, p) in enumerate(steps):
                ms = slice(m * P, (m + 1) * P)
                blocks = range(4 * p, 4 * p + 4)

                def take(bank, use):
                    n = nth(bank, it, use) - 1
                    if n:
                        pe.wait_ge(read[bank], n)

                def scores(bank, use, rr, left, right):
                    take(bank, use)
                    rows = slice(64 * rr, 64 * rr + 64)
                    for j, b in enumerate(blocks):
                        mm = nc.tensor.matmul(t.bank[bank][:, j * P:(j + 1) * P], left[rows, b, ms], right[rows, b, ms], start=True, stop=True)
                    mm.then_inc(full[bank], 1)

                for rr in range(2):
                    scores(rr, L, rr, sigma, ag)
                    scores(2 + rr, LT, rr, ag, sigma)
                    scores(4 + rr, AK, rr, k, sigma)
                    scores(6, rr, rr, ag, r)
                    scores(7, rr, rr, k, r)
                for l in range(1, TOP + 1):
                    for rr in range(2):
                        u = buf[rr]
                        if l == 1:
                            pe.wait_ge(s_t0, 4 * it + 2 * rr + 2)
                        else:
                            pe.wait_ge(read[2 + rr], nth(2 + rr, it, l - 1))
                        pe.wait_ge(s_et, 2 * TOP * it + 2 * (l - 1) + rr + 1)
                        take(rr, l)
                        for j in range(4):
                            mm = nc.tensor.matmul(t.bank[rr][:, j * P:(j + 1) * P], u["et"][:, l % 2, j], u["t"][:, j], start=True, stop=True)
                        mm.then_inc(full[rr], 1)
                    for rr in range(2):
                        u = buf[rr]
                        pe.wait_ge(read[rr], nth(rr, it, l))
                        take(4 + rr, l)
                        if l < TOP:
                            take(2 + rr, l)
                            for j in range(4):
                                mm = nc.tensor.matmul(t.bank[2 + rr][:, j * P:(j + 1) * P], u["tt"][:, j], u["x"][:, j], start=True, stop=True)
                            mm.then_inc(full[2 + rr], 1)
                        for j in range(4):
                            mm = nc.tensor.matmul(t.bank[4 + rr][:, j * P:(j + 1) * P], u["x"][:, j], u["tt"][:, j], start=True, stop=True)
                        mm.then_inc(full[4 + rr], 1)
                head = lambda b, rr: slice((2 * b + rr) * W_HD, (2 * b + rr + 1) * W_HD)
                if m:
                    pe.wait_ge(s_st, 2 * (it - 2) + 2)
                for rr in range(2):
                    u, rows = buf[rr], slice(64 * rr, 64 * rr + 64)
                    take(rr, RHS)
                    for j, b in enumerate(blocks):
                        o = t.bank[rr][:, j * W_HD:(j + 1) * W_HD]
                        if m:
                            nc.tensor.matmul(o, sigma[rows, b, ms], state[rows, b, :], start=True, stop=False)
                        mm = nc.tensor.matmul(o, u["ak"][:, j], v[:, m, head(b, rr)], start=not m, stop=True)
                    mm.then_inc(full[rr], 1)
                for rr in range(2):
                    u = buf[rr]
                    pe.wait_ge(read[rr], nth(rr, it, RHS))
                    pe.wait_ge(read[4 + rr], nth(4 + rr, it, TOP))
                    for j in range(4):
                        mm = nc.tensor.matmul(t.bank[rr][:, j * W_HD:(j + 1) * W_HD], u["tt"][:, j], u["rhs"][:, j * W_HD:(j + 1) * W_HD],
                                              start=True, stop=True)
                    mm.then_inc(full[rr], 1)
                for rr in range(2):
                    u, rows = buf[rr], slice(64 * rr, 64 * rr + 64)
                    pe.wait_ge(read[rr], nth(rr, it, SA))
                    take(2 + rr, Y)
                    for j, b in enumerate(blocks):
                        o, js = t.bank[2 + rr][:, j * W_HD:(j + 1) * W_HD], slice(j * W_HD, (j + 1) * W_HD)
                        if m:
                            nc.tensor.matmul(o, r[rows, b, ms], state[rows, b, :], start=True, stop=False)
                        nc.tensor.matmul(o, u["rb"][:, j], u["sa"][:, js], start=not m, stop=False)
                        mm = nc.tensor.matmul(o, u["rk"][:, j], v[:, m, head(b, rr)], start=False, stop=True)
                    mm.then_inc(full[2 + rr], 1)
                    take(4 + rr, UP)
                    for j, b in enumerate(blocks):
                        o, js = t.bank[4 + rr][rows, j * W_HD:(j + 1) * W_HD], slice(j * W_HD, (j + 1) * W_HD)
                        nc.tensor.matmul(o, btok[:, m, head(b, rr)], u["sa"][:, js], start=True, stop=False)
                        mm = nc.tensor.matmul(o, ktok[:, m, head(b, rr)], v[:, m, head(b, rr)], start=False, stop=True)
                    mm.then_inc(full[4 + rr], 1)

        @block.scalar
        def _(act):
            for it, (m, p) in enumerate(steps):
                for rr in range(2):
                    act.wait_ge(full[2 + rr], nth(2 + rr, it, LT))
                    if it:
                        act.wait_ge(s_et, 2 * TOP * it)
                    nc.scalar.activation(buf[rr]["lt"], four(t.bank[2 + rr][:, :]), ACT.Copy).then_inc(read[2 + rr], 1)
                for l in range(1, TOP + 1):
                    for rr in range(2):
                        act.wait_ge(full[rr], nth(rr, it, l))
                        nc.scalar.activation(buf[rr]["x"], four(t.bank[rr][:, :]), ACT.Copy).then_inc(read[rr], 1)
                for use, name in ((RHS, "rhs"), (SA, "sa")):
                    for rr in range(2):
                        act.wait_ge(full[rr], nth(rr, it, use))
                        nc.scalar.activation(buf[rr][name], t.bank[rr][:, 0:4 * W_HD], ACT.Copy).then_inc(read[rr], 1)
                for rr in range(2):
                    act.wait_ge(full[4 + rr], nth(4 + rr, it, UP))
                    dst = btok[:, m, 8 * p * W_HD:8 * (p + 1) * W_HD].rearrange("p (b r n) -> p b r n", b=4, r=2)[:, :, rr, :]
                    nc.scalar.activation(dst, t.bank[2 + rr][:, 0:4 * W_HD].rearrange("p (b n) -> p b n", b=4), ACT.Copy).then_inc(read[2 + rr], 1)

        @block.vector
        def _(dve):
            ch = Chain(dve, s_dve)
            ident = mask(C_IDENT)
            for it, (m, p) in enumerate(steps):
                for rr in range(2):
                    u = buf[rr]
                    dve.wait_ge(full[rr], nth(rr, it, L))
                    ch.add(nc.vector.tensor_tensor(u["t"], four(t.bank[rr][:, :]), low0, ALU.mult))
                    read_l = ch.n
                    dve.wait_ge(read[2 + rr], nth(2 + rr, it, LT))
                    ch.link(nc.vector.tensor_tensor(u["tt"], u["lt"], up(0), ALU.mult))
                    nc.vector.tensor_tensor(u["t"], u["t"], ident, ALU.add).then_inc(s_t0, 1)
                    nc.vector.tensor_tensor(u["tt"], u["tt"], ident, ALU.add).then_inc(s_t0, 1)
                    dve.wait_ge(s_t0, 4 * it + 2 * rr + 2)
                    dve.sem_inc(read[rr], 1)
                    for bank, use, name, col in ((4 + rr, AK, "ak", C_BEFORE), (6, rr, "rb", C_UPTO), (7, rr, "rk", C_UPTO)):
                        dve.wait_ge(full[bank], nth(bank, it, use))
                        nc.vector.tensor_tensor(u[name], four(t.bank[bank][:, :]), mask(col), ALU.mult).then_inc(read[bank], 1)
                for l in range(1, TOP + 1):
                    for rr in range(2):
                        for bank, name in ((2 + rr, "t"), (4 + rr, "tt")):
                            if name == "t" and l == TOP:
                                continue
                            dve.wait_ge(full[bank], nth(bank, it, l))
                            if l > 1:
                                dve.wait_ge(read[bank], nth(bank, it, l - 1))
                            nc.vector.tensor_tensor(buf[rr][name], buf[rr][name], four(t.bank[bank][:, :]), ALU.add).then_inc(read[bank], 1)
                for rr in range(2):
                    rows = slice(64 * rr, 64 * rr + 64)
                    st = state[rows, 4 * p:4 * p + 4, :]
                    new = t.bank[4 + rr][rows, 0:4 * W_HD].rearrange("p (b n) -> p b n", b=4)
                    dve.wait_ge(full[4 + rr], nth(4 + rr, it, UP))
                    if m:
                        ins = nc.vector.tensor_tensor(st, st, new, ALU.add)
                    else:
                        ins = nc.vector.tensor_copy(st, new)
                    ins.then_inc(read[4 + rr], 1)
                    dve.wait_ge(read[4 + rr], nth(4 + rr, it, UP))
                    f = keep["factor"][rows, 4 * p:4 * p + 4, m:m + 1]
                    if m + 1 < NT:
                        nc.vector.tensor_tensor(st, st, wide(f, 64, 4, W_HD), ALU.mult).then_inc(s_st, 1)

        @block.gpsimd
        def _(pool):
            for it, (m, p) in enumerate(steps):
                for l in range(1, TOP + 1):
                    for rr in range(2):
                        u = buf[rr]
                        if l == 1:
                            pool.wait_ge(read[2 + rr], nth(2 + rr, it, LT))
                        if l > 2:
                            pool.wait_ge(full[rr], nth(rr, it, l - 2))
                        elif it:
                            pool.wait_ge(full[rr], nth(rr, it - 1, TOP - 2 + l))
                        nc.gpsimd.tensor_tensor(u["et"][:, l % 2], u["lt"], up(l), ALU.mult).then_inc(s_et, 1)


def rwkv_post_phase(t, a, y, v, g, lnw, lnb, sq, keep):
    nc = t.nc
    with ExitStack() as c:
        sem = lambda n: t.semaphore(f"post_{n}")
        s_ln, s_dve, s_c, s_sq, s_var, s_rt, s_bv, s_pool = (sem(n) for n in ("ln", "dve", "centred", "squares", "var", "root", "bonus_v", "pool"))
        mean = c.enter_context(nc.sbuf_tensor("post_mean", [P, NT, W_HEADS], F32))
        var = c.enter_context(nc.sbuf_tensor("post_var", [P, NT, W_HEADS], F32))
        block = c.enter_context(nc.Block())
        heads = lambda ap: ap.rearrange("p (h n) -> p h n", h=W_HEADS)
        per_head = lambda ap: wide(ap.unsqueeze(2), P, W_HEADS, W_HD)

        @block.sync
        def _(sp):
            sp.dma_start(lnw, wide(a["lnx"][0:1, :], P, D)).then_inc(s_ln, 16)
            sp.dma_start(lnb, wide(a["lnx"][1:2, :], P, D)).then_inc(s_ln, 16)

        @block.gpsimd
        def _(pool):
            ch = Chain(pool, s_pool)
            for m in range(NT):
                bonus = keep["bonus"][:, m * W_HEADS:(m + 1) * W_HEADS]
                nc.gpsimd.tensor_tensor(heads(v[:, m, :]), heads(v[:, m, :]), per_head(bonus), ALU.mult).then_inc(s_bv, 1)
                pool.wait_ge(s_c, m + 1)
                if m:
                    pool.wait_ge(s_var, m)
                nc.gpsimd.tensor_tensor(sq, y[:, m, :], y[:, m, :], ALU.mult).then_inc(s_sq, 1)

        @block.scalar
        def _(act):
            act.wait_ge(s_var, NT)
            nc.scalar.activation(var[:, :, :], var[:, :, :], ACT.Sqrt, bias=t.eps[:, 2:3], scale=1.0 / W_HD).then_inc(s_rt, 1)

        @block.vector
        def _(dve):
            ch = Chain(dve, s_dve)
            for m in range(NT):
                ch.link(nc.vector.tensor_reduce(mean[:, m, :], heads(y[:, m, :]), AX.X, ALU.add))
                ch.link(nc.vector.tensor_scalar(mean[:, m, :], mean[:, m, :], 1.0 / W_HD, None, ALU.mult))
                nc.vector.tensor_tensor(heads(y[:, m, :]), heads(y[:, m, :]), per_head(mean[:, m, :]), ALU.subtract).then_inc(s_c, 1)
                if m:
                    dve.wait_ge(s_sq, m)
                    nc.vector.tensor_reduce(var[:, m - 1, :], heads(sq), AX.X, ALU.add).then_inc(s_var, 1)
            dve.wait_ge(s_sq, NT)
            nc.vector.tensor_reduce(var[:, NT - 1, :], heads(sq), AX.X, ALU.add).then_inc(s_var, 1)
            dve.wait_ge(s_rt, 1)
            ch.link(nc.vector.reciprocal(var[:, :, :], var[:, :, :]))
            dve.wait_ge(s_ln, 32)
            dve.wait_ge(s_c, NT)
            dve.wait_ge(s_bv, NT)
            for m in range(NT):
                ch.link(nc.vector.tensor_tensor(heads(y[:, m, :]), heads(y[:, m, :]), per_head(var[:, m, :]), ALU.mult))
                ch.link(nc.vector.tensor_tensor(y[:, m, :], y[:, m, :], lnw, ALU.mult))
                ch.link(nc.vector.tensor_tensor(y[:, m, :], y[:, m, :], lnb, ALU.add))
                ch.link(nc.vector.tensor_tensor(y[:, m, :], y[:, m, :], v[:, m, :], ALU.add))
                ch.link(nc.vector.tensor_tensor(y[:, m, :], y[:, m, :], g[:, m, :], ALU.mult))


def rwkv(t, a):
    M = views(t, RING, [("ut", (KD, SEQ)), ("xj0", (KD, SEQ)), ("xj1", (KD, SEQ)), ("sigma", (KD, SEQ)), ("ag", (KD, SEQ)), ("r", (KD, SEQ)),
                        ("k", (KD, SEQ)), ("v", (NT, D)), ("sg", (2, SEQ)), ("lw", (SEQ,)), ("la", (SEQ,))])
    at_xj, at_v, at_sg = RING + KD * SEQ, RING + 7 * KD * SEQ, RING + 8 * KD * SEQ
    xn = views(t, at_v, [("xn", (NT, D))])["xn"]
    norm_phase(t, "mix1", t.col("mix1"), xn, M["ut"])
    keep = {"one_minus_mu": t.l0c[:, 0:6 * KD], "mid": t.l0c[:, 64:64 + KD * NT].rearrange("p (b m) -> p b m", b=KD),
            "end": t.l0c[:, 128:128 + KD * NT].rearrange("p (b m) -> p b m", b=KD),
            "factor": t.l0c[:, 192:192 + KD * NT].rearrange("p (b m) -> p b m", b=KD), "bonus": t.l0c[:, 256:256 + NT * W_HEADS]}
    g = views(t, RING, [("g", (NT, D))])["g"]
    rwkv_proj_phase(t, a, M["ut"], [M["xj0"], M["xj1"]], M["sg"], [M["lw"], M["la"]], M["sigma"], M["ag"], M["r"], M["k"], M["v"], g, keep)
    l1c = views(t, at_sg, [("l1c", (L1_ALL,))])["l1c"]
    B = views(t, 0, [("kkn", (KD, SEQ)), ("k2", (2, SEQ)), ("x", (2, SEQ))])
    T = views(t, at_xj, [(n, (2, NT, P)) for n in ("c", "d1", "d2", "pt", "pinv", "pb")] + [("sq", (2, SEQ)), ("root", (2, SEQ))])
    rwkv_keys_phase(t, a, M["k"], B["kkn"], T["sq"], T["root"], l1c)
    rwkv_decay_phase(t, M["sigma"], M["ag"], M["r"], M["k"], B["kkn"], {**T, "k2": B["k2"], "x": B["x"]}, keep)
    btok, ktok = t.ring[0].rearrange("p k n -> p (k n)").rearrange("p (m n) -> p m n", m=NT), t.ring[1].rearrange("p k n -> p (k n)").rearrange("p (m n) -> p m n", m=NT)
    rwkv_rows_phase(t, M["ag"], M["k"], btok, ktok)
    spec = [("t", (4, P)), ("tt", (4, P)), ("lt", (4, P)), ("et", (2, 4, P)), ("x", (4, P)), ("ak", (4, P)), ("rb", (4, P))]
    buf = [views(t, at_xj + i * 8 * HALF, spec) for i in range(2)]
    for i in range(2):
        buf[i].update(views(t, at_sg + L1_ALL + i * 2 * HALF // 2 * 2, [("rk", (4, P)), ("rhs", (4 * W_HD,)), ("sa", (4 * W_HD,))]))
    state = t.zero[:, 0:KD * W_HD].rearrange("p (b n) -> p b n", b=KD)
    rwkv_scan_phase(t, M["sigma"], M["ag"], M["r"], M["k"], M["v"], btok, ktok, buf, state, keep, l1c)
    E = views(t, at_xj, [("lnw", (D,)), ("lnb", (D,)), ("sq", (D,))])
    rwkv_post_phase(t, a, btok, M["v"], g, E["lnw"], E["lnb"], E["sq"], keep)
    return btok


def final_phase(t, a, out, w, y):
    nc = t.nc
    with ExitStack() as c:
        sem = lambda n: t.semaphore(f"final_{n}")
        s_w, s_ms, s_rs, s_y, s_out = (sem(n) for n in ("weight", "ms", "rs", "y", "out"))
        ms = c.enter_context(nc.sbuf_tensor("final_ms", [P, NT], F32))
        block = c.enter_context(nc.Block())

        @block.sync
        def _(sp):
            sp.dma_start(w, wide(a["final_w"], P, D)).then_inc(s_w, 16)
            rows = out.rearrange("o (m p) d -> p (o m) d", p=P)
            for m in range(NT):
                sp.wait_ge(s_y, m + 1)
                sp.dma_start(rows[:, m, :], y[:, m, :]).then_inc(s_out, 16)
            sp.wait_ge(s_out, 16 * NT)

        @block.scalar
        def _(act):
            act.wait_ge(s_ms, NT)
            nc.scalar.activation(ms[:, :], ms[:, :], ACT.Sqrt, bias=t.eps[:, 0:1]).then_inc(s_rs, 1)

        @block.vector
        def _(dve):
            for m in range(NT):
                nc.vector.tensor_tensor_reduce(y[:, m, :], t.h[:, m, :], t.h[:, m, :], 1.0 / D, 0.0, ALU.mult, ALU.add,
                                               ms[:, m:m + 1]).then_inc(s_ms, 1)
            dve.wait_ge(s_rs, 1)
            nc.vector.reciprocal(ms[:, :], ms[:, :]).then_inc(s_rs, 1)
            dve.wait_ge(s_rs, 2)
            dve.wait_ge(s_w, 16)
            for m in range(NT):
                nc.vector.scalar_tensor_tensor(out=y[:, m, :], in0=t.h[:, m, :], scalar=ms[:, m:m + 1], in1=w, op0=ALU.mult,
                                               op1=ALU.mult).then_inc(s_y, 1)


def _(sp):
            sp.dma_start(out.rearrange("o (m p) d -> p (o m) d", p=P), t.h[:, :, :] if srcs is None else srcs).then_inc(s, 16)
            sp.wait_ge(s, 16)


INPUTS = {"x": (1, SEQ, D), "w_in_e": None, "w_out_e": None, "cols": (P, N_COLS), "rows": (1, N_ROWS), "common": (P, C_ALL),
          "layer0": (P, L0_ALL), "layer1": (P, L1_ALL)}


def views(t, start, spec):
    out, at = {}, start
    for name, shape in spec:
        n = int(np.prod(shape))
        v = t.arena[:, at:at + n]
        if len(shape) == 2:
            v = v.rearrange("p (a b) -> p a b", a=shape[0])
        if len(shape) == 3:
            v = v.rearrange("p (a b c) -> p a b c", a=shape[0], b=shape[1])
        if len(shape) == 4:
            v = v.rearrange("p (a b c d) -> p a b c d", a=shape[0], b=shape[1], c=shape[2])
        out[name] = v
        at += n
    assert at <= ARENA, (at, ARENA)
    return out


ARENA = 44800
RING = 2 * KD * HALF


def trunk(nc, a, out):
    with ExitStack() as c:
        t = Trunk(nc)
        sb = lambda name, shape, dt=F32: c.enter_context(nc.sbuf_tensor(name, shape, dt))
        t.h = sb("h", [P, NT, D])
        t.cols, t.rows = sb("cols", [P, N_COLS]), sb("rows", [P, N_ROWS])
        t.common, t.l0c = sb("common", [P, C_ALL]), sb("layer0", [P, L0_ALL])
        t.zero = sb("zero", [P, D])
        t.eps = sb("eps", [P, 3])
        t.weight, t.slot, t.meta = sb("weight", [P, NT, 2]), sb("slot", [P, NT, 2], U32), sb("meta", [1, 1 + MAX_BLOCKS], I32)
        t.arena = sb("arena", [P, ARENA])
        t.bank = [c.enter_context(nc.psum_tensor(f"bank{i}", [P, HALF], F32)) for i in range(8)]
        t.ident = t.common[:, C_IDENT:C_IDENT + P]
        t.col = lambda n: t.cols[:, COLS[n][0]:COLS[n][0] + COLS[n][1]]
        t.row = lambda n: t.rows[:, ROWS[n][0]:ROWS[n][0] + ROWS[n][1]]
        t.s_win = [c.enter_context(nc.semaphore(f"w_in_loaded{i}")) for i in range(2)]
        t.s_wout = [c.enter_context(nc.semaphore(f"w_out_loaded{i}")) for i in range(2)]
        t.s_rwout = [c.enter_context(nc.semaphore(f"rw_out_loaded{i}")) for i in range(2)]
        t.s_clear = c.enter_context(nc.semaphore("slots_cleared"))
        t.xg = a["xg"]
        ring = views(t, 0, [("r0", (KD, HALF)), ("r1", (KD, HALF))])
        t.ring = [ring["r0"], ring["r1"]]

        load_phase(t, a)
        at = RING
        A = views(t, at, [("ut", (KD, SEQ)), ("xbc", (XBC_BLOCKS, XPAD)), ("xc", (XBC_BLOCKS, SEQ)), ("z", (NT, D)), ("g", (NT, D)),
                          ("v", (NT, D)), ("q", (NT, HALF)), ("k", (NT, HALF)), ("dt", (NT, S_HEADS)), ("a_dt", (NT * S_HEADS,)),
                          ("nacum", (NT * S_HEADS,)), ("cum", (3 * NT * S_HEADS,)), ("ecum", (3 * NT * S_HEADS,)),
                          ("ea", ((NT + 1) * S_HEADS,)), ("bt", (NT, S_GROUPS * S_N)), ("tmp", (2, NT, R_HEADS, R_QK // 2))])
        at_ut, at_xbc = at, at + KD * SEQ
        at_xc = at_xbc + XBC_BLOCKS * XPAD
        at_z = at_xc + XBC_BLOCKS * SEQ
        at_v = at_z + 2 * NT * D
        at_q = at_v + NT * D
        at_tmp = ARENA_TMP = at_q + 2 * NT * HALF + (1 + 1 + 1 + 3 + 3 + 1) * NT * S_HEADS + S_HEADS + NT * S_GROUPS * S_N
        xn = views(t, at_xc, [("xn", (NT, D))])["xn"]
        norm_phase(t, "mix0", t.col("mix0"), xn, A["ut"])
        in_proj_phase(t, a, A["ut"], A["xbc"], A["xc"], A["z"], A["g"], A["v"], A["q"], A["k"], A["dt"])
        R = views(t, at_xbc, [("qr", (NT, HALF)), ("kr", (NT, HALF)), ("kd", (NT, HALF))])
        xs = views(t, at_ut, [("xs", (NT, D))])["xs"]
        qt, kt = (A[n].rearrange("p m n -> p (m n)").rearrange("p (h n) -> p h n", h=R_HEADS) for n in "qk")
        rows_phase(t, A["xc"], xs, A["bt"], A["q"], A["k"], R["qr"], R["kr"], qt, kt, R["kd"], A["tmp"], A["dt"], A["a_dt"],
                   A["nacum"], A["cum"], A["ecum"], A["ea"])
        T = views(t, at_tmp, [("s", (2, R_HEADS, P))])
        T2 = views(t, RING - 2 * R_HEADS * R_V, [("state", (2, R_HEADS, R_V))])
        yr = views(t, at_xc, [("yr", (NT, D))])["yr"]
        yraw = views(t, 0, [("yraw", (NT, D))])["yraw"]
        retention_phase(t, qt, kt, R["kd"], A["v"], A["g"], T["s"], T2["state"], yraw, yr)
        S1 = views(t, at_q, [("e", (2, S_HPG, P)), ("xdt", (2, HALF)), ("xde", (2, HALF))])
        S2 = views(t, at_tmp, [("state", (S_GROUPS, HALF)), ("decayed", (S_GROUPS, HALF))])
        y1 = views(t, at_xbc, [("y1", (2, HALF))])["y1"]
        ys = A["v"]
        ssd_phase(t, A["xc"], xs, A["bt"], A["z"], A["dt"], A["a_dt"], A["nacum"], A["ecum"], S1["e"], S1["xdt"], S1["xde"],
                  S2["state"], S2["decayed"], y1, ys)
        mt = views(t, at_z, [("mt", (2 * KD, SEQ))])["mt"]
        w = a["w_out_e"][0].rearrange("(j k p) n -> j p k n", p=P, k=KD)
        proj_phase(t, "wout", [ys, yr], [t.col("ssdn"), None], mt,
                   [w[j][:, :, n * HALF:(n + 1) * HALF] for n in range(2) for j in range(2)], t.ring, t.s_wout)
        moe(t, a, 0)
        t.recycle_semaphores()
        y = rwkv(t, a)
        O = views(t, RING + 3 * KD * SEQ, [("ring0", (KD, HALF)), ("ring1", (KD, HALF)), ("mt", (KD, SEQ))])
        w = a["rw_wo"][0].rearrange("(k p) n -> p k n", p=P)
        proj_phase(t, "rwout", [y], [None], O["mt"], [w[:, :, n * HALF:(n + 1) * HALF] for n in range(2)], [O["ring0"], O["ring1"]], t.s_rwout)
        moe(t, a, 1)
        final_phase(t, a, out, *(views(t, 0, [("w", (D,)), ("y", (NT, D))])[n] for n in ("w", "y")))


def kernel(**inputs):
    import concourse.bacc as bacc
    from concourse.bass_utils import run_bass_kernel_spmd

    f = {k: np.asarray(v) for k, v in inputs.items()}

    def blocks(v):
        return np.ascontiguousarray(v.reshape(-1, P).T)

    named = {"mix0": f["norm_mix_w"][0], "mix1": f["norm_mix_w"][1], "ffn0": f["norm_ffn_w"][0], "ffn1": f["norm_ffn_w"][1],
             "conv": f["ssd_conv_w"], "convb": f["ssd_conv_b"], "ssdn": f["ssd_norm_w"], "mu": f["rw_mu"], "w0": f["rw_w0"],
             "a0": f["rw_a0"], "kk": f["rw_kk"], "ka": f["rw_ka"], "rk": f["rw_rk"]}
    common, layer0, layer1 = shape_constants()
    mb = [np.concatenate([f["moe_bg"][i], f["moe_be"][i]]) for i in range(DEPTH)]
    arrays = {"x": f["x"], "w_in_e": f["w_in_e"], "w_out_e": f["w_out_e"],
              "cols": np.concatenate([blocks(named[n]) for n in COLS], 1),
              "rows": np.concatenate([f["ssd_dt_bias"][0], f["ssd_a_log"][0], f["ssd_d"][0], *mb])[None],
              "common": common, "layer0": layer0, "layer1": layer1}
    for n in ("rw_wr", "rw_wk", "rw_wv", "rw_wo", "rw_w1", "rw_w2", "rw_a1", "rw_a2", "rw_g1", "rw_g2", "moe_w1", "moe_w3", "moe_w2"):
        arrays[n] = f[n]
    arrays["router"] = np.ascontiguousarray(np.concatenate([f["moe_wg"], f["moe_we"]], 2).reshape(DEPTH, KD, P, -1).transpose(0, 2, 1, 3))
    arrays["final_w"] = f["norm_final_w"][None]
    arrays["lnx"] = np.stack([f["rw_lnx_w"][0], f["rw_lnx_b"][0]])
    nc = bacc.Bacc("TRN2", target_bir_lowering=False, num_devices=1)
    feed = {f"in_{n}": np.ascontiguousarray(v) for n, v in arrays.items()}
    aps = {n: nc.dram_tensor(f"in_{n}", v.shape, mybir.dt.from_np(v.dtype), kind="ExternalInput").ap() for n, v in arrays.items()}
    aps["xg"] = nc.dram_tensor("slot_rows", (MAX_BLOCKS * SLOTS, D), F32, kind="Internal").ap()
    out = nc.dram_tensor("out_trunk", (1, SEQ, D), F32, kind="ExternalOutput").ap()
    trunk(nc, aps, out)
    r = run_bass_kernel_spmd(nc, [feed], core_ids=[0])
    return r.results[0]["out_trunk"]
```

```python
from contextlib import ExitStack

import concourse.bass as bass
import numpy as np
from concourse import mybir

ALU = mybir.AluOpType
ACT = mybir.ActivationFunctionType
F32 = mybir.dt.float32
I32 = mybir.dt.int32
U32 = mybir.dt.uint32
AX = mybir.AxisListType

P = 128
SEQ, D = 512, 1024
NT = SEQ // P
KD = D // P
HALF = 512
DEPTH = 2
RMS_EPS = 1e-6
S_HEADS, S_HD, S_GROUPS, S_N, S_CONV = 16, 64, 2, 128, 4
S_HPG = S_HEADS // S_GROUPS
XBC_BLOCKS = (D + 2 * S_GROUPS * S_N) // P
XPAD = SEQ + S_CONV - 1
R_HEADS, R_QK, R_V = 4, 128, 256
W_HEADS, W_HD, W_LORA, G_LORA = 16, 64, 64, 160
LN_EPS = 64e-5
LOG_DECAY = -float(np.exp(-0.5))
LEVELS = 7
GROUPS, EPG = 4, 4
EXPERTS, FF = GROUPS * EPG, 512
SLOTS = P
MAX_BLOCKS = 24

Z0, X0 = 0, D
DT0 = X0 + XBC_BLOCKS * P
Q0 = DT0 + S_HEADS
K0 = Q0 + R_HEADS * R_QK
V0 = K0 + R_HEADS * R_QK
G0 = V0 + D
IN_CHUNKS = ([("x", X0 + HALF * i, HALF) for i in range(3)] + [("q", Q0, HALF), ("k", K0, HALF)]
             + [("dt", DT0, S_HEADS)] + [("v", V0, HALF), ("v", V0 + HALF, HALF)]
             + [("z", Z0, HALF), ("z", Z0 + HALF, HALF), ("g", G0, HALF), ("g", G0 + HALF, HALF)])

COLS = {}
for _n, _w in (("mix0", KD), ("mix1", KD), ("ffn0", KD), ("ffn1", KD), ("conv", S_CONV * XBC_BLOCKS),
               ("convb", XBC_BLOCKS), ("ssdn", KD), ("mu", 6 * KD), ("w0", KD), ("a0", KD), ("kk", KD),
               ("ka", KD), ("rk", KD)):
    COLS[_n] = (sum(w for _, w in COLS.values()), _w)
N_COLS = sum(w for _, w in COLS.values())
ROWS = {}
for _n, _w in (("dtb", S_HEADS), ("alog", S_HEADS), ("dskip", S_HEADS), ("mb0", GROUPS + EXPERTS), ("mb1", GROUPS + EXPERTS)):
    ROWS[_n] = (sum(w for _, w in ROWS.values()), _w)
N_ROWS = sum(w for _, w in ROWS.values())


def shape_constants():
    i = np.arange(P)
    f = np.float32
    ident = np.eye(P)
    upto = (i[:, None] <= i[None, :])
    before = (i[:, None] < i[None, :])
    neg = np.where(upto, 0.0, -1e30)
    same_half = (i[:, None] // 64 == i[None, :] // 64)
    half_sel = np.stack([i < 64, i >= 64], 1)
    iota4 = np.tile(np.arange(4), (P, 1))
    blk = np.tile(np.arange(MAX_BLOCKS), (P, 1))
    common = np.concatenate([ident, upto, before, neg, same_half, half_sel, iota4, blk, np.ones((P, P))], 1).astype(f)
    lg = np.log(1.0 - 2.0 ** (-5.0 - np.arange(R_HEADS)))
    ret = np.where(upto[:, None, :], np.exp(-(i[:, None, None] + 1.0) * lg[None, :, None]) * R_QK ** -0.5, 0.0)
    qdec = np.exp((i[:, None] + 1.0) * lg[None])
    kdec = np.exp((P - 1.0 - i[:, None]) * lg[None]) * R_QK ** -0.5
    half = R_QK // 2
    inv = f(10000.0) ** (-np.arange(half, dtype=f) / f(half))
    ang = np.arange(SEQ, dtype=f)[:, None] * inv[None]
    cos = np.cos(ang.astype(np.float64)).reshape(NT, P, half).transpose(1, 0, 2).reshape(P, -1)
    sin = np.sin(ang.astype(np.float64)).reshape(NT, P, half).transpose(1, 0, 2).reshape(P, -1)
    layer0 = np.concatenate([ret.reshape(P, -1), qdec, kdec, cos, sin], 1).astype(f)
    lev = []
    for l in range(LEVELS):
        b = i >> l
        lev.append((b[:, None] >> 1 == b[None, :] >> 1) & (b[:, None] & 1 == 1) & (b[None, :] & 1 == 0))
    low = np.stack(lev, 1)
    up = np.stack([m.T for m in lev], 1)
    layer1 = np.concatenate([low.reshape(P, -1), up.reshape(P, -1)], 1).astype(f)
    return common, layer0, layer1


C_IDENT, C_UPTO, C_BEFORE, C_NEG, C_SAME = (P * n for n in range(5))
C_HALF = 5 * P
C_IOTA = C_HALF + 2
C_BLK = C_IOTA + 4
C_ONES = C_BLK + MAX_BLOCKS
C_ALL = C_ONES + P
L0_RET = 0
L0_QDEC = R_HEADS * P
L0_KDEC = L0_QDEC + R_HEADS
L0_COS = L0_KDEC + R_HEADS
L0_SIN = L0_COS + NT * R_QK // 2
L0_ALL = L0_SIN + NT * R_QK // 2
L1_ALL = 2 * LEVELS * P


class Chain:

    def __init__(self, engine, sem):
        self.engine, self.sem, self.n = engine, sem, 0

    def add(self, ins):
        ins.then_inc(self.sem, 1)
        self.n += 1
        return self.n

    def wait(self, n=None):
        self.engine.wait_ge(self.sem, self.n if n is None else n)

    def link(self, ins):
        self.add(ins)
        self.wait()


class Trunk:

    def __init__(self, nc):
        self.nc, self.phase_semaphores = nc, []

    def semaphore(self, name):
        self.phase_semaphores.append(self.nc.alloc_semaphore(name))
        return self.phase_semaphores[-1]

    def recycle_semaphores(self):
        self.nc.clear_and_free_semaphores(self.phase_semaphores)
        self.nc.all_engine_barrier()
        self.phase_semaphores = []


def wide(ap, *shape):
    return ap.to_broadcast(list(shape))


def norm_phase(t, tag, w_col, xn, ut, loading=False, prefetch=None):
    nc = t.nc
    with ExitStack() as c:
        s_ms = t.semaphore(f"{tag}_ms")
        s_rs = t.semaphore(f"{tag}_rs")
        s_xn = t.semaphore(f"{tag}_xn")
        s_tr = t.semaphore(f"{tag}_transposed")
        s_ev = t.semaphore(f"{tag}_evacuated")
        ms = c.enter_context(nc.sbuf_tensor(f"{tag}_ms", [P, NT], F32))
        block = c.enter_context(nc.Block())

        if prefetch is not None:
            @block.sync
            def _(sp):
                prefetch(sp)

        @block.vector
        def _(dve):
            if loading:
                dve.wait_ge(t.s_x, 16)
                dve.wait_ge(t.s_const, 5 * 16)

            def evacuate(m):
                for b in range(2):
                    dve.wait_ge(s_tr, 2 * m + b + 1)
                    nc.vector.tensor_tensor(ut[:, 4 * b:4 * b + 4, m * P:(m + 1) * P],
                                            t.bank[(2 * m + b) % 8][:, :].rearrange("p (k n) -> p k n", k=4),
                                            wide(w_col[:, 4 * b:4 * b + 4].unsqueeze(2), P, 4, P), ALU.mult).then_inc(s_ev, 1)

            for m in range(NT):
                nc.vector.tensor_tensor_reduce(xn[:, m, :], t.h[:, m, :], t.h[:, m, :], 1.0 / D, 0.0,
                                               ALU.mult, ALU.add, ms[:, m:m + 1]).then_inc(s_ms, 1)
            dve.wait_ge(s_rs, 1)
            nc.vector.reciprocal(ms[:, :], ms[:, :]).then_inc(s_rs, 1)
            dve.wait_ge(s_rs, 2)
            for m in range(NT):
                nc.vector.tensor_scalar(xn[:, m, :], t.h[:, m, :], ms[:, m:m + 1], None, ALU.mult).then_inc(s_xn, 1)
                if m:
                    evacuate(m - 1)
            evacuate(NT - 1)

        @block.scalar
        def _(act):
            act.wait_ge(s_ms, NT)
            nc.scalar.activation(ms[:, :], ms[:, :], ACT.Sqrt, bias=t.eps[:, 0:1]).then_inc(s_rs, 1)

        @block.tensor
        def _(pe):
            if loading:
                pe.wait_ge(t.s_const, 5 * 16)
            for m in range(NT):
                pe.wait_ge(s_xn, m + 1)
                for k in range(KD):
                    mm = nc.tensor.transpose(t.bank[(2 * m + k // 4) % 8][:, (k % 4) * P:(k % 4 + 1) * P],
                                             xn[:, m, k * P:(k + 1) * P], t.ident)
                    if k % 4 == 3:
                        mm.then_inc(s_tr, 1)


def load_phase(t, a):
    nc = t.nc
    with ExitStack() as c:
        block = c.enter_context(nc.Block())

        @block.sync
        def _(sp):
            sp.dma_start(t.h[:, :, :], a["x"].rearrange("o (m p) d -> p (o m) d", p=P)).then_inc(t.s_x, 16)
            for n in range(2):
                _, c0, width = IN_CHUNKS[n]
                sp.dma_start(t.ring[n % 2][:, :, 0:width], a["w_in_e"][0].rearrange("(k p) n -> p k n", p=P)[:, :, c0:c0 + width]
                             ).then_inc(t.s_win[n % 2], 16)

        @block.scalar
        def _(act):
            act.dma_start(t.common[:, :], a["common"]).then_inc(t.s_const, 16)
            act.dma_start(t.cols[:, :], a["cols"]).then_inc(t.s_const, 16)
            act.dma_start(t.l0c[:, :], a["layer0"]).then_inc(t.s_const, 16)
            act.dma_start(t.rows[:, :], wide(a["rows"], P, N_ROWS)).then_inc(t.s_const, 16)
            act.dma_start(t.router[:, :, :, :], a["router"]).then_inc(t.s_const, 16)

        @block.vector
        def _(dve):
            nc.vector.memset(t.zero[:, :], 0.0)
            for i, eps in enumerate((RMS_EPS, 1e-5, LN_EPS)):
                nc.vector.memset(t.eps[:, i:i + 1], eps)


def in_proj_phase(t, a, ut, xbc, xc, z, g, v, q, k, dt):
    nc = t.nc
    win = a["w_in_e"][0].rearrange("(k p) n -> p k n", p=P)
    out = {"z": z, "g": g, "v": v, "q": q, "k": k}
    first = {"z": Z0, "g": G0, "v": V0, "q": Q0, "k": K0}
    order = [kind for kind, _, _ in IN_CHUNKS]
    n_x = order.count("x")
    with ExitStack() as c:
        s_pe = t.semaphore("in_group")
        s_ev = t.semaphore("in_evacuated")
        s_pad = t.semaphore("in_pad")
        s_dve = t.semaphore("in_dve")
        s_conv = t.semaphore("in_conv")
        block = c.enter_context(nc.Block())

        @block.sync
        def _(sp):
            for n in range(2, len(IN_CHUNKS)):
                sp.wait_ge(s_pe, NT * (n - 1))
                _, c0, width = IN_CHUNKS[n]
                sp.dma_start(t.ring[n % 2][:, :, 0:width], win[:, :, c0:c0 + width]).then_inc(t.s_win[n % 2], 16)

        @block.tensor
        def _(pe):
            for n, (kind, _, width) in enumerate(IN_CHUNKS):
                pe.wait_ge(t.s_win[n % 2], 16 * (n // 2 + 1))
                w = t.ring[n % 2]
                for m in range(NT):
                    i = NT * n + m
                    if i >= 8:
                        pe.wait_ge(s_ev, i - 7)
                    for kk in range(KD):
                        if kind == "x":
                            mm = nc.tensor.matmul(t.bank[i % 8][:, :], w[:, kk, m * P:(m + 1) * P], ut[:, kk, :],
                                                  start=kk == 0, stop=kk == KD - 1)
                        else:
                            mm = nc.tensor.matmul(t.bank[i % 8][:, 0:width], ut[:, kk, m * P:(m + 1) * P],
                                                  w[:, kk, 0:width], start=kk == 0, stop=kk == KD - 1)
                    mm.then_inc(s_pe, 1)

        @block.scalar
        def _(act):
            act.wait_ge(s_pad, 1)
            for n, (kind, c0, width) in enumerate(IN_CHUNKS):
                for m in range(NT):
                    i = NT * n + m
                    act.wait_ge(s_pe, i + 1)
                    src = t.bank[i % 8]
                    if kind == "x":
                        nc.scalar.activation(xbc[:, NT * n + m, S_CONV - 1:XPAD], src[:, :], ACT.Copy).then_inc(s_ev, 1)
                    elif kind == "dt":
                        nc.scalar.activation(dt[:, m, :], src[:, 0:width], ACT.Copy).then_inc(s_ev, 1)
                    else:
                        o = c0 - first[kind]
                        nc.scalar.activation(out[kind][:, m, o:o + width], src[:, 0:width],
                                             ACT.Silu if kind in "zg" else ACT.Copy).then_inc(s_ev, 1)
            act.wait_ge(s_conv, XBC_BLOCKS)
            for b in range(XBC_BLOCKS):
                nc.scalar.activation(xc[:, b, :], xc[:, b, :], ACT.Silu)

        @block.gpsimd
        def _(pool):
            for b in range(MAX_BLOCKS + 2):
                if b % 4 == 0:
                    pool.wait_ge(s_pe, 4 + 6 * (b // 4))
                pool.dma_start(t.xg[b * SLOTS:(b + 1) * SLOTS, :], t.zero[:, :]).then_inc(t.s_clear, 16)

        @block.vector
        def _(dve):
            chain = Chain(dve, s_dve)
            nc.vector.memset(xbc[:, :, 0:S_CONV - 1], 0.0).then_inc(s_pad, 1)
            cw, cb = t.col("conv"), t.col("convb")
            for b in range(XBC_BLOCKS):
                dve.wait_ge(s_ev, b + 1)
                chain.link(nc.vector.tensor_scalar(xc[:, b, :], xbc[:, b, 0:SEQ], cw[:, b:b + 1], cb[:, b:b + 1],
                                                   ALU.mult, ALU.add))
                for j in range(1, S_CONV):
                    w = cw[:, j * XBC_BLOCKS + b:j * XBC_BLOCKS + b + 1]
                    ins = nc.vector.scalar_tensor_tensor(out=xc[:, b, :], in0=xbc[:, b, j:j + SEQ], scalar=w,
                                                         in1=xc[:, b, :], op0=ALU.mult, op1=ALU.add)
                    if j < S_CONV - 1:
                        chain.link(ins)
                    else:
                        ins.then_inc(s_conv, 1)


def rope(nc, chain, t, dst, src, tmp, s_done):
    h = R_QK // 2
    s4 = src[:, :, :].rearrange("p m (h d) -> p m h d", h=R_HEADS)
    d4 = dst[:, :, :].rearrange("p m (h d) -> p m h d", h=R_HEADS)
    cos = t.l0c[:, L0_COS:L0_SIN].rearrange("p (m d) -> p m d", m=NT)
    sin = t.l0c[:, L0_SIN:L0_ALL].rearrange("p (m d) -> p m d", m=NT)
    for m in range(NT):
        c = wide(cos[:, m, :].unsqueeze(1), P, R_HEADS, h)
        s = wide(sin[:, m, :].unsqueeze(1), P, R_HEADS, h)
        x1, x2, y1, y2 = s4[:, m, :, 0:h], s4[:, m, :, h:], d4[:, m, :, 0:h], d4[:, m, :, h:]
        chain.add(nc.vector.tensor_tensor(y1, x1, c, ALU.mult))
        chain.add(nc.vector.tensor_tensor(tmp[:, 0, m], x2, s, ALU.mult))
        chain.add(nc.vector.tensor_tensor(y2, x1, s, ALU.mult))
        chain.add(nc.vector.tensor_tensor(tmp[:, 1, m], x2, c, ALU.mult))
    chain.wait()
    for m in range(NT):
        y1, y2 = d4[:, m, :, 0:h], d4[:, m, :, h:]
        nc.vector.tensor_tensor(y1, y1, tmp[:, 0, m], ALU.subtract).then_inc(s_done, 1)
        nc.vector.tensor_tensor(y2, y2, tmp[:, 1, m], ALU.add).then_inc(s_done, 1)


def rows_phase(t, xc, xs, bt, q, k, qr, kr, qt, kt, kd, tmp, dt, a_dt, nacum, cum, ecum, ea):
    nc = t.nc
    n_x, n_b, n_q = KD * NT // 4, S_GROUPS * NT // 4, 2 * R_HEADS
    with ExitStack() as c:
        s_tr = t.semaphore("row_transposed")
        s_ev = t.semaphore("row_evacuated")
        s_dve = t.semaphore("row_dve")
        s_abs = t.semaphore("row_abs")
        s_exp = t.semaphore("row_exp")
        s_rope = t.semaphore("row_rope")
        s_a = t.semaphore("row_a")
        s_sum = t.semaphore("row_sum")
        s_cum = t.semaphore("row_cum")
        block = c.enter_context(nc.Block())

        @block.tensor
        def _(pe):
            todo = [[xc[:, b + j, m * P:(m + 1) * P] for j in range(4)] for m in range(NT) for b in (0, 4)]
            todo += [[xc[:, KD + j % 2, (m + j // 2) * P:(m + j // 2 + 1) * P] for j in range(4)] for m in (0, 2)]
            todo += [[src[:, m, h * P:(h + 1) * P] for m in range(NT)] for src in (qr, kr) for h in range(R_HEADS)]
            for n, four in enumerate(todo):
                if n == n_x + n_b:
                    pe.wait_ge(s_a, 1)
                    nc.tensor.matmul(t.bank[7][:, 0:NT * S_HEADS], t.common[:, C_UPTO:C_UPTO + P], a_dt[:, :], start=True, stop=True)
                    nc.tensor.matmul(t.bank[7][:, NT * S_HEADS:2 * NT * S_HEADS], t.common[:, C_ONES:C_ONES + P], a_dt[:, :],
                                     start=True, stop=True).then_inc(s_sum, 1)
                    pe.wait_ge(s_rope, 2 * NT)
                if n == n_x + n_b + R_HEADS:
                    pe.wait_ge(s_rope, 4 * NT)
                if n >= 7:
                    pe.wait_ge(s_ev, n - 6)
                for j, src in enumerate(four):
                    mm = nc.tensor.transpose(t.bank[n % 7][:, j * P:(j + 1) * P], src, t.ident)
                mm.then_inc(s_tr, 1)

        @block.scalar
        def _(act):
            act.wait_ge(s_abs, 1)
            nc.scalar.activation(ea[:, 0:NT * S_HEADS], ea[:, 0:NT * S_HEADS], ACT.Exp, scale=-1.0).then_inc(s_exp, 1)
            nc.scalar.activation(ea[:, NT * S_HEADS:], t.row("alog"), ACT.Exp).then_inc(s_exp, 1)
            act.wait_ge(s_exp, 1)
            nc.scalar.activation(ea[:, 0:NT * S_HEADS], ea[:, 0:NT * S_HEADS], ACT.Ln, bias=1.0).then_inc(s_exp, 1)
            for n in range(n_x + n_b + n_q):
                act.wait_ge(s_tr, n + 1)
                if n < n_x:
                    dst = xs[:, n // 2, (n % 2) * HALF:(n % 2 + 1) * HALF]
                elif n < n_x + n_b:
                    dst = bt[:, 2 * (n - n_x):2 * (n - n_x) + 2, :].rearrange("p a b -> p (a b)")
                else:
                    dst = (qt, kt)[(n - n_x - n_b) // R_HEADS][:, (n - n_x - n_b) % R_HEADS, :]
                nc.scalar.activation(dst, t.bank[n % 7][:, :], ACT.Copy).then_inc(s_ev, 1)
            act.wait_ge(s_cum, 3)
            nc.scalar.activation(ecum[:, :], cum[:, :], ACT.Exp)

        @block.vector
        def _(dve):
            ch = Chain(dve, s_dve)
            w = NT * S_HEADS
            per_head = wide(t.row("dtb").unsqueeze(1), P, NT, S_HEADS)
            ch.link(nc.vector.tensor_tensor(dt[:, :, :], dt[:, :, :], per_head, ALU.add))
            flat = dt[:, :, :].rearrange("p m h -> p (m h)")
            nc.vector.scalar_tensor_tensor(out=ea[:, 0:w], in0=flat, scalar=-1.0, in1=flat, op0=ALU.mult, op1=ALU.max).then_inc(s_abs, 1)
            ch.link(nc.vector.tensor_scalar(flat, flat, 0.0, None, ALU.max))
            dve.wait_ge(s_exp, 3)
            ch.link(nc.vector.tensor_tensor(flat, flat, ea[:, 0:w], ALU.add))
            a3 = a_dt[:, :].rearrange("p (m h) -> p m h", m=NT)
            nc.vector.scalar_tensor_tensor(out=a3, in0=dt[:, :, :], scalar=-1.0, in1=wide(ea[:, w:].unsqueeze(1), P, NT, S_HEADS),
                                           op0=ALU.mult, op1=ALU.mult).then_inc(s_a, 1)
            rope(nc, ch, t, qr, q, tmp, s_rope)
            dve.wait_ge(s_sum, 1)
            nc.vector.tensor_copy(cum[:, 0:2 * w], t.bank[7][:, 0:2 * w]).then_inc(s_cum, 1)
            dve.wait_ge(s_cum, 1)
            nc.vector.tensor_scalar(nacum[:, :], cum[:, 0:w], -1.0, None, ALU.mult).then_inc(s_cum, 1)
            nc.vector.tensor_tensor(cum[:, 2 * w:], cum[:, w:2 * w], cum[:, 0:w], ALU.subtract).then_inc(s_cum, 1)
            dve.wait_ge(s_rope, 2 * NT)
            rope(nc, ch, t, kr, k, tmp, s_rope)
            dve.wait_ge(s_rope, 4 * NT)
            for h in range(R_HEADS):
                hs = slice(h * R_QK, (h + 1) * R_QK)
                nc.vector.tensor_scalar(kd[:, :, hs], kr[:, :, hs], t.l0c[:, L0_KDEC + h:L0_KDEC + h + 1], None, ALU.mult)


def retention_phase(t, qt, kt, kd, v, g, s, state, yraw, y):
    nc = t.nc
    gamma = [1.0 - 2.0 ** (-5.0 - h) for h in range(R_HEADS)]
    with ExitStack() as c:
        s_qk = t.semaphore("ret_scores")
        s_msk = t.semaphore("ret_masked")
        s_y = t.semaphore("ret_y")
        s_up = t.semaphore("ret_update")
        s_st = t.semaphore("ret_state")
        s_raw = t.semaphore("ret_raw")
        s_ms = t.semaphore("ret_ms")
        s_rs = t.semaphore("ret_rs")
        ss = c.enter_context(nc.sbuf_tensor("ret_ss", [P, NT, R_HEADS], F32))
        block = c.enter_context(nc.Block())

        @block.tensor
        def _(pe):
            def scores(m):
                ms = slice(m * P, (m + 1) * P)
                if m >= 2:
                    pe.wait_ge(s_msk, m - 1)
                for h in range(R_HEADS):
                    mm = nc.tensor.matmul(t.bank[m % 2][:, h * P:(h + 1) * P], kt[:, h, ms], qt[:, h, ms], start=True, stop=True)
                mm.then_inc(s_qk, 1)

            scores(0)
            for m in range(NT):
                if m + 1 < NT:
                    scores(m + 1)
                    if m:
                        pe.wait_ge(s_st, R_HEADS * m)
                    for h in range(R_HEADS):
                        mm = nc.tensor.matmul(t.bank[6 + h // 2][:, (h % 2) * R_V:(h % 2 + 1) * R_V], kd[:, m, h * P:(h + 1) * P],
                                              v[:, m, h * R_V:(h + 1) * R_V], start=True, stop=True)
                    mm.then_inc(s_up, 1)
                pe.wait_ge(s_msk, m + 1)
                if m >= 2:
                    pe.wait_ge(s_raw, R_HEADS * (m - 1))
                if m:
                    pe.wait_ge(s_st, R_HEADS * m)
                for h in range(R_HEADS):
                    o = t.bank[2 + 2 * (m % 2) + h // 2][:, (h % 2) * R_V:(h % 2 + 1) * R_V]
                    mm = nc.tensor.matmul(o, s[:, m % 2, h, :], v[:, m, h * R_V:(h + 1) * R_V], start=True, stop=m == 0)
                    if m:
                        mm = nc.tensor.matmul(o, qt[:, h, m * P:(m + 1) * P], state[:, (m - 1) % 2, h, :], start=False, stop=True)
                mm.then_inc(s_y, 1)

        @block.scalar
        def _(act):
            for m in range(NT):
                act.wait_ge(s_y, m + 1)
                for h in range(R_HEADS):
                    o = t.bank[2 + 2 * (m % 2) + h // 2][:, (h % 2) * R_V:(h % 2 + 1) * R_V]
                    nc.scalar.activation(yraw[:, m, h * R_V:(h + 1) * R_V], o, ACT.Copy,
                                         scale=t.l0c[:, L0_QDEC + h:L0_QDEC + h + 1]).then_inc(s_raw, 1)
            act.wait_ge(s_ms, NT * R_HEADS)
            nc.scalar.activation(ss[:, :, :], ss[:, :, :], ACT.Sqrt, bias=t.eps[:, 0:1]).then_inc(s_rs, 1)

        @block.vector
        def _(dve):
            table = t.l0c[:, L0_RET:L0_RET + R_HEADS * P].rearrange("p (h n) -> p h n", h=R_HEADS)

            def squares(m):
                dve.wait_ge(s_raw, R_HEADS * (m + 1))
                for h in range(R_HEADS):
                    hs = slice(h * R_V, (h + 1) * R_V)
                    nc.vector.tensor_tensor_reduce(y[:, m, hs], yraw[:, m, hs], yraw[:, m, hs], 1.0 / R_V, 0.0, ALU.mult, ALU.add,
                                                   ss[:, m, h:h + 1]).then_inc(s_ms, 1)

            def norm(m):
                for h in range(R_HEADS):
                    hs = slice(h * R_V, (h + 1) * R_V)
                    nc.vector.scalar_tensor_tensor(out=y[:, m, hs], in0=yraw[:, m, hs], scalar=ss[:, m, h:h + 1],
                                                   in1=g[:, m, hs], op0=ALU.mult, op1=ALU.mult)

            for m in range(NT):
                dve.wait_ge(s_qk, m + 1)
                if m >= 2:
                    dve.wait_ge(s_y, m - 1)
                nc.vector.tensor_tensor(s[:, m % 2], t.bank[m % 2][:, :].rearrange("p (h n) -> p h n", h=R_HEADS), table,
                                        ALU.mult).then_inc(s_msk, 1)
                if m + 1 < NT:
                    dve.wait_ge(s_up, m + 1)
                    if m:
                        dve.wait_ge(s_st, R_HEADS * m)
                    if m >= 2:
                        dve.wait_ge(s_y, m)
                    for h in range(R_HEADS):
                        up = t.bank[6 + h // 2][:, (h % 2) * R_V:(h % 2 + 1) * R_V]
                        if m:
                            ins = nc.vector.scalar_tensor_tensor(out=state[:, m % 2, h, :], in0=state[:, (m - 1) % 2, h, :],
                                                                 scalar=gamma[h] ** P, in1=up, op0=ALU.mult, op1=ALU.add)
                        else:
                            ins = nc.vector.tensor_copy(state[:, m % 2, h, :], up)
                        ins.then_inc(s_st, 1)
                if m:
                    squares(m - 1)
            squares(NT - 1)
            dve.wait_ge(s_rs, 1)
            nc.vector.reciprocal(ss[:, :, :], ss[:, :, :]).then_inc(s_rs, 1)
            dve.wait_ge(s_rs, 2)
            for m in range(NT):
                norm(m)


def ssd_phase(t, xc, xs, bt, z, dt, a_dt, nacum, ecum, e, xdt, xde, state, decayed, y1, y):
    nc = t.nc
    steps = [(m, gr) for m in range(NT) for gr in range(S_GROUPS)]
    w = S_HPG * S_HD
    nh = NT * S_HEADS
    with ExitStack() as c:
        s_seg = t.semaphore("ssd_segments")
        s_e = t.semaphore("ssd_decays")
        s_cb = t.semaphore("ssd_scores")
        s_m = t.semaphore("ssd_masked")
        s_x = t.semaphore("ssd_x")
        s_off = t.semaphore("ssd_state_read")
        s_y = t.semaphore("ssd_y")
        s_h = t.semaphore("ssd_state")
        s_t = t.semaphore("ssd_y_read")
        s_dve = t.semaphore("ssd_dve")
        s_pool = t.semaphore("ssd_pool")
        s_skip = t.semaphore("ssd_skip")
        s_ms = t.semaphore("ssd_ms")
        s_rs = t.semaphore("ssd_rs")
        ss = c.enter_context(nc.sbuf_tensor("ssd_ss", [P, len(steps)], F32))
        block = c.enter_context(nc.Block())

        @block.tensor
        def _(pe):
            def front(u):
                m, gr = steps[u]
                if u:
                    pe.wait_ge(s_e, S_HPG * u)
                for i in range(2):
                    nc.tensor.matmul(t.bank[i][:, :].rearrange("p (h n) -> p h n", h=4), t.ident,
                                     wide(t.common[:, C_NEG:C_NEG + P].unsqueeze(1), P, 4, P), start=True, stop=False)
                    for j in range(4):
                        col = m * S_HEADS + gr * S_HPG + 4 * i + j
                        mm = nc.tensor.matmul(t.bank[i][:, j * P:(j + 1) * P], wide(a_dt[:, col:col + 1], P, P),
                                              t.common[:, C_UPTO:C_UPTO + P], start=False, stop=j == 3)
                mm.then_inc(s_seg, 1)
                if u:
                    pe.wait_ge(s_m, u)
                ms = slice(m * P, (m + 1) * P)
                nc.tensor.matmul(t.bank[2][:, 0:P], xc[:, KD + gr, ms], xc[:, KD + S_GROUPS + gr, ms],
                                 start=True, stop=True).then_inc(s_cb, 1)

            front(0)
            for u, (m, gr) in enumerate(steps):
                ms = slice(m * P, (m + 1) * P)
                if u >= 2:
                    pe.wait_ge(s_t, u - 1)
                if m:
                    pe.wait_ge(s_h, u - 1)
                    nc.tensor.matmul(t.bank[3 + u % 2][:, :], xc[:, KD + S_GROUPS + gr, ms], state[:, gr, :],
                                     start=True, stop=True).then_inc(s_off, 1)
                pe.wait_ge(s_x, u + 1)
                if m + 1 < NT:
                    if u:
                        pe.wait_ge(s_h, u)
                    nc.tensor.matmul(t.bank[7][:, :], bt[:, m, gr * P:(gr + 1) * P], xde[:, u % 2, :], start=True, stop=True)
                if u + 1 < len(steps):
                    front(u + 1)
                pe.wait_ge(s_m, u + 1)
                for h in range(S_HPG):
                    mm = nc.tensor.matmul(t.bank[5 + u % 2][:, h * S_HD:(h + 1) * S_HD], e[:, u % 2, h, :],
                                          xdt[:, u % 2, h * S_HD:(h + 1) * S_HD], start=True, stop=True)
                mm.then_inc(s_y, 1)

        @block.scalar
        def _(act):
            for u, (m, gr) in enumerate(steps):
                act.wait_ge(s_seg, u + 1)
                if u >= 2:
                    act.wait_ge(s_y, u - 1)
                for h in range(S_HPG):
                    col = m * S_HEADS + gr * S_HPG + h
                    nc.scalar.activation(e[:, u % 2, h, :], t.bank[h // 4][:, (h % 4) * P:(h % 4 + 1) * P], ACT.Exp,
                                         bias=nacum[:, col:col + 1]).then_inc(s_e, 1)
            act.wait_ge(s_ms, len(steps))
            nc.scalar.activation(ss[:, :], ss[:, :], ACT.Sqrt, bias=t.eps[:, 1:2]).then_inc(s_rs, 1)

        @block.gpsimd
        def _(pool):
            ch = Chain(pool, s_pool)

            for u, (m, gr) in enumerate(steps):
                c0 = m * S_HEADS + gr * S_HPG
                x = xs[:, m, gr * w:(gr + 1) * w].rearrange("p (h d) -> p h d", h=S_HPG)
                xd = xdt[:, u % 2, :].rearrange("p (h d) -> p h d", h=S_HPG)
                xe = xde[:, u % 2, :].rearrange("p (h d) -> p h d", h=S_HPG)
                if u >= 2:
                    pool.wait_ge(s_y, u - 1)
                dts = dt[:, m, gr * S_HPG:(gr + 1) * S_HPG]
                ch.link(nc.gpsimd.tensor_tensor(xd, x, wide(dts.unsqueeze(2), P, S_HPG, S_HD), ALU.mult))
                if m:
                    pool.wait_ge(s_h, u - 1)
                    ch.add(nc.gpsimd.tensor_tensor(decayed[:, gr, :].rearrange("p (h d) -> p h d", h=S_HPG),
                                                   state[:, gr, :].rearrange("p (h d) -> p h d", h=S_HPG),
                                                   wide(ecum[:, nh + c0:nh + c0 + S_HPG].unsqueeze(2), P, S_HPG, S_HD), ALU.mult))
                ch.wait()
                nc.gpsimd.tensor_tensor(xe, xd, wide(ecum[:, 2 * nh + c0:2 * nh + c0 + S_HPG].unsqueeze(2), P, S_HPG, S_HD),
                                        ALU.mult).then_inc(s_x, 1)
                nc.gpsimd.tensor_tensor(x, x, wide(t.row("dskip")[:, gr * S_HPG:(gr + 1) * S_HPG].unsqueeze(2), P, S_HPG, S_HD),
                                        ALU.mult).then_inc(s_skip, 1)


        @block.vector
        def _(dve):
            ch = Chain(dve, s_dve)

            def tail(u):
                m, gr = steps[u]
                c0 = m * S_HEADS + gr * S_HPG
                gs = slice(gr * w, (gr + 1) * w)
                yy = y1[:, u % 2, :]
                dve.wait_ge(s_y, u + 1)
                if m + 1 < NT:
                    if m:
                        nc.vector.tensor_tensor(state[:, gr, :], decayed[:, gr, :], t.bank[7][:, :], ALU.add).then_inc(s_h, 1)
                    else:
                        nc.vector.tensor_copy(state[:, gr, :], t.bank[7][:, :]).then_inc(s_h, 1)
                if m:
                    ch.link(nc.vector.tensor_tensor(yy.rearrange("p (h d) -> p h d", h=S_HPG),
                                                    t.bank[3 + u % 2][:, :].rearrange("p (h d) -> p h d", h=S_HPG),
                                                    wide(ecum[:, c0:c0 + S_HPG].unsqueeze(2), P, S_HPG, S_HD), ALU.mult))
                    ch.link(nc.vector.tensor_tensor(yy, yy, xs[:, m, gs], ALU.add))
                    nc.vector.tensor_tensor(yy, yy, t.bank[5 + u % 2][:, :], ALU.add).then_inc(s_t, 1)
                else:
                    nc.vector.tensor_tensor(yy, xs[:, m, gs], t.bank[5 + u % 2][:, :], ALU.add).then_inc(s_t, 1)
                dve.wait_ge(s_t, u + 1)
                ch.link(nc.vector.tensor_tensor(y[:, m, gs], yy, z[:, m, gs], ALU.mult))
                nc.vector.tensor_tensor_reduce(yy, y[:, m, gs], y[:, m, gs], 1.0 / w, 0.0, ALU.mult, ALU.add,
                                               ss[:, u:u + 1]).then_inc(s_ms, 1)
                dve.wait_ge(s_ms, u + 1)

            for u in range(len(steps)):
                dve.wait_ge(s_e, S_HPG * (u + 1))
                dve.wait_ge(s_cb, u + 1)
                nc.vector.tensor_tensor(e[:, u % 2], e[:, u % 2], wide(t.bank[2][:, 0:P].unsqueeze(1), P, S_HPG, P),
                                        ALU.mult).then_inc(s_m, 1)
                dve.wait_ge(s_skip, u + 1)
                tail(u)
            dve.wait_ge(s_rs, 1)
            nc.vector.reciprocal(ss[:, :], ss[:, :]).then_inc(s_rs, 1)
            dve.wait_ge(s_rs, 2)
            for u, (m, gr) in enumerate(steps):
                gs = slice(gr * w, (gr + 1) * w)
                nc.vector.tensor_scalar(y[:, m, gs], y[:, m, gs], ss[:, u:u + 1], None, ALU.mult)


def proj_phase(t, tag, srcs, scales, mt, chunks, ring, w_sem):
    nc = t.nc
    n_half = len(srcs)
    with ExitStack() as c:
        s_tr = t.semaphore(f"{tag}_transposed")
        s_ev = t.semaphore(f"{tag}_evacuated")
        s_pe = t.semaphore(f"{tag}_group")
        s_add = t.semaphore(f"{tag}_added")
        s_use = t.semaphore(f"{tag}_chunk_used")
        block = c.enter_context(nc.Block())
        banks = n_half * KD

        @block.sync
        def _(sp):
            for n in range(len(chunks)):
                if n >= 2:
                    half, part = divmod(n - 2, n_half)
                    if part == n_half - 1:
                        sp.wait_ge(s_pe, NT * (half + 1))
                    else:
                        sp.wait_ge(s_use, half + 1)
                sp.dma_start(ring[n % 2], chunks[n]).then_inc(w_sem[n % 2], 16)

        @block.tensor
        def _(pe):
            for n in range(banks):
                if n >= 8:
                    pe.wait_ge(s_ev, n - 7)
                for m in range(NT):
                    mm = nc.tensor.transpose(t.bank[n % 8][:, m * P:(m + 1) * P], srcs[n // KD][:, m, (n % KD) * P:(n % KD + 1) * P], t.ident)
                mm.then_inc(s_tr, 1)
            pe.wait_ge(s_ev, banks)
            for n in range(len(chunks)):
                half, part = divmod(n, n_half)
                pe.wait_ge(w_sem[n % 2], 16 * (n // 2 + 1))
                for m in range(NT):
                    for kk in range(KD):
                        mm = nc.tensor.matmul(t.bank[4 * half + m][:, :], mt[:, part * KD + kk, m * P:(m + 1) * P],
                                              ring[n % 2][:, kk, :], start=part == 0 and kk == 0,
                                              stop=part == n_half - 1 and kk == KD - 1)
                    if part == n_half - 1:
                        mm.then_inc(s_pe, 1)
                    elif m == NT - 1:
                        mm.then_inc(s_use, 1)

        @block.scalar
        def _(act):
            for n in range(0, banks):
                act.wait_ge(s_tr, n + 1)
                sc = scales[n // KD]
                nc.scalar.activation(mt[:, n, :], t.bank[n % 8][:, :], ACT.Copy,
                                     scale=1.0 if sc is None else sc[:, n % KD:n % KD + 1]).then_inc(s_ev, 1)

        @block.vector
        def _(dve):
            for half in range(2):
                for m in range(NT):
                    dve.wait_ge(s_pe, NT * half + m + 1)
                    hs = t.h[:, m, half * HALF:(half + 1) * HALF]
                    nc.vector.tensor_tensor(hs, hs, t.bank[4 * half + m][:, :], ALU.add).then_inc(s_add, 1)


def first_max(nc, chain, onehot, x, mx, least, cand, iota):
    shape = [P, NT, x.shape[2]]
    chain.link(nc.vector.tensor_reduce(mx, x, AX.X, ALU.max))
    chain.link(nc.vector.tensor_tensor(cand, x, wide(mx.unsqueeze(2), *shape), ALU.is_equal))
    chain.link(nc.vector.scalar_tensor_tensor(out=cand, in0=cand, scalar=-8.0, in1=wide(iota.unsqueeze(1), *shape),
                                              op0=ALU.mult, op1=ALU.add))
    chain.link(nc.vector.tensor_reduce(least, cand, AX.X, ALU.min))
    chain.link(nc.vector.tensor_tensor(onehot, cand, wide(least.unsqueeze(2), *shape), ALU.is_equal))


def route_phase(t, layer, ut, xn, at):
    nc = t.nc
    NL = GROUPS + EXPERTS
    with ExitStack() as c:
        sem = lambda n: t.semaphore(f"route{layer}_{n}")
        s_lg, s_exp, s_dve, s_pick, s_rank, s_slot, s_put = (sem(n) for n in (
            "logits", "exp", "dve", "picked", "ranked", "slots", "scattered"))
        taken = [at]

        def sb(n, shape):
            v = views(t, taken[0], [(n, tuple(shape[1:]))])[n]
            taken[0] += int(np.prod(shape[1:]))
            return v

        wr = t.router[:, layer]
        lg = sb("logits", [P, NT, NL])
        oh_g, sel, sel2, cand = (sb(n, [P, NT, EPG]) for n in ("group", "sel", "sel2", "cand"))
        oh = [sb(f"first{j}", [P, NT, EPG]) for j in range(2)]
        mx = [sb(f"max{j}", [P, NT]) for j in range(3)]
        least, ex, den, gsum = (sb(n, [P, NT]) for n in ("least", "ex", "den", "gsum"))
        gexp = sb("gexp", [P, NT, GROUPS])
        pick = [sb(f"pick{j}", [P, NT, EXPERTS]) for j in range(3)]
        prod = sb("prod", [P, NT, EXPERTS])
        cnt, nb, incl, base = (sb(n, [P, EXPERTS]) for n in ("count", "blocks", "incl", "base"))
        pos = sb("pos", [P, NT, 2])
        table = sb("table", [P, MAX_BLOCKS, EXPERTS])
        ebf = sb("expert_of", [P, 1 + MAX_BLOCKS])
        even = sb("even", [P, MAX_BLOCKS // 2])
        block = c.enter_context(nc.Block())

        @block.tensor
        def _(pe):
            for m in range(NT):
                for k in range(KD):
                    mm = nc.tensor.matmul(t.bank[0][:, m * NL:(m + 1) * NL], ut[:, k, m * P:(m + 1) * P], wr[:, k, :],
                                          start=k == 0, stop=k == KD - 1)
            mm.then_inc(s_lg, 1)
            pe.wait_ge(s_pick, 1)
            before, ones = t.common[:, C_BEFORE:C_BEFORE + P], t.common[:, C_ONES:C_ONES + P]
            for m in range(NT + 1):
                o = t.bank[1][:, m * EXPERTS:(m + 1) * EXPERTS]
                n = min(m, NT)
                for j in range(n):
                    mm = nc.tensor.matmul(o, ones, pick[2][:, j, :], start=j == 0, stop=m == NT and j == n - 1)
                if m < NT:
                    mm = nc.tensor.matmul(o, before, pick[2][:, m, :], start=m == 0, stop=True)
            mm.then_inc(s_rank, 1)

        @block.scalar
        def _(act):
            act.wait_ge(s_exp, 1)
            nc.scalar.activation(gexp[:, :, :], gexp[:, :, :], ACT.Exp).then_inc(s_exp, 1)
            act.wait_ge(s_exp, 3)
            nc.scalar.activation(ex[:, :], ex[:, :], ACT.Exp).then_inc(s_exp, 1)

        @block.vector
        def _(dve):
            ch = Chain(dve, s_dve)
            iota = t.common[:, C_IOTA:C_IOTA + EPG]
            shape = [P, NT, EPG]
            dve.wait_ge(s_lg, 1)
            ch.link(nc.vector.tensor_tensor(lg[:, :, :], t.bank[0][:, 0:NT * NL].rearrange("p (m n) -> p m n", m=NT),
                                            wide(t.row(f"mb{layer}").unsqueeze(1), P, NT, NL), ALU.add))
            g = lg[:, :, 0:GROUPS]
            first_max(nc, ch, oh_g[:, :, :], g, mx[0][:, :], least[:, :], cand[:, :, :], iota)
            nc.vector.tensor_tensor(gexp[:, :, :], g, wide(mx[0][:, :].unsqueeze(2), *shape), ALU.subtract).then_inc(s_exp, 1)
            for gr in range(GROUPS):
                e = lg[:, :, GROUPS + gr * EPG:GROUPS + (gr + 1) * EPG]
                on = wide(oh_g[:, :, gr:gr + 1], *shape)
                if gr == 0:
                    ch.link(nc.vector.tensor_tensor(sel[:, :, :], e, on, ALU.mult))
                else:
                    ch.link(nc.vector.tensor_tensor(cand[:, :, :], e, on, ALU.mult))
                    ch.link(nc.vector.tensor_tensor(sel[:, :, :], sel[:, :, :], cand[:, :, :], ALU.add))
            first_max(nc, ch, oh[0][:, :, :], sel[:, :, :], mx[1][:, :], least[:, :], cand[:, :, :], iota)
            ch.link(nc.vector.scalar_tensor_tensor(out=sel2[:, :, :], in0=oh[0][:, :, :], scalar=-3e38, in1=sel[:, :, :],
                                                   op0=ALU.mult, op1=ALU.add))
            first_max(nc, ch, oh[1][:, :, :], sel2[:, :, :], mx[2][:, :], least[:, :], cand[:, :, :], iota)
            dve.wait_ge(s_exp, 2)
            nc.vector.tensor_tensor(ex[:, :], mx[2][:, :], mx[1][:, :], ALU.subtract).then_inc(s_exp, 1)
            for j in range(2):
                for gr in range(GROUPS):
                    ch.add(nc.vector.tensor_tensor(pick[j][:, :, gr * EPG:(gr + 1) * EPG], oh[j][:, :, :],
                                                   wide(oh_g[:, :, gr:gr + 1], *shape), ALU.mult))
            ch.wait()
            nc.vector.tensor_tensor(pick[2][:, :, :], pick[0][:, :, :], pick[1][:, :, :], ALU.add).then_inc(s_pick, 1)
            ch.link(nc.vector.tensor_reduce(gsum[:, :], gexp[:, :, :], AX.X, ALU.add))
            dve.wait_ge(s_exp, 4)
            ch.link(nc.vector.tensor_scalar(den[:, :], ex[:, :], 1.0, None, ALU.add))
            ch.link(nc.vector.tensor_tensor(den[:, :], den[:, :], gsum[:, :], ALU.mult))
            ch.link(nc.vector.reciprocal(t.weight[:, :, 0], den[:, :]))
            ch.link(nc.vector.tensor_tensor(t.weight[:, :, 1], t.weight[:, :, 0], ex[:, :], ALU.mult))
            dve.wait_ge(s_rank, 1)
            ch.link(nc.vector.tensor_copy(cnt[:, :], t.bank[1][:, NT * EXPERTS:(NT + 1) * EXPERTS]))
            ch.link(nc.vector.tensor_scalar(nb[:, :], cnt[:, :], 0.0, None, ALU.is_gt))
            for j in range(1, SEQ // SLOTS):
                ch.link(nc.vector.scalar_tensor_tensor(out=nb[:, :], in0=cnt[:, :], scalar=float(j * SLOTS), in1=nb[:, :],
                                                       op0=ALU.is_gt, op1=ALU.add))
            ch.link(nc.vector.tensor_tensor_scan(incl[:, :], t.common[:, C_ONES:C_ONES + EXPERTS], nb[:, :], 0.0, ALU.mult, ALU.add))
            ch.link(nc.vector.tensor_tensor(base[:, :], incl[:, :], nb[:, :], ALU.subtract))
            ch.link(nc.vector.tensor_scalar(base[:, :], base[:, :], float(SLOTS), None, ALU.mult))
            ch.link(nc.vector.tensor_tensor(prod[:, :, :], t.bank[1][:, 0:NT * EXPERTS].rearrange("p (m e) -> p m e", m=NT),
                                            wide(base[:, :].unsqueeze(1), P, NT, EXPERTS), ALU.add))
            for j in range(2):
                ch.link(nc.vector.tensor_tensor(pick[j][:, :, :], pick[j][:, :, :], prod[:, :, :], ALU.mult))
                ch.link(nc.vector.tensor_reduce(pos[:, :, j], pick[j][:, :, :], AX.X, ALU.add))
            nc.vector.tensor_copy(t.slot[:, :, :], pos[:, :, :]).then_inc(s_slot, 1)
            ch.link(nc.vector.tensor_tensor(table[:, :, :], wide(t.common[:, C_BLK:C_BLK + MAX_BLOCKS].unsqueeze(2), P, MAX_BLOCKS, EXPERTS),
                                            wide(incl[:, :].unsqueeze(1), P, MAX_BLOCKS, EXPERTS), ALU.is_ge))
            ch.link(nc.vector.tensor_reduce(ebf[:, 1:], table[:, :, :], AX.X, ALU.add))
            ch.link(nc.vector.tensor_scalar(ebf[:, 1:], ebf[:, 1:], float(EXPERTS - 1), None, ALU.min))
            ch.link(nc.vector.tensor_scalar(even[:, :], t.common[:, C_BLK:C_BLK + MAX_BLOCKS].rearrange("p (b two) -> p b two", two=2)[:, :, 0],
                                            incl[:, EXPERTS - 1:EXPERTS], None, ALU.is_lt))
            ch.link(nc.vector.tensor_reduce(ebf[:, 0:1], even[:, :], AX.X, ALU.add))
            nc.vector.tensor_copy(t.meta[:, :], ebf[0:1, :])

        @block.gpsimd
        def _(pool):
            pool.wait_ge(t.s_clear, 16 * (MAX_BLOCKS + 2))
            pool.wait_ge(s_slot, 1)
            for m in range(NT):
                for j in range(2):
                    nc.gpsimd.indirect_dma_start(out=t.xg[:, :], out_offset=bass.IndirectOffsetOnAxis(ap=t.slot[:, m, j:j + 1], axis=0),
                                                 in_=xn[:, m, :], in_offset=None).then_inc(s_put, 16)
            pool.wait_ge(s_put, 16 * 2 * NT)


def experts_phase(t, layer, w_col, b, w1, w3, w2, s_w13, s_w2):
    nc = t.nc
    XT, Y = ((1, 2), (5, 6)), ((3, 4), (7, 1))
    with ExitStack() as c:
        sem = lambda n: t.semaphore(f"moe{layer}_{n}")
        s_x = [sem(f"x_loaded{i}") for i in range(2)]
        s_xt, s_xte = sem("x_transposed"), sem("x_evacuated")
        s_h, s_silu, s_u = sem("hidden"), sem("silu"), sem("gated")
        s_ht, s_hte = sem("gated_transposed"), sem("gated_evacuated")
        s_y, s_ye = sem("y"), sem("y_evacuated")
        s_st = [sem(f"y_stored{i}") for i in range(2)]
        s_yfree = sem("y_free")
        block = c.enter_context(nc.Block())
        bank = t.bank

        def pairs(engine):
            return engine.value_load(t.meta[0:1, 0:1], min_val=1, max_val=MAX_BLOCKS // 2)

        @block.sync
        def _(sp):
            n = pairs(sp)
            for s in range(2):
                sp.dma_start(b["x"][:, s, :], t.xg[s * SLOTS:(s + 1) * SLOTS, :]).then_inc(s_x[s], 16)
            sp.wait_ge(s_w13[0], 32)
            sp.wait_ge(s_w13[1], 32)
            sp.wait_ge(s_w2[0], 16)
            sp.wait_ge(s_w2[1], 16)
            with sp.Fori(0, n) as i:
                e = [sp.value_load(t.meta[0:1, bass.ds(i * 2 + s + 1, 1)], min_val=0, max_val=EXPERTS - 1) for s in range(2)]
                other = [(e[s] + EXPERTS * i) != s for s in range(2)]
                row = [sp.snap((i * 2 + 2 + s) * SLOTS) for s in range(2)]
                for s in range(2):
                    sp.wait_ge(s_h, 4 * i + 2 * s + 2)
                    for w, name in ((w1, "w1"), (w3, "w3")):
                        sp.dma_start(b[name][:, s], w[bass.ds(e[s], 1)].rearrange("o (k p) n -> p (o k) n", p=P),
                                     cond=other[s]).then_inc(s_w13[s], 16)
                    sp.wait_ge(s_xt, 4 * i + 2 * s + 2)
                    sp.dma_start(b["x"][:, s, :], t.xg[bass.ds(row[s], SLOTS), :]).then_inc(s_x[s], 16)
                for s in range(2):
                    sp.wait_ge(s_y, 4 * i + 2 * s + 2)
                    sp.dma_start(b["w2"][:, s], w2[bass.ds(e[s], 1)].rearrange("o (k p) n -> p (o k) n", p=P),
                                 cond=other[s]).then_inc(s_w2[s], 16)

        @block.tensor
        def _(pe):
            n = pairs(pe)
            pe.sem_inc(s_h, 4)
            pe.sem_inc(s_y, 4)

            def x_transposes(s):
                for k in range(KD):
                    mm = nc.tensor.transpose(bank[XT[s][k // 4]][:, (k % 4) * P:(k % 4 + 1) * P], b["x"][:, s, k * P:(k + 1) * P], t.ident)
                    if k % 4 == 3:
                        mm.then_inc(s_xt, 1)

            for s in range(2):
                pe.wait_ge(s_x[s], 16)
                x_transposes(s)
            with pe.Fori(0, n) as i:
                for s in range(2):
                    pe.wait_ge(s_w13[s], 32 * i + 64)
                    pe.wait_ge(s_xte, 4 * i + 4)
                    pe.wait_ge(s_ye, 4 * i + 2 + s)
                    for j, name in enumerate(("w1", "w3")):
                        for k in range(KD):
                            mm = nc.tensor.matmul(bank[4 + 2 * s + j][:, :], b["xt"][:, s, k, :], b[name][:, s, k, :],
                                                  start=k == 0, stop=k == KD - 1)
                        mm.then_inc(s_h, 1)
                for s in range(2):
                    pe.wait_ge(s_u, 2 * i + s + 1)
                    for k in range(FF // P):
                        mm = nc.tensor.transpose(bank[0][:, k * P:(k + 1) * P], b["u"][:, s, k * P:(k + 1) * P], t.ident)
                    mm.then_inc(s_ht, 1)
                    pe.wait_ge(s_x[s], 16 * i + 32)
                    if s == 0:
                        pe.wait_ge(s_ye, 4 * i + 4)
                    x_transposes(s)
                    pe.wait_ge(s_w2[s], 16 * i + 32)
                    pe.wait_ge(s_hte, 2 * i + s + 1)
                    if s:
                        pe.wait_ge(s_xte, 4 * i + 6)
                    for j in range(2):
                        for k in range(FF // P):
                            mm = nc.tensor.matmul(bank[Y[s][j]][:, :], b["ht"][:, s, k, :], b["w2"][:, s, k, j * HALF:(j + 1) * HALF],
                                                  start=k == 0, stop=k == FF // P - 1)
                        mm.then_inc(s_y, 1)

        @block.vector
        def _(dve):
            n = pairs(dve)

            def x_evacuation(s, j):
                nc.vector.tensor_tensor(b["xt"][:, s, 4 * j:4 * j + 4, :], bank[XT[s][j]][:, :].rearrange("p (k n) -> p k n", k=4),
                                        wide(w_col[:, 4 * j:4 * j + 4].unsqueeze(2), P, 4, P), ALU.mult).then_inc(s_xte, 1)

            for s in range(2):
                for j in range(2):
                    dve.wait_ge(s_xt, 2 * s + j + 1)
                    x_evacuation(s, j)
            with dve.Fori(0, n) as i:
                for s in range(2):
                    dve.wait_ge(s_h, 4 + 4 * i + 2 * s + 2)
                    dve.wait_ge(s_silu, 2 * i + s + 1)
                    nc.vector.tensor_tensor(b["u"][:, s, :], b["u"][:, s, :], bank[5 + 2 * s][:, :], ALU.mult).then_inc(s_u, 1)
                for s in range(2):
                    for j in range(2):
                        dve.wait_ge(s_xt, 4 * i + 4 + 2 * s + j + 1)
                        x_evacuation(s, j)

        @block.scalar
        def _(act):
            n = pairs(act)
            act.sem_inc(s_ye, 4)
            with act.Fori(0, n) as i:
                for s in range(2):
                    act.wait_ge(s_h, 4 + 4 * i + 2 * s + 1)
                    nc.scalar.activation(b["u"][:, s, :], bank[4 + 2 * s][:, :], ACT.Silu).then_inc(s_silu, 1)
                for s in range(2):
                    act.wait_ge(s_ht, 2 * i + s + 1)
                    nc.scalar.activation(b["ht"][:, s].rearrange("p k n -> p (k n)"), bank[0][:, :], ACT.Copy).then_inc(s_hte, 1)
                    act.wait_ge(s_yfree, 2 * i + s + 1)
                    for j in range(2):
                        act.wait_ge(s_y, 4 + 4 * i + 2 * s + j + 1)
                        nc.scalar.activation(b["y"][:, s, j * HALF:(j + 1) * HALF], bank[Y[s][j]][:, :], ACT.Copy).then_inc(s_ye, 1)

        @block.gpsimd
        def _(pool):
            n = pairs(pool)
            pool.sem_inc(s_yfree, 2)
            with pool.Fori(0, n) as i:
                for s in range(2):
                    pool.wait_ge(s_ye, 4 + 4 * i + 2 * s + 2)
                    pool.dma_start(t.xg[bass.ds(i * 2 * SLOTS + s * SLOTS, SLOTS), :], b["y"][:, s, :]).then_inc(s_st[s], 16)
                    pool.wait_ge(s_st[s], 16 * i + 16)
                    pool.sem_inc(s_yfree, 1)


def combine_phase(t, layer, y):
    nc = t.nc
    with ExitStack() as c:
        s_y = [t.semaphore(f"combine{layer}_row{i}") for i in range(4)]
        s_add = t.semaphore(f"combine{layer}_added")
        block = c.enter_context(nc.Block())
        steps = [(m, j) for m in range(NT) for j in range(2)]

        @block.gpsimd
        def _(pool):
            for n, (m, j) in enumerate(steps):
                if n >= 4:
                    pool.wait_ge(s_y[n % 4], 16)
                nc.gpsimd.indirect_dma_start(out=y[:, n, :], out_offset=None, in_=t.xg[:, :],
                                             in_offset=bass.IndirectOffsetOnAxis(ap=t.slot[:, m, j:j + 1], axis=0)).then_inc(s_y[n % 4], 16)

        @block.vector
        def _(dve):
            for n, (m, j) in enumerate(steps):
                dve.wait_ge(s_y[n % 4], 16 * (n // 4 + 1))
                if j:
                    dve.wait_ge(s_add, n)
                nc.vector.scalar_tensor_tensor(out=t.h[:, m, :], in0=y[:, n, :], scalar=t.weight[:, m, j:j + 1], in1=t.h[:, m, :],
                                               op0=ALU.mult, op1=ALU.add).then_inc(s_add, 1)


def moe(t, a, layer):
    at = 3 * (2 * KD * HALF)
    A = views(t, at, [("ut", (KD, SEQ)), ("xn", (NT, D))])
    w_col = t.col(f"ffn{layer}")
    b = views(t, 0, [("w1", (2, KD, FF)), ("w3", (2, KD, FF)), ("w2", (2, FF // P, D)), ("x", (2, D)), ("xt", (2, KD, P)),
                     ("u", (2, FF)), ("ht", (2, FF // P, P)), ("y", (2, D))])
    s_w13 = [t.semaphore(f"moe{layer}_w13_loaded{i}") for i in range(2)]
    s_w2 = [t.semaphore(f"moe{layer}_w2_loaded{i}") for i in range(2)]
    w1, w3, w2 = (a[n][layer] for n in ("moe_w1", "moe_w3", "moe_w2"))

    def first_weights(sp):
        for s in range(2):
            for w, name, sem in ((w1, "w1", s_w13), (w3, "w3", s_w13), (w2, "w2", s_w2)):
                sp.dma_start(b[name][:, s], w[s].rearrange("(k p) n -> p k n", p=P)).then_inc(sem[s], 16)

    norm_phase(t, f"ffn{layer}", w_col, A["xn"], A["ut"], prefetch=first_weights)
    route_phase(t, layer, A["ut"], A["xn"], at + KD * SEQ + NT * D)
    experts_phase(t, layer, w_col, b, w1, w3, w2, s_w13, s_w2)
    combine_phase(t, layer, views(t, 0, [("y", (2 * NT, D))])["y"])


def rwkv_proj_phase(t, a, ut, xj, sg, lora, sigma, ag, r, k, v, g, kkn, sq, root, tmp, keep):
    nc = t.nc
    W1, A1, W2, A2, R0, G1, K0_, V0_, G2 = 0, 1, 2, 10, 18, 26, 28, 36, 44
    order = (1, 4, 0, 5, 2, 3)
    last_use = (W1, A1, R0 + 7, G1 + 1)
    GB = G_LORA - P
    MID = P // 2 - 1
    BANKS, SUM, BONUS = 6, 6, 7
    flat = [t.ring[i].rearrange("p k n -> p (k n)") for i in range(2)]
    with ExitStack() as c:
        sem = lambda n: t.semaphore(f"rw_{n}")
        s_w = [sem(f"weights{i}") for i in range(2)]
        s_xj, s_pe, s_ev, s_one, s_dve = sem("mix"), sem("group"), sem("evacuated"), sem("one_minus_mu"), sem("proj_dve")
        s_sq, s_sum, s_max, s_root, s_inv = (sem(n) for n in ("key_squares", "key_sums", "key_floored", "key_roots", "key_inverse"))
        s_d, s_p, s_k2, s_bon, s_out, s_pool, s_ends, s_rk = (sem(n) for n in (
            "decay_sums", "decay_exps", "decayed_by_dve", "bonus", "decayed_by_pool", "pool", "ends", "rk"))
        block = c.enter_context(nc.Block())
        mu = t.col("mu")
        ones = t.common[:, C_ONES:C_ONES + P]

        @block.sync
        def _(sp):
            def lora_weights(slot, first, second):
                sp.dma_start(flat[slot][:, 0:KD * W_LORA].rearrange("p (k n) -> p k n", k=KD),
                             a[first][0].rearrange("(k p) n -> p k n", p=P)).then_inc(s_w[slot], 16)
                sp.dma_start(flat[slot][0:W_LORA, KD * W_LORA:KD * W_LORA + D], a[second][0]).then_inc(s_w[slot], 16)

            def half_of(name, half, slot):
                sp.dma_start(t.ring[slot][:, :, :], a[name][0].rearrange("(k p) n -> p k n", p=P)[:, :, half * HALF:(half + 1) * HALF]
                             ).then_inc(s_w[slot], 16)

            lora_weights(0, "rw_w1", "rw_w2")
            lora_weights(1, "rw_a1", "rw_a2")
            sp.wait_ge(s_pe, W2 + 8)
            half_of("rw_wr", 0, 0)
            sp.wait_ge(s_pe, A2 + 8)
            half_of("rw_wr", 1, 1)
            sp.wait_ge(s_pe, R0 + 4)
            sp.dma_start(flat[0][:, 0:KD * G_LORA].rearrange("p (k n) -> p k n", k=KD), a["rw_g1"][0].rearrange("(k p) n -> p k n", p=P)
                         ).then_inc(s_w[0], 16)
            for name, half, slot, done in (("rw_wk", 0, 1, R0 + 8), ("rw_wk", 1, 0, G1 + 2), ("rw_wv", 0, 1, K0_ + 4), ("rw_wv", 1, 0, K0_ + 8)):
                sp.wait_ge(s_pe, done)
                half_of(name, half, slot)
            sp.wait_ge(s_pe, V0_ + 4)
            sp.dma_start(flat[1][:, 0:D], a["rw_g2"][0, 0:P, :]).then_inc(s_w[1], 16)
            sp.dma_start(flat[1][0:GB, D:2 * D], a["rw_g2"][0, P:G_LORA, :]).then_inc(s_w[1], 16)

        @block.tensor
        def _(pe):
            def group(i, rows, pairs):
                if i >= BANKS:
                    pe.wait_ge(s_ev, i - BANKS + 1)
                for n, (left, right) in enumerate(pairs):
                    mm = nc.tensor.matmul(t.bank[i % BANKS][0:rows, :], left, right, start=n == 0, stop=n == len(pairs) - 1)
                mm.then_inc(s_pe, 1)

            def key_sums(b):
                pe.wait_ge(s_sq, b + 1)
                if b:
                    pe.wait_ge(s_max, b)
                nc.tensor.matmul(t.bank[SUM][:, :], t.common[:, C_SAME:C_SAME + P], sq[:, b % 2, :], start=True, stop=True).then_inc(s_sum, 1)

            def bonus(b):
                pe.wait_ge(s_rk, b + 1)
                for m in range(NT):
                    mm = nc.tensor.matmul(t.bank[BONUS][:, m * W_HEADS + 2 * b:m * W_HEADS + 2 * b + 2], tmp["x"][:, b % 2, m * P:(m + 1) * P],
                                          t.common[:, C_HALF:C_HALF + 2], start=True, stop=True)
                mm.then_inc(s_bon, 1)

            for j, i in enumerate((W1, A1)):
                pe.wait_ge(s_w[j], 32)
                pe.wait_ge(s_xj, KD * (j + 1))
                group(i, W_LORA, [(flat[j][:, k_ * W_LORA:(k_ + 1) * W_LORA], xj[j][:, k_, :]) for k_ in range(KD)])
            for j, i0 in enumerate((W2, A2)):
                pe.wait_ge(s_ev, j + 1)
                for b in range(KD):
                    o = KD * W_LORA + b * P
                    group(i0 + b, P, [(flat[j][0:W_LORA, o:o + P], lora[j][0:W_LORA, :])])
            pe.wait_ge(s_xj, KD * 3)
            for b in range(KD):
                if b % 4 == 0:
                    pe.wait_ge(s_w[b // 4], 48)
                group(R0 + b, P, [(t.ring[b // 4][:, k_, (b % 4) * P:(b % 4 + 1) * P], xj[0][:, k_, :]) for k_ in range(KD)])
            pe.wait_ge(s_xj, KD * 4)
            pe.wait_ge(s_w[0], 64)
            for j, (c0, rows) in enumerate(((0, P), (P, GB))):
                group(G1 + j, rows, [(flat[0][:, k_ * G_LORA + c0:k_ * G_LORA + c0 + rows], xj[1][:, k_, :]) for k_ in range(KD)])
            pe.wait_ge(s_xj, KD * 5)
            for b in range(KD):
                slot = 1 - b // 4
                if b % 4 == 0:
                    pe.wait_ge(s_w[slot], 64 if slot else 80)
                group(K0_ + b, P, [(t.ring[slot][:, k_, (b % 4) * P:(b % 4 + 1) * P], xj[0][:, k_, :]) for k_ in range(KD)])
                if b:
                    key_sums(b - 1)
            pe.wait_ge(s_xj, KD * 6)
            for n in range(2 * NT):
                half, m = divmod(n, NT)
                slot = 1 - half
                if m == 0:
                    pe.wait_ge(s_w[slot], 80 if slot else 96)
                group(V0_ + n, P, [(xj[1][:, k_, m * P:(m + 1) * P], t.ring[slot][:, k_, :]) for k_ in range(KD)])
                if n == 0:
                    key_sums(KD - 1)
                if n >= 2:
                    bonus(n - 2)
            pe.wait_ge(s_w[1], 112)
            for n in range(2 * NT):
                m, half = divmod(n, 2)
                ms = slice(m * P, (m + 1) * P)
                o = half * HALF
                group(G2 + n, P, [(sg[:, 0, ms], flat[1][:, o:o + HALF]), (sg[0:GB, 1, ms], flat[1][0:GB, o + D:o + D + HALF])])
                if n == 4:
                    bonus(KD - 2)
            bonus(KD - 1)

        @block.scalar
        def _(act):
            def evacuate(i, dst, func, rows=P, bias=0.0):
                act.wait_ge(s_pe, i + 1)
                kw = {} if func is ACT.Copy else {"bias": bias}
                nc.scalar.activation(dst, t.bank[i % BANKS][0:rows, :], func, **kw).then_inc(s_ev, 1)

            def key_root(b):
                act.wait_ge(s_max, b + 1)
                nc.scalar.activation(root, root, ACT.Sqrt).then_inc(s_root, 1)

            for j, i in enumerate((W1, A1)):
                evacuate(i, lora[j][0:W_LORA, :], ACT.Copy if j else ACT.Tanh, W_LORA)
            for b in range(KD):
                evacuate(W2 + b, sigma[:, b, :], ACT.Sigmoid, bias=t.col("w0")[:, b:b + 1])
            for b in range(KD):
                evacuate(A2 + b, ag[:, b, :], ACT.Sigmoid, bias=t.col("a0")[:, b:b + 1])
            for b in range(KD):
                evacuate(R0 + b, r[:, b, :], ACT.Copy)
            evacuate(G1, sg[:, 0, :], ACT.Sigmoid)
            evacuate(G1 + 1, sg[0:GB, 1, :], ACT.Sigmoid, GB)
            for b in range(KD):
                evacuate(K0_ + b, k[:, b, :], ACT.Copy)
                act.wait_ge(s_ev, K0_ + b + 1)
                if b >= 2:
                    act.wait_ge(s_sum, b - 1)
                nc.scalar.activation(sq[:, b % 2, :], k[:, b, :], ACT.Square, scale=t.col("kk")[:, b:b + 1]).then_inc(s_sq, 1)
                if b:
                    key_root(b - 1)
            key_root(KD - 1)
            for b in range(KD):
                act.wait_ge(s_d, 2 * (b + 1))
                if b >= 2:
                    act.wait_ge(s_out, 2 * (b - 1))
                    act.wait_ge(s_k2, 2 * (b - 1))
                for name, src, sign in (("pinv", "d1", -1.0), ("pt", "d1", 1.0), ("pb", "d2", 1.0)):
                    nc.scalar.activation(tmp[name][:, b % 2], tmp[src][:, b % 2], ACT.Exp, scale=sign * LOG_DECAY).then_inc(s_p, 1)
                half, m = divmod(b, NT)
                evacuate(V0_ + b, v[:, m, half * HALF:(half + 1) * HALF], ACT.Copy)
            for name in ("mid", "end"):
                nc.scalar.activation(keep[name], keep[name], ACT.Exp, scale=LOG_DECAY).then_inc(s_ends, 1)
            for m in range(NT):
                for half in range(2):
                    evacuate(G2 + 2 * m + half, g[:, m, half * HALF:(half + 1) * HALF], ACT.Copy)

        @block.vector
        def _(dve):
            ch = Chain(dve, s_dve)
            one = keep["one_minus_mu"]
            nc.vector.tensor_scalar(one, mu, -1.0, 1.0, ALU.mult, ALU.add).then_inc(s_one, 1)
            dve.wait_ge(s_one, 1)
            for j, which in enumerate(order):
                if j >= 2:
                    dve.wait_ge(s_pe, last_use[j - 2] + 1)
                for b in range(KD):
                    col = which * KD + b
                    dst = xj[j % 2][:, b, :]
                    ch.add(nc.vector.tensor_scalar(dst, ut[:, b, :], one[:, col:col + 1], None, ALU.mult))
                ch.wait()
                for b in range(KD):
                    col = which * KD + b
                    dst = xj[j % 2][:, b, 1:]
                    nc.vector.scalar_tensor_tensor(out=dst, in0=ut[:, b, 0:SEQ - 1], scalar=mu[:, col:col + 1], in1=dst,
                                                   op0=ALU.mult, op1=ALU.add).then_inc(s_xj, 1)

            for b in range(KD):
                dve.wait_ge(s_sum, b + 1)
                nc.vector.tensor_scalar(root, t.bank[SUM][:, :], 1e-24, None, ALU.max).then_inc(s_max, 1)
                dve.wait_ge(s_root, b + 1)
                nc.vector.reciprocal(root, root).then_inc(s_inv, 1)
                dve.wait_ge(s_inv, 2 * b + 1)
                nc.vector.scalar_tensor_tensor(out=kkn[:, b, :], in0=k[:, b, :], scalar=t.col("kk")[:, b:b + 1], in1=root,
                                               op0=ALU.mult, op1=ALU.mult).then_inc(s_inv, 1)
                dve.wait_ge(s_inv, 2 * b + 2)

            def sums(b):
                cs, d1 = tmp["c"][:, b % 2], tmp["d1"][:, b % 2]
                if b >= 2:
                    dve.wait_ge(s_out, 2 * (b - 1))
                    dve.wait_ge(s_k2, 2 * (b - 1))
                for m in range(NT):
                    ch.add(nc.vector.tensor_tensor_scan(cs[:, m, :], ones, sigma[:, b, m * P:(m + 1) * P], 0.0, ALU.mult, ALU.add))
                ch.wait()
                ch.add(nc.vector.tensor_tensor(d1, cs, wide(cs[:, :, MID:MID + 1], P, NT, P), ALU.subtract))
                ch.add(nc.vector.tensor_copy(keep["mid"][:, b, :].unsqueeze(2), cs[:, :, MID:MID + 1]))
                ch.wait()
                nc.vector.tensor_copy(keep["end"][:, b, :].unsqueeze(2), d1[:, :, P - 1:P]).then_inc(s_d, 1)
                nc.vector.tensor_tensor(tmp["d2"][:, b % 2], d1, sigma[:, b, :].rearrange("p (m n) -> p m n", m=NT),
                                        ALU.subtract).then_inc(s_d, 1)

            def products(b):
                pinv, pb = (tmp[n][:, b % 2].rearrange("p m n -> p (m n)") for n in ("pinv", "pb"))
                k2, x = tmp["k2"][:, b % 2], tmp["x"][:, b % 2]
                if b >= 2:
                    dve.wait_ge(s_bon, b - 1)
                ch.link(nc.vector.tensor_scalar(k2, ag[:, b, :], 1.0, t.col("ka")[:, b:b + 1], ALU.subtract, ALU.mult))
                ch.link(nc.vector.scalar_tensor_tensor(out=k2, in0=k2, scalar=1.0, in1=k[:, b, :], op0=ALU.add, op1=ALU.mult))
                nc.vector.scalar_tensor_tensor(out=x, in0=r[:, b, :], scalar=t.col("rk")[:, b:b + 1], in1=k2, op0=ALU.mult,
                                               op1=ALU.mult).then_inc(s_rk, 1)
                dve.wait_ge(s_p, 3 * (b + 1))
                nc.vector.tensor_tensor(k[:, b, :], k2, pinv, ALU.mult).then_inc(s_k2, 1)
                dve.wait_ge(s_d, 2 * (b + 1))
                nc.vector.scalar_tensor_tensor(out=sigma[:, b, :], in0=kkn[:, b, :], scalar=-1.0, in1=pb, op0=ALU.mult,
                                               op1=ALU.mult).then_inc(s_k2, 1)

            for b in range(KD):
                sums(b)
                if b:
                    products(b - 1)
            products(KD - 1)
            dve.wait_ge(s_ends, 2)
            nc.vector.tensor_tensor(keep["factor"][:, :, 0:NT - 1], keep["end"][:, :, 0:NT - 1], keep["mid"][:, :, 1:NT], ALU.mult)
            dve.wait_ge(s_bon, KD)
            nc.vector.tensor_copy(keep["bonus"], t.bank[BONUS][:, 0:NT * W_HEADS])

        @block.gpsimd
        def _(pool):
            ch = Chain(pool, s_pool)
            for b in range(KD):
                pt, pinv = (tmp[n][:, b % 2].rearrange("p m n -> p (m n)") for n in ("pt", "pinv"))
                pool.wait_ge(s_p, 3 * (b + 1))
                pool.wait_ge(s_rk, b + 1)
                nc.gpsimd.tensor_tensor(r[:, b, :], r[:, b, :], pt, ALU.mult).then_inc(s_out, 1)
                ch.link(nc.gpsimd.tensor_tensor(ag[:, b, :], ag[:, b, :], kkn[:, b, :], ALU.mult))
                nc.gpsimd.tensor_tensor(ag[:, b, :], ag[:, b, :], pinv, ALU.mult).then_inc(s_out, 1)


def rwkv_rows_phase(t, a, ag, k, btok, ktok, l1c):
    nc = t.nc
    with ExitStack() as c:
        s_tr = t.semaphore("bk_transposed")
        s_ev = [t.semaphore(f"bk_evacuated{i}") for i in range(2)]
        s_tab = t.semaphore("bk_tables")
        block = c.enter_context(nc.Block())
        todo = [(src, dst, m, j) for src, dst in ((ag, btok), (k, ktok)) for m in range(NT) for j in range(2)]

        @block.tensor
        def _(pe):
            for n, (src, _, m, j) in enumerate(todo):
                if n >= 8:
                    pe.wait_ge(s_ev[n % 2], (n - 8) // 2 + 1)
                for i in range(4):
                    mm = nc.tensor.transpose(t.bank[n % 8][:, i * P:(i + 1) * P], src[:, 4 * j + i, m * P:(m + 1) * P], t.ident)
                mm.then_inc(s_tr, 1)

        @block.sync
        def _(sp):
            sp.dma_start(l1c, a["layer1"]).then_inc(s_tab, 16)
            sp.wait_ge(s_tab, 16)

        @block.scalar
        def _(act):
            for n, (_, dst, m, j) in enumerate(todo):
                if n % 2 == 0:
                    act.wait_ge(s_tr, n + 1)
                    nc.scalar.activation(dst[:, m, j * HALF:(j + 1) * HALF], t.bank[n % 8][:, :], ACT.Copy).then_inc(s_ev[0], 1)

        @block.vector
        def _(dve):
            for n, (_, dst, m, j) in enumerate(todo):
                if n % 2:
                    dve.wait_ge(s_tr, n + 1)
                    nc.vector.tensor_copy(dst[:, m, j * HALF:(j + 1) * HALF], t.bank[n % 8][:, :]).then_inc(s_ev[1], 1)


def rwkv_scan_phase(t, sigma, ag, r, k, v, btok, ktok, buf, state, keep, l1c):
    nc = t.nc
    steps = [(m, p) for m in range(NT) for p in range(2)]
    USES = (9, 9, 7, 7, 8, 8, 2, 2)
    TOP = LEVELS - 1
    L, RHS, SA = 0, TOP + 1, TOP + 2
    LT, Y = 0, TOP
    AK, UP = 0, TOP + 1

    def nth(bank, it, use):
        return it * USES[bank] + use + 1

    four = lambda ap: ap.rearrange("p (h n) -> p h n", h=4)
    with ExitStack() as c:
        sem = lambda n: t.semaphore(f"scan_{n}")
        full = [sem(f"full{i}") for i in range(8)]
        read = [sem(f"read{i}") for i in range(8)]
        s_t0, s_et, s_st, s_dve = sem("T_begun"), sem("E_masked"), sem("state"), sem("dve")
        block = c.enter_context(nc.Block())
        mask = lambda col: wide(t.common[:, col:col + P].unsqueeze(1), P, 4, P)
        low0 = wide(l1c[:, 0:P].unsqueeze(1), P, 4, P)
        up = lambda l: wide(l1c[:, (LEVELS + l) * P:(LEVELS + l + 1) * P].unsqueeze(1), P, 4, P)

        @block.tensor
        def _(pe):
            for it, (m, p) in enumerate(steps):
                ms = slice(m * P, (m + 1) * P)
                blocks = range(4 * p, 4 * p + 4)

                def take(bank, use):
                    n = nth(bank, it, use) - 1
                    if n:
                        pe.wait_ge(read[bank], n)

                def scores(bank, use, rr, left, right):
                    take(bank, use)
                    rows = slice(64 * rr, 64 * rr + 64)
                    for j, b in enumerate(blocks):
                        mm = nc.tensor.matmul(t.bank[bank][:, j * P:(j + 1) * P], left[rows, b, ms], right[rows, b, ms], start=True, stop=True)
                    mm.then_inc(full[bank], 1)

                for rr in range(2):
                    scores(rr, L, rr, sigma, ag)
                    scores(2 + rr, LT, rr, ag, sigma)
                    scores(4 + rr, AK, rr, k, sigma)
                    scores(6, rr, rr, ag, r)
                    scores(7, rr, rr, k, r)
                for l in range(1, TOP + 1):
                    for rr in range(2):
                        u = buf[rr]
                        if l == 1:
                            pe.wait_ge(s_t0, 4 * it + 2 * rr + 2)
                        else:
                            pe.wait_ge(read[2 + rr], nth(2 + rr, it, l - 1))
                        pe.wait_ge(s_et, 2 * TOP * it + 2 * (l - 1) + rr + 1)
                        take(rr, l)
                        for j in range(4):
                            mm = nc.tensor.matmul(t.bank[rr][:, j * P:(j + 1) * P], u["et"][:, l % 2, j], u["t"][:, j], start=True, stop=True)
                        mm.then_inc(full[rr], 1)
                        if l > 1:
                            take(4 + rr, l - 1)
                            for j in range(4):
                                mm = nc.tensor.transpose(t.bank[4 + rr][:, j * P:(j + 1) * P], u["t"][:, j], t.ident)
                            mm.then_inc(full[4 + rr], 1)
                    for rr in range(2):
                        u = buf[rr]
                        pe.wait_ge(read[rr], nth(rr, it, l))
                        take(4 + rr, l)
                        if l < TOP:
                            take(2 + rr, l)
                            for j in range(4):
                                mm = nc.tensor.matmul(t.bank[2 + rr][:, j * P:(j + 1) * P], u["tt"][:, j], u["x"][:, j], start=True, stop=True)
                            mm.then_inc(full[2 + rr], 1)
                        else:
                            for j in range(4):
                                mm = nc.tensor.matmul(t.bank[4 + rr][:, j * P:(j + 1) * P], u["x"][:, j], u["tt"][:, j], start=True, stop=True)
                            mm.then_inc(full[4 + rr], 1)
                head = lambda b, rr: slice((2 * b + rr) * W_HD, (2 * b + rr + 1) * W_HD)
                if m:
                    pe.wait_ge(s_st, 2 * (it - 2) + 2)
                for rr in range(2):
                    u, rows = buf[rr], slice(64 * rr, 64 * rr + 64)
                    take(rr, RHS)
                    for j, b in enumerate(blocks):
                        o = t.bank[rr][:, j * W_HD:(j + 1) * W_HD]
                        if m:
                            nc.tensor.matmul(o, sigma[rows, b, ms], state[rows, b, :], start=True, stop=False)
                        mm = nc.tensor.matmul(o, u["ak"][:, j], v[:, m, head(b, rr)], start=not m, stop=True)
                    mm.then_inc(full[rr], 1)
                for rr in range(2):
                    u = buf[rr]
                    pe.wait_ge(read[rr], nth(rr, it, RHS))
                    pe.wait_ge(read[4 + rr], nth(4 + rr, it, TOP))
                    for j in range(4):
                        mm = nc.tensor.matmul(t.bank[rr][:, j * W_HD:(j + 1) * W_HD], u["tt"][:, j], u["rhs"][:, j * W_HD:(j + 1) * W_HD],
                                              start=True, stop=True)
                    mm.then_inc(full[rr], 1)
                for rr in range(2):
                    u, rows = buf[rr], slice(64 * rr, 64 * rr + 64)
                    pe.wait_ge(read[rr], nth(rr, it, SA))
                    take(2 + rr, Y)
                    for j, b in enumerate(blocks):
                        o, js = t.bank[2 + rr][:, j * W_HD:(j + 1) * W_HD], slice(j * W_HD, (j + 1) * W_HD)
                        if m:
                            nc.tensor.matmul(o, r[rows, b, ms], state[rows, b, :], start=True, stop=False)
                        nc.tensor.matmul(o, u["rb"][:, j], u["sa"][:, js], start=not m, stop=False)
                        mm = nc.tensor.matmul(o, u["rk"][:, j], v[:, m, head(b, rr)], start=False, stop=True)
                    mm.then_inc(full[2 + rr], 1)
                    take(4 + rr, UP)
                    for j, b in enumerate(blocks):
                        o, js = t.bank[4 + rr][rows, j * W_HD:(j + 1) * W_HD], slice(j * W_HD, (j + 1) * W_HD)
                        nc.tensor.matmul(o, btok[:, m, head(b, rr)], u["sa"][:, js], start=True, stop=False)
                        mm = nc.tensor.matmul(o, ktok[:, m, head(b, rr)], v[:, m, head(b, rr)], start=False, stop=True)
                    mm.then_inc(full[4 + rr], 1)

        @block.scalar
        def _(act):
            for it, (m, p) in enumerate(steps):
                for rr in range(2):
                    act.wait_ge(full[2 + rr], nth(2 + rr, it, LT))
                    if it:
                        act.wait_ge(s_et, 2 * TOP * it)
                    nc.scalar.activation(buf[rr]["lt"], four(t.bank[2 + rr][:, :]), ACT.Copy).then_inc(read[2 + rr], 1)
                for l in range(1, TOP + 1):
                    for rr in range(2):
                        act.wait_ge(full[rr], nth(rr, it, l))
                        nc.scalar.activation(buf[rr]["x"], four(t.bank[rr][:, :]), ACT.Copy).then_inc(read[rr], 1)
                        if l > 1:
                            act.wait_ge(full[4 + rr], nth(4 + rr, it, l - 1))
                            nc.scalar.activation(buf[rr]["tt"], four(t.bank[4 + rr][:, :]), ACT.Copy).then_inc(read[4 + rr], 1)
                for use, name in ((RHS, "rhs"), (SA, "sa")):
                    for rr in range(2):
                        act.wait_ge(full[rr], nth(rr, it, use))
                        nc.scalar.activation(buf[rr][name], t.bank[rr][:, 0:4 * W_HD], ACT.Copy).then_inc(read[rr], 1)
                for rr in range(2):
                    act.wait_ge(full[4 + rr], nth(4 + rr, it, UP))
                    dst = btok[:, m, 8 * p * W_HD:8 * (p + 1) * W_HD].rearrange("p (b r n) -> p b r n", b=4, r=2)[:, :, rr, :]
                    nc.scalar.activation(dst, t.bank[2 + rr][:, 0:4 * W_HD].rearrange("p (b n) -> p b n", b=4), ACT.Copy).then_inc(read[2 + rr], 1)

        @block.vector
        def _(dve):
            ch = Chain(dve, s_dve)
            ident = mask(C_IDENT)
            for it, (m, p) in enumerate(steps):
                for rr in range(2):
                    u = buf[rr]
                    dve.wait_ge(full[rr], nth(rr, it, L))
                    ch.add(nc.vector.tensor_tensor(u["t"], four(t.bank[rr][:, :]), low0, ALU.mult))
                    read_l = ch.n
                    dve.wait_ge(read[2 + rr], nth(2 + rr, it, LT))
                    ch.link(nc.vector.tensor_tensor(u["tt"], u["lt"], up(0), ALU.mult))
                    nc.vector.tensor_tensor(u["t"], u["t"], ident, ALU.add).then_inc(s_t0, 1)
                    nc.vector.tensor_tensor(u["tt"], u["tt"], ident, ALU.add).then_inc(s_t0, 1)
                    dve.wait_ge(s_t0, 4 * it + 2 * rr + 2)
                    dve.sem_inc(read[rr], 1)
                    for bank, use, name, col in ((4 + rr, AK, "ak", C_BEFORE), (6, rr, "rb", C_UPTO), (7, rr, "rk", C_UPTO)):
                        dve.wait_ge(full[bank], nth(bank, it, use))
                        nc.vector.tensor_tensor(u[name], four(t.bank[bank][:, :]), mask(col), ALU.mult).then_inc(read[bank], 1)
                for l in range(1, TOP + 1):
                    for rr in range(2):
                        bank, name = (2 + rr, "t") if l < TOP else (4 + rr, "tt")
                        dve.wait_ge(full[bank], nth(bank, it, l))
                        if l > 1:
                            dve.wait_ge(read[bank], nth(bank, it, l - 1))
                        nc.vector.tensor_tensor(buf[rr][name], buf[rr][name], four(t.bank[bank][:, :]), ALU.add).then_inc(read[bank], 1)
                for rr in range(2):
                    rows = slice(64 * rr, 64 * rr + 64)
                    st = state[rows, 4 * p:4 * p + 4, :]
                    new = t.bank[4 + rr][rows, 0:4 * W_HD].rearrange("p (b n) -> p b n", b=4)
                    dve.wait_ge(full[4 + rr], nth(4 + rr, it, UP))
                    if m:
                        ins = nc.vector.tensor_tensor(st, st, new, ALU.add)
                    else:
                        ins = nc.vector.tensor_copy(st, new)
                    ins.then_inc(read[4 + rr], 1)
                    dve.wait_ge(read[4 + rr], nth(4 + rr, it, UP))
                    f = keep["factor"][rows, 4 * p:4 * p + 4, m:m + 1]
                    if m + 1 < NT:
                        nc.vector.tensor_tensor(st, st, wide(f, 64, 4, W_HD), ALU.mult).then_inc(s_st, 1)

        @block.gpsimd
        def _(pool):
            for it, (m, p) in enumerate(steps):
                for l in range(1, TOP + 1):
                    for rr in range(2):
                        u = buf[rr]
                        if l == 1:
                            pool.wait_ge(read[2 + rr], nth(2 + rr, it, LT))
                        if l > 2:
                            pool.wait_ge(full[rr], nth(rr, it, l - 2))
                        elif it:
                            pool.wait_ge(full[rr], nth(rr, it - 1, TOP - 2 + l))
                        nc.gpsimd.tensor_tensor(u["et"][:, l % 2], u["lt"], up(l), ALU.mult).then_inc(s_et, 1)


def rwkv_out_phase(t, a, y, v, g, lnw, lnb, sq, mt, ring, keep):
    nc = t.nc
    wo = a["rw_wo"][0].rearrange("(k p) n -> p k n", p=P)
    with ExitStack() as c:
        sem = lambda n: t.semaphore(f"out_{n}")
        s_ln, s_dve, s_c, s_sq, s_var, s_rt, s_bv, s_y = (sem(n) for n in ("ln", "dve", "centred", "squares", "var", "root", "bonus_v", "y"))
        s_w = [sem(f"weights{i}") for i in range(2)]
        s_tr, s_ev, s_pe, s_add = sem("transposed"), sem("evacuated"), sem("product"), sem("added")
        mean = c.enter_context(nc.sbuf_tensor("out_mean", [P, NT, W_HEADS], F32))
        var = c.enter_context(nc.sbuf_tensor("out_var", [P, NT, W_HEADS], F32))
        block = c.enter_context(nc.Block())
        heads = lambda ap: ap.rearrange("p (h n) -> p h n", h=W_HEADS)
        per_head = lambda ap: wide(ap.unsqueeze(2), P, W_HEADS, W_HD)

        @block.sync
        def _(sp):
            sp.dma_start(lnw, wide(a["lnx"][0:1, :], P, D)).then_inc(s_ln, 16)
            sp.dma_start(lnb, wide(a["lnx"][1:2, :], P, D)).then_inc(s_ln, 16)
            for half in range(2):
                sp.dma_start(ring[half], wo[:, :, half * HALF:(half + 1) * HALF]).then_inc(s_w[half], 16)

        @block.gpsimd
        def _(pool):
            for m in range(NT):
                pool.wait_ge(s_c, m + 1)
                if m:
                    pool.wait_ge(s_var, m)
                nc.gpsimd.tensor_tensor(sq, y[:, m, :], y[:, m, :], ALU.mult).then_inc(s_sq, 1)
                bonus = keep["bonus"][:, m * W_HEADS:(m + 1) * W_HEADS]
                nc.gpsimd.tensor_tensor(heads(v[:, m, :]), heads(v[:, m, :]), per_head(bonus), ALU.mult).then_inc(s_bv, 1)

        @block.tensor
        def _(pe):
            def transposes(m):
                pe.wait_ge(s_y, m + 1)
                if m >= 2:
                    pe.wait_ge(s_ev, 2 * (m - 1))
                for i in range(2):
                    for j in range(4):
                        mm = nc.tensor.transpose(t.bank[2 * (m % 2) + i][:, j * P:(j + 1) * P], y[:, m, (4 * i + j) * P:(4 * i + j + 1) * P], t.ident)
                    mm.then_inc(s_tr, 1)

            for m in range(NT):
                transposes(m)
                pe.wait_ge(s_ev, 2 * (m + 1))
                for half in range(2):
                    if m == 0:
                        pe.wait_ge(s_w[half], 16)
                    if m >= 2:
                        pe.wait_ge(s_add, 2 * (m - 2) + half + 1)
                    for k_ in range(KD):
                        mm = nc.tensor.matmul(t.bank[4 + 2 * (m % 2) + half][:, :], mt[:, k_, m * P:(m + 1) * P], ring[half][:, k_, :],
                                              start=k_ == 0, stop=k_ == KD - 1)
                    mm.then_inc(s_pe, 1)

        @block.scalar
        def _(act):
            for m in range(NT):
                act.wait_ge(s_var, m + 1)
                nc.scalar.activation(var[:, m, :], var[:, m, :], ACT.Sqrt, bias=t.eps[:, 2:3], scale=1.0 / W_HD).then_inc(s_rt, 1)
                for i in range(2):
                    if m:
                        evacuated = 2 * (m - 1) + i
                        act.wait_ge(s_tr, evacuated + 1)
                        nc.scalar.activation(mt[:, 4 * i:4 * i + 4, (m - 1) * P:m * P],
                                             t.bank[2 * ((m - 1) % 2) + i][:, :].rearrange("p (k n) -> p k n", k=4), ACT.Copy).then_inc(s_ev, 1)
            for i in range(2):
                act.wait_ge(s_tr, 2 * (NT - 1) + i + 1)
                nc.scalar.activation(mt[:, 4 * i:4 * i + 4, (NT - 1) * P:NT * P],
                                     t.bank[2 * ((NT - 1) % 2) + i][:, :].rearrange("p (k n) -> p k n", k=4), ACT.Copy).then_inc(s_ev, 1)

        @block.vector
        def _(dve):
            ch = Chain(dve, s_dve)

            def centre(m):
                ch.link(nc.vector.tensor_reduce(mean[:, m, :], heads(y[:, m, :]), AX.X, ALU.add))
                ch.link(nc.vector.tensor_scalar(mean[:, m, :], mean[:, m, :], 1.0 / W_HD, None, ALU.mult))
                nc.vector.tensor_tensor(heads(y[:, m, :]), heads(y[:, m, :]), per_head(mean[:, m, :]), ALU.subtract).then_inc(s_c, 1)

            def variance(m):
                dve.wait_ge(s_sq, m + 1)
                nc.vector.tensor_reduce(var[:, m, :], heads(sq), AX.X, ALU.add).then_inc(s_var, 1)

            def finish(m):
                dve.wait_ge(s_rt, m + 1)
                ch.link(nc.vector.reciprocal(var[:, m, :], var[:, m, :]))
                ch.link(nc.vector.tensor_tensor(heads(y[:, m, :]), heads(y[:, m, :]), per_head(var[:, m, :]), ALU.mult))
                ch.link(nc.vector.tensor_tensor(y[:, m, :], y[:, m, :], lnw, ALU.mult))
                ch.link(nc.vector.tensor_tensor(y[:, m, :], y[:, m, :], lnb, ALU.add))
                dve.wait_ge(s_bv, m + 1)
                ch.link(nc.vector.tensor_tensor(y[:, m, :], y[:, m, :], v[:, m, :], ALU.add))
                nc.vector.tensor_tensor(y[:, m, :], y[:, m, :], g[:, m, :], ALU.mult).then_inc(s_y, 1)

            def residual(m):
                for half in range(2):
                    dve.wait_ge(s_pe, 2 * m + half + 1)
                    hs = t.h[:, m, half * HALF:(half + 1) * HALF]
                    nc.vector.tensor_tensor(hs, hs, t.bank[4 + 2 * (m % 2) + half][:, :], ALU.add).then_inc(s_add, 1)

            centre(0)
            variance(0)
            dve.wait_ge(s_ln, 32)
            for m in range(NT):
                finish(m)
                if m + 1 < NT:
                    centre(m + 1)
                    variance(m + 1)
                if m:
                    residual(m - 1)
            residual(NT - 1)


def rwkv(t, a):
    M = views(t, RING, [("ut", (KD, SEQ)), ("mix0", (KD, SEQ)), ("mix1", (KD, SEQ)), ("sigma", (KD, SEQ)), ("ag", (KD, SEQ)), ("r", (KD, SEQ)),
                        ("k", (KD, SEQ)), ("kkn", (KD, SEQ)), ("sg", (2, SEQ)), ("lw", (SEQ,)), ("la", (SEQ,)), ("k2", (2, SEQ)), ("root", (SEQ,))])
    at_kkn, at_sg = RING + 7 * KD * SEQ, RING + 8 * KD * SEQ
    V = views(t, RING + KD * SEQ, [("v", (NT, D)), ("g", (NT, D))])
    xn = views(t, at_kkn, [("xn", (NT, D))])["xn"]
    norm_phase(t, "mix1", t.col("mix1"), xn, M["ut"])
    keep = {"one_minus_mu": t.l0c[:, 0:6 * KD], "mid": t.l0c[:, 64:64 + KD * NT].rearrange("p (b m) -> p b m", b=KD),
            "end": t.l0c[:, 128:128 + KD * NT].rearrange("p (b m) -> p b m", b=KD),
            "factor": t.l0c[:, 192:192 + KD * NT].rearrange("p (b m) -> p b m", b=KD), "bonus": t.l0c[:, 256:256 + NT * W_HEADS]}
    T = views(t, RING, [(n, (2, NT, P)) for n in ("c", "d1", "d2")] + [("x", (2, SEQ))])
    T.update({"k2": M["k2"], "pinv": T["c"], "pt": T["d1"], "pb": T["d2"]})
    rwkv_proj_phase(t, a, M["ut"], [M["mix0"], M["mix1"]], M["sg"], [M["lw"], M["la"]], M["sigma"], M["ag"], M["r"], M["k"], V["v"], V["g"],
                    M["kkn"], M["k2"], M["root"], T, keep)
    l1c = views(t, at_sg, [("l1c", (L1_ALL,))])["l1c"]
    btok, ktok = (t.ring[i].rearrange("p k n -> p (k n)").rearrange("p (m n) -> p m n", m=NT) for i in range(2))
    rwkv_rows_phase(t, a, M["ag"], M["k"], btok, ktok, l1c)
    spec = [("t", (4, P)), ("tt", (4, P)), ("lt", (4, P)), ("et", (2, 4, P)), ("x", (4, P)), ("ak", (4, P)), ("rb", (4, P))]
    rest = [("rk", (4, P)), ("rhs", (4 * W_HD,)), ("sa", (4 * W_HD,))]
    buf = [{**views(t, at, spec), **views(t, at_sg + L1_ALL + i * 2 * HALF, rest)} for i, at in enumerate((RING, at_kkn))]
    state = t.zero[:, 0:KD * W_HD].rearrange("p (b n) -> p b n", b=KD)
    rwkv_scan_phase(t, M["sigma"], M["ag"], M["r"], M["k"], V["v"], btok, ktok, buf, state, keep, l1c)
    E = views(t, RING, [("lnw", (D,)), ("lnb", (D,)), ("sq", (D,))])
    O = views(t, RING + 3 * KD * SEQ, [("ring0", (KD, HALF)), ("ring1", (KD, HALF)), ("mt", (KD, SEQ))])
    rwkv_out_phase(t, a, btok, V["v"], V["g"], E["lnw"], E["lnb"], E["sq"], O["mt"], [O["ring0"], O["ring1"]], keep)


def final_phase(t, a, out, w, y):
    nc = t.nc
    with ExitStack() as c:
        sem = lambda n: t.semaphore(f"final_{n}")
        s_w, s_ms, s_rs, s_y, s_out = (sem(n) for n in ("weight", "ms", "rs", "y", "out"))
        ms = c.enter_context(nc.sbuf_tensor("final_ms", [P, NT], F32))
        block = c.enter_context(nc.Block())

        @block.sync
        def _(sp):
            sp.dma_start(w, wide(a["final_w"], P, D)).then_inc(s_w, 16)
            rows = out.rearrange("o (m p) d -> p (o m) d", p=P)
            for m in range(NT):
                sp.wait_ge(s_y, m + 1)
                sp.dma_start(rows[:, m, :], y[:, m, :]).then_inc(s_out, 16)
            sp.wait_ge(s_out, 16 * NT)

        @block.scalar
        def _(act):
            act.wait_ge(s_ms, NT)
            nc.scalar.activation(ms[:, :], ms[:, :], ACT.Sqrt, bias=t.eps[:, 0:1]).then_inc(s_rs, 1)

        @block.vector
        def _(dve):
            for m in range(NT):
                nc.vector.tensor_tensor_reduce(y[:, m, :], t.h[:, m, :], t.h[:, m, :], 1.0 / D, 0.0, ALU.mult, ALU.add,
                                               ms[:, m:m + 1]).then_inc(s_ms, 1)
            dve.wait_ge(s_rs, 1)
            nc.vector.reciprocal(ms[:, :], ms[:, :]).then_inc(s_rs, 1)
            dve.wait_ge(s_rs, 2)
            dve.wait_ge(s_w, 16)
            for m in range(NT):
                nc.vector.scalar_tensor_tensor(out=y[:, m, :], in0=t.h[:, m, :], scalar=ms[:, m:m + 1], in1=w, op0=ALU.mult,
                                               op1=ALU.mult).then_inc(s_y, 1)


def _(sp):
            sp.dma_start(out.rearrange("o (m p) d -> p (o m) d", p=P), t.h[:, :, :] if srcs is None else srcs).then_inc(s, 16)
            sp.wait_ge(s, 16)


INPUTS = {"x": (1, SEQ, D), "w_in_e": None, "w_out_e": None, "cols": (P, N_COLS), "rows": (1, N_ROWS), "common": (P, C_ALL),
          "layer0": (P, L0_ALL), "layer1": (P, L1_ALL)}


def views(t, start, spec):
    out, at = {}, start
    for name, shape in spec:
        n = int(np.prod(shape))
        v = t.arena[:, at:at + n]
        if len(shape) == 2:
            v = v.rearrange("p (a b) -> p a b", a=shape[0])
        if len(shape) == 3:
            v = v.rearrange("p (a b c) -> p a b c", a=shape[0], b=shape[1])
        if len(shape) == 4:
            v = v.rearrange("p (a b c d) -> p a b c d", a=shape[0], b=shape[1], c=shape[2])
        out[name] = v
        at += n
    assert at <= ARENA, (at, ARENA)
    return out


ARENA = 44800
RING = 2 * KD * HALF


def trunk(nc, a, out):
    with ExitStack() as c:
        t = Trunk(nc)
        sb = lambda name, shape, dt=F32: c.enter_context(nc.sbuf_tensor(name, shape, dt))
        t.h = sb("h", [P, NT, D])
        t.cols, t.rows = sb("cols", [P, N_COLS]), sb("rows", [P, N_ROWS])
        t.common, t.l0c = sb("common", [P, C_ALL]), sb("layer0", [P, L0_ALL])
        t.zero = sb("zero", [P, D])
        t.router = sb("router", [P, DEPTH, KD, GROUPS + EXPERTS])
        t.eps = sb("eps", [P, 3])
        t.weight, t.slot, t.meta = sb("weight", [P, NT, 2]), sb("slot", [P, NT, 2], U32), sb("meta", [1, 1 + MAX_BLOCKS], I32)
        t.arena = sb("arena", [P, ARENA])
        t.bank = [c.enter_context(nc.psum_tensor(f"bank{i}", [P, HALF], F32)) for i in range(8)]
        t.ident = t.common[:, C_IDENT:C_IDENT + P]
        t.col = lambda n: t.cols[:, COLS[n][0]:COLS[n][0] + COLS[n][1]]
        t.row = lambda n: t.rows[:, ROWS[n][0]:ROWS[n][0] + ROWS[n][1]]
        t.s_win = [c.enter_context(nc.semaphore(f"w_in_loaded{i}")) for i in range(2)]
        t.s_wout = [c.enter_context(nc.semaphore(f"w_out_loaded{i}")) for i in range(2)]
        t.s_x, t.s_const = c.enter_context(nc.semaphore("x_loaded")), c.enter_context(nc.semaphore("constants_loaded"))
        t.s_clear = c.enter_context(nc.semaphore("slots_cleared"))
        t.xg = a["xg"]
        ring = views(t, 0, [("r0", (KD, HALF)), ("r1", (KD, HALF))])
        t.ring = [ring["r0"], ring["r1"]]

        load_phase(t, a)
        at = RING
        A = views(t, at, [("ut", (KD, SEQ)), ("xbc", (XBC_BLOCKS, XPAD)), ("xc", (XBC_BLOCKS, SEQ)), ("z", (NT, D)), ("g", (NT, D)),
                          ("v", (NT, D)), ("q", (NT, HALF)), ("k", (NT, HALF)), ("dt", (NT, S_HEADS)), ("a_dt", (NT * S_HEADS,)),
                          ("nacum", (NT * S_HEADS,)), ("cum", (3 * NT * S_HEADS,)), ("ecum", (3 * NT * S_HEADS,)),
                          ("ea", ((NT + 1) * S_HEADS,)), ("bt", (NT, S_GROUPS * S_N)), ("tmp", (2, NT, R_HEADS, R_QK // 2))])
        at_ut, at_xbc = at, at + KD * SEQ
        at_xc = at_xbc + XBC_BLOCKS * XPAD
        at_z = at_xc + XBC_BLOCKS * SEQ
        at_v = at_z + 2 * NT * D
        at_q = at_v + NT * D
        at_tmp = ARENA_TMP = at_q + 2 * NT * HALF + (1 + 1 + 1 + 3 + 3 + 1) * NT * S_HEADS + S_HEADS + NT * S_GROUPS * S_N
        xn = views(t, at_xc, [("xn", (NT, D))])["xn"]
        norm_phase(t, "mix0", t.col("mix0"), xn, A["ut"], loading=True)
        in_proj_phase(t, a, A["ut"], A["xbc"], A["xc"], A["z"], A["g"], A["v"], A["q"], A["k"], A["dt"])
        R = views(t, at_xbc, [("qr", (NT, HALF)), ("kr", (NT, HALF)), ("kd", (NT, HALF))])
        xs = views(t, at_ut, [("xs", (NT, D))])["xs"]
        qt, kt = (A[n].rearrange("p m n -> p (m n)").rearrange("p (h n) -> p h n", h=R_HEADS) for n in "qk")
        rows_phase(t, A["xc"], xs, A["bt"], A["q"], A["k"], R["qr"], R["kr"], qt, kt, R["kd"], A["tmp"], A["dt"], A["a_dt"],
                   A["nacum"], A["cum"], A["ecum"], A["ea"])
        T = views(t, at_tmp, [("s", (2, R_HEADS, P))])
        T2 = views(t, RING - 2 * R_HEADS * R_V, [("state", (2, R_HEADS, R_V))])
        yr = views(t, at_xc, [("yr", (NT, D))])["yr"]
        yraw = views(t, 0, [("yraw", (NT, D))])["yraw"]
        retention_phase(t, qt, kt, R["kd"], A["v"], A["g"], T["s"], T2["state"], yraw, yr)
        S1 = views(t, at_q, [("e", (2, S_HPG, P)), ("xdt", (2, HALF)), ("xde", (2, HALF))])
        S2 = views(t, at_tmp, [("state", (S_GROUPS, HALF)), ("decayed", (S_GROUPS, HALF))])
        y1 = views(t, at_xbc, [("y1", (2, HALF))])["y1"]
        ys = A["v"]
        ssd_phase(t, A["xc"], xs, A["bt"], A["z"], A["dt"], A["a_dt"], A["nacum"], A["ecum"], S1["e"], S1["xdt"], S1["xde"],
                  S2["state"], S2["decayed"], y1, ys)
        mt = views(t, at_z, [("mt", (2 * KD, SEQ))])["mt"]
        w = a["w_out_e"][0].rearrange("(j k p) n -> j p k n", p=P, k=KD)
        proj_phase(t, "wout", [ys, yr], [t.col("ssdn"), None], mt,
                   [w[j][:, :, n * HALF:(n + 1) * HALF] for n in range(2) for j in range(2)], t.ring, t.s_wout)
        moe(t, a, 0)
        t.recycle_semaphores()
        rwkv(t, a)
        moe(t, a, 1)
        final_phase(t, a, out, *(views(t, 0, [("w", (D,)), ("y", (NT, D))])[n] for n in ("w", "y")))


def kernel(**inputs):
    import concourse.bacc as bacc
    from concourse.bass_utils import run_bass_kernel_spmd

    f = {k: np.asarray(v) for k, v in inputs.items()}

    def blocks(v):
        return np.ascontiguousarray(v.reshape(-1, P).T)

    named = {"mix0": f["norm_mix_w"][0], "mix1": f["norm_mix_w"][1], "ffn0": f["norm_ffn_w"][0], "ffn1": f["norm_ffn_w"][1],
             "conv": f["ssd_conv_w"], "convb": f["ssd_conv_b"], "ssdn": f["ssd_norm_w"], "mu": f["rw_mu"], "w0": f["rw_w0"],
             "a0": f["rw_a0"], "kk": f["rw_kk"], "ka": f["rw_ka"], "rk": f["rw_rk"]}
    common, layer0, layer1 = shape_constants()
    mb = [np.concatenate([f["moe_bg"][i], f["moe_be"][i]]) for i in range(DEPTH)]
    arrays = {"x": f["x"], "w_in_e": f["w_in_e"], "w_out_e": f["w_out_e"],
              "cols": np.concatenate([blocks(named[n]) for n in COLS], 1),
              "rows": np.concatenate([f["ssd_dt_bias"][0], f["ssd_a_log"][0], f["ssd_d"][0], *mb])[None],
              "common": common, "layer0": layer0, "layer1": layer1}
    for n in ("rw_wr", "rw_wk", "rw_wv", "rw_wo", "rw_w1", "rw_w2", "rw_a1", "rw_a2", "rw_g1", "rw_g2", "moe_w1", "moe_w3", "moe_w2"):
        arrays[n] = f[n]
    arrays["router"] = np.ascontiguousarray(np.concatenate([f["moe_wg"], f["moe_we"]], 2).reshape(DEPTH, KD, P, -1).transpose(2, 0, 1, 3))
    arrays["final_w"] = f["norm_final_w"][None]
    arrays["lnx"] = np.stack([f["rw_lnx_w"][0], f["rw_lnx_b"][0]])
    nc = bacc.Bacc("TRN2", target_bir_lowering=False, num_devices=1)
    feed = {f"in_{n}": np.ascontiguousarray(v) for n, v in arrays.items()}
    aps = {n: nc.dram_tensor(f"in_{n}", v.shape, mybir.dt.from_np(v.dtype), kind="ExternalInput").ap() for n, v in arrays.items()}
    aps["xg"] = nc.dram_tensor("slot_rows", ((MAX_BLOCKS + 2) * SLOTS, D), F32, kind="Internal").ap()
    out = nc.dram_tensor("out_trunk", (1, SEQ, D), F32, kind="ExternalOutput").ap()
    trunk(nc, aps, out)
    r = run_bass_kernel_spmd(nc, [feed], core_ids=[0])
    return r.results[0]["out_trunk"]
```
